# Optimizing a Trainium2 kernel written in Bass

```python
import jax, jax.numpy as jnp
from jax import lax
import numpy as np

D_MODEL = 1024
BATCH = 1
SEQ = 1024
DEPTH = 1

N_META = 16
D_MIX = D_MODEL
ATTN_HEADS = 8
HEAD_DIM = 64
D_ATTN = ATTN_HEADS * HEAD_DIM
D_CONF = D_MIX // 4
D_SC = D_MIX - D_ATTN - D_CONF
CONF_KERNEL = 31
SC_KERNEL = 3
D_FF = 4 * D_MODEL
Q_BLOCK = 128
EPS = 1e-6
N_IN = 3 * D_ATTN + ATTN_HEADS + 2 * D_CONF + 3 * D_SC

kernel_name = 'hybrid_fox_conformer_shortconv_block'

def _rmsnorm(x, g):
    xf = x.astype(jnp.float32)
    y = xf * lax.rsqrt(jnp.mean(xf * xf, axis=-1, keepdims=True) + EPS)
    return (y * g.astype(jnp.float32)).astype(x.dtype)

def _layernorm(x, g, b):
    xf = x.astype(jnp.float32)
    mu = jnp.mean(xf, axis=-1, keepdims=True)
    xc = xf - mu
    y = xc * lax.rsqrt(jnp.mean(xc * xc, axis=-1, keepdims=True) + EPS)
    return (y * g.astype(jnp.float32) + b.astype(jnp.float32)).astype(x.dtype)

def _causal_dwconv(x, w):
    K, C = w.shape
    return lax.conv_general_dilated(
        x, w[:, None, :].astype(x.dtype), window_strides=(1,), padding=[(K - 1, 0)],
        dimension_numbers=('NWC', 'WIO', 'NWC'), feature_group_count=C)

def _fox_attend(q_blk, c_q, q_pos, k, v, c_k, k_pos):
    s = jnp.einsum('bhqd,bhkd->bhqk', q_blk, k, preferred_element_type=jnp.float32) * (HEAD_DIM ** -0.5)
    s = s + c_q[..., :, None] - c_k[..., None, :]
    s = jnp.where(q_pos[:, None] >= k_pos[None, :], s, -jnp.inf)
    p = jax.nn.softmax(s, axis=-1)
    return jnp.einsum('bhqk,bhkd->bhqd', p.astype(v.dtype), v)

def _fox_attention(q, k, v, log_f):
    bsz, L, H, dh = q.shape
    n_real = L - N_META
    nb = n_real // Q_BLOCK
    c = jnp.cumsum(log_f, axis=1).transpose(0, 2, 1)
    qh = q.transpose(0, 2, 1, 3)
    kh = k.transpose(0, 2, 1, 3)
    vh = v.transpose(0, 2, 1, 3)
    k_pos = jnp.arange(L)
    meta_out = _fox_attend(qh[:, :, :N_META], c[:, :, :N_META], k_pos[:N_META],
                           kh[:, :, :N_META], vh[:, :, :N_META], c[:, :, :N_META], k_pos[:N_META])
    q_blocks = qh[:, :, N_META:].reshape(bsz, H, nb, Q_BLOCK, dh).transpose(2, 0, 1, 3, 4)
    c_blocks = c[:, :, N_META:].reshape(bsz, H, nb, Q_BLOCK).transpose(2, 0, 1, 3)

    def body(args):
        q_blk, c_q, i = args
        q_pos = N_META + i * Q_BLOCK + jnp.arange(Q_BLOCK)
        return _fox_attend(q_blk, c_q, q_pos, kh, vh, c, k_pos)

    real_out = lax.map(body, (q_blocks, c_blocks, jnp.arange(nb)))
    real_out = real_out.transpose(1, 0, 3, 2, 4).reshape(bsz, n_real, H * dh)
    meta_out = meta_out.transpose(0, 2, 1, 3).reshape(bsz, N_META, H * dh)
    return jnp.concatenate([meta_out, real_out], axis=1)

def setup_inputs(seed: int = 0) -> dict:
    key = jax.random.key(seed)
    ks = jax.random.split(key, 20)
    nrm = jax.random.normal
    f32 = jnp.float32
    return {
        'x': nrm(ks[0], (BATCH, SEQ, D_MODEL), f32),
        'meta_tokens': nrm(ks[1], (N_META, D_MODEL), f32),
        'mix_norm_g': 1.0 + 0.1 * nrm(ks[2], (DEPTH, D_MODEL), f32),
        'w_in': nrm(ks[3], (DEPTH, D_MODEL, N_IN), f32) * D_MODEL ** -0.5,
        'b_forget': jax.random.uniform(ks[4], (DEPTH, ATTN_HEADS), f32, 1.0, 5.0),
        'w_conf_dw': nrm(ks[5], (DEPTH, CONF_KERNEL, D_CONF), f32) * CONF_KERNEL ** -0.5,
        'b_conf_dw': 0.02 * nrm(ks[6], (DEPTH, D_CONF), f32),
        'conf_ln_g': 1.0 + 0.1 * nrm(ks[7], (DEPTH, D_CONF), f32),
        'conf_ln_b': 0.02 * nrm(ks[8], (DEPTH, D_CONF), f32),
        'w_conf_pw': nrm(ks[9], (DEPTH, D_CONF, D_CONF), f32) * D_CONF ** -0.5,
        'b_conf_pw': 0.02 * nrm(ks[10], (DEPTH, D_CONF), f32),
        'w_sc_conv': nrm(ks[11], (DEPTH, SC_KERNEL, D_SC), f32) * SC_KERNEL ** -0.5,
        'w_out': nrm(ks[12], (DEPTH, D_MIX, D_MODEL), f32) * D_MIX ** -0.5,
        'mlp_norm_g': 1.0 + 0.1 * nrm(ks[13], (DEPTH, D_MODEL), f32),
        'w_mlp1': nrm(ks[14], (DEPTH, D_MODEL, D_FF), f32) * D_MODEL ** -0.5,
        'w_mlp2': nrm(ks[15], (DEPTH, D_FF, D_MODEL), f32) * D_FF ** -0.5,
        'final_norm_g': 1.0 + 0.1 * nrm(ks[16], (D_MODEL,), f32),
    }

def reference(x, meta_tokens, mix_norm_g, w_in, b_forget, w_conf_dw, b_conf_dw, conf_ln_g,
              conf_ln_b, w_conf_pw, b_conf_pw, w_sc_conv, w_out, mlp_norm_g, w_mlp1, w_mlp2,
              final_norm_g):
    bsz = x.shape[0]
    meta = jnp.broadcast_to(meta_tokens[None].astype(x.dtype), (bsz, N_META, D_MODEL))
    h = jnp.concatenate([meta, x], axis=1)
    L = h.shape[1]
    sizes = [D_ATTN, D_ATTN, D_ATTN, ATTN_HEADS, D_CONF, D_CONF, D_SC, D_SC, D_SC]
    splits = np.cumsum(sizes)[:-1].tolist()
    for l in range(DEPTH):
        hn = _rmsnorm(h, mix_norm_g[l])
        proj = hn @ w_in[l]
        q, k, v, f_logit, conf_a, conf_gate, sc_b, sc_c, sc_u = jnp.split(proj, splits, axis=-1)
        log_f = jax.nn.log_sigmoid(f_logit.astype(jnp.float32) + b_forget[l].astype(jnp.float32))
        attn = _fox_attention(q.reshape(bsz, L, ATTN_HEADS, HEAD_DIM),
                              k.reshape(bsz, L, ATTN_HEADS, HEAD_DIM),
                              v.reshape(bsz, L, ATTN_HEADS, HEAD_DIM), log_f)
        glu = conf_a * jax.nn.sigmoid(conf_gate)
        dw = _causal_dwconv(glu, w_conf_dw[l]) + b_conf_dw[l]
        conf = jax.nn.silu(_layernorm(dw, conf_ln_g[l], conf_ln_b[l])) @ w_conf_pw[l] + b_conf_pw[l]
        sc = sc_b * _causal_dwconv(sc_c * sc_u, w_sc_conv[l])
        h = h + jnp.concatenate([attn, conf, sc], axis=-1) @ w_out[l]
        hn = _rmsnorm(h, mlp_norm_g[l])
        h = h + jnp.square(jax.nn.relu(hn @ w_mlp1[l])) @ w_mlp2[l]
    out = _rmsnorm(h, final_norm_g)
    return out[:, N_META:]


_drawn_inputs = setup_inputs


def setup_inputs(seed=0):
    import zlib

    import numpy as np

    out = dict(_drawn_inputs(seed))
    spreads = {}
    factors = {'b_conf_dw': 5.185, 'conf_ln_b': 8.0, 'b_conf_pw': 5.98}
    for name, (base, spread) in spreads.items():
        noise = np.random.default_rng([zlib.crc32(name.encode()), seed]).standard_normal(out[name].shape)
        drawn = base * np.exp(spread * noise) if base else spread * noise
        out[name] = __import__('jax').numpy.asarray(drawn.astype(out[name].dtype))
    for name, factor in factors.items():
        out[name] = (out[name] * factor).astype(out[name].dtype)
    return out
```

```python
from contextlib import ExitStack

import numpy as np

import concourse.bass as bass
from concourse import mybir

F32 = mybir.dt.float32
F32R = mybir.dt.float32r
BF16 = mybir.dt.bfloat16
ALU = mybir.AluOpType
ACT = mybir.ActivationFunctionType
AX = mybir.AxisListType

P = 128
D = 1024
SEQ = 1024
META = 16
TOK = SEQ + META
HEADS = 8
HD = 64
D_ATTN = HEADS * HD
D_CONF = 256
CONF_K = 31
SC_K = 3
FF = 4096
EPS = 1e-6
KT = D // P
NB = SEQ // P
VF = D_ATTN + HEADS
HALF = 512
CH = FF // HALF
FT = HALF // P

G1, G2 = 0, 8
B_DW, W_DW = 16, 18
LN_G, LN_B = W_DW + 2 * CONF_K, W_DW + 2 * CONF_K + 2
B_PW = LN_B + 2
W_SC = B_PW + 2
B_F = W_SC + 2 * SC_K
N_PAR = B_F + HEADS

GATE, CONF_A, SC_B, SC_C, SC_U, Q, K = range(7)
ORDER = [(GATE, 0), (CONF_A, 0), (GATE, 1), (CONF_A, 1)] \
    + [(kind, j) for j in range(2) for kind in (SC_C, SC_U, SC_B)] \
    + [(kind, p) for p in range(4) for kind in (Q, K)]
FIRST_COL = {Q: 0, K: D_ATTN, CONF_A: 3 * D_ATTN + HEADS, GATE: 3 * D_ATTN + HEADS + D_CONF,
             SC_B: 3 * D_ATTN + HEADS + 2 * D_CONF, SC_C: 3 * D_ATTN + HEADS + 3 * D_CONF,
             SC_U: 3 * D_ATTN + HEADS + 4 * D_CONF}
N_PROJ = len(ORDER)
N_EARLY = 10

ALL_TOKENS = [(0, 352), (352, 344), (696, 344)]
REAL_TOKENS = [(META, HALF), (META + HALF, HALF)]

UNITS = [(1, T) for T in range(NB + 1)] + [(0, T) for T in range(NB // 2 + 1)]
NU = len(UNITS)
RING = 4
N_FILLS = 8
LAG = 2
MAXES = [(0, 0, 144, 1), (1, 0, 272, 1), (2, 0, 400, 1), (3, 0, 264, 2), (4, 0, 328, 2), (5, 0, 392, 2),
         (6, 0, 456, 2), (7, 0, 348, 2), (7, 696, 344, 1)]
NM = len(MAXES)


def cols_of(T):
    return (0, META) if T == 0 else (META + P * (T - 1), P)


def unit(u):
    c, T = UNITS[u]
    k0, rows = cols_of(T)
    ahead = max(0, T - 1 - 4 * c)
    q0 = HALF * c + P * ahead
    return k0, rows, q0, HALF * (c + 1) - q0, T >= 1 and T - 1 >= 4 * c


def build(nc, x, meta, par, consts, w_vf, w_proj, w_pw, w_out, w1, w2, g_fin, out):
    with ExitStack() as ctx:
        base = 16512
        at = [base]

        def sb(name, shape, dt, offset=None):
            if offset is not None:
                at[0] = offset
            size = 4 if dt != BF16 else 2
            for n in shape[1:]:
                size *= n
            t = nc.alloc_sbuf_tensor_at(name, shape, dt, offset=at[0])
            at[0] += -(-size // 32) * 32
            assert at[0] <= 229344, (name, at[0])
            return t

        def sem(name):
            return ctx.enter_context(nc.semaphore(name))

        R_HN = base
        R_MIX = R_HN + 2 * KT * TOK * 4
        R_H = R_MIX + KT * SEQ * 4
        R_QKV = R_H + KT * SEQ * 4
        R_RING = R_QKV + 2 * 4 * (SEQ + META) * 4 - 4 * META * 4 + (NB + 1) * D_ATTN * 4
        R_C = R_RING + 6 * 4096

        ident = sb("ident", [P, P], F32, R_C)
        identb = sb("identb", [P, P], BF16)
        mask_qk = sb("mask_qk", [P, P], BF16)
        mask_kq = sb("mask_kq", [P, P], BF16)
        prm = sb("prm", [P, N_PAR], F32)
        sumsq = sb("sumsq", [P, 12], F32)
        meansq = sb("meansq", [P, 12], F32)
        std = sb("std", [P, 12], F32)
        rstd = sb("rstd", [P, 12], F32)
        f_raw = sb("f_raw", [P, NB + 1, HEADS], F32)
        c_q = sb("c_q", [P, HEADS, NB], F32)
        mx = sb("mx", [P, NM], F32)
        m_q = sb("m_q", [P, NB], F32)
        r_q = sb("r_q", [P, NB], F32)
        r_hi = sb("r_hi", [P, NB], F32R)

        hn_hi = sb("hn_hi", [P, KT, TOK], F32R, R_HN)
        hn_lo = sb("hn_lo", [P, KT, TOK], F32R)
        x_in = sb("x_in", [P, NB, D], F32, R_H)
        x_meta = sb("x_meta", [META, D], F32, R_QKV)
        xs = sb("xs", [P, 2, D], F32)
        squares = sb("squares", [P, D], F32)
        wv_hi = sb("wv_hi", [P, KT, VF], F32R, R_QKV + 16384)
        wv_lo = sb("wv_lo", [P, KT, VF], F32R, R_MIX)
        hn32 = sb("hn32", [P, KT, P], F32, R_MIX + 16640)
        hn32b = sb("hn32b", [P, KT, P], F32)
        consts_f = sb("consts_f", [P, 3, P], F32)
        wv_raw = sb("wv_raw", [P, KT, VF], F32, R_RING)
        w_raw = sb("w_raw", [P, 2, D], F32, R_RING)
        w_hi = sb("w_hi", [P, 2, KT, P], F32R)
        w_lo = sb("w_lo", [P, 2, KT, P], F32R)
        q_raw = sb("q_raw", [P, 4, SEQ], F32, R_QKV)
        k_raw = sb("k_raw", [P, 4, TOK], F32)
        v_raw = sb("v_raw", [P, NB + 1, D_ATTN], F32)
        hn32 = [hn32, hn32b]
        lf = [sb(f"lf{i}", [P, NB + 1, HEADS], F32, R_QKV + 16384 + i * 288) for i in range(10)]
        lf_t = sb("lf_t", [HEADS, TOK], F32, R_QKV)
        c_t = sb("c_t", [HEADS, TOK], F32)
        c_neg = sb("c_neg", [HEADS, TOK], F32)
        c_hi = sb("c_hi", [HEADS, TOK], F32R, R_MIX)
        c_lo = sb("c_lo", [HEADS, TOK], F32R)
        PAD = CONF_K - 1 - META
        GLU = -(-(PAD + TOK) * 4 // 32) * 32
        glu = [sb("glu0", [P, PAD + TOK], F32, R_H), sb("glu1", [P, PAD + TOK], F32)]
        sig_gate = sb("sig_gate", [P, TOK], F32)
        sc_c = sb("sc_c", [P, TOK], F32)
        sc_cu = sb("sc_cu", [P, TOK], F32)
        dw = sb("dw", [P, 2, SEQ], F32)
        z = sb("z", [P, 2, SEQ], F32, R_H)
        normed = sb("normed", [P, NB, D_CONF], F32, R_H + 2 * GLU)
        silu = sb("silu", [P, 2, SEQ], F32, R_H + 2 * GLU + 3 * TOK * 4)
        ln_stats = sb("ln_stats", [P, NB, 6], F32)
        ln_mv = sb("ln_mv", [P, NB, 2], F32)
        ln_std = sb("ln_std", [P, NB], F32)
        ln_rstd = sb("ln_rstd", [P, NB], F32)
        s_hi = sb("s_hi", [P, 2, SEQ], F32R, R_MIX)
        s_lo = sb("s_lo", [P, 2, SEQ], F32R)
        mix = sb("mix", [P, KT, SEQ], F32, R_MIX)
        assert PAD >= 0 and R_H + KT * SEQ * 4 == R_QKV

        qm = [sb(f"qm{s}", [P, SEQ], F32R, R_HN if s == 0 else None) for s in range(2)]
        qx = [sb(f"qx{s}", [P, SEQ], F32R) for s in range(2)]
        km = [sb(f"km{s}", [P, TOK], F32R) for s in range(2)]
        kx = [sb(f"kx{s}", [P, TOK], F32R) for s in range(2)]
        v_one = [sb(f"v_one{s}", [P, NB + 1, P], F32) for s in range(2)]
        o_r0 = sb("o_r0", [P, HALF], F32)
        o_t = sb("o_t", [P, HALF], F32)
        o_r1 = sb("o_r1", [P, HALF], F32)
        r_pad = sb("r_pad", [P, NB, HD + 4], F32)
        p32 = sb("p32", [P, RING, HALF], F32, R_RING)

        h = sb("h", [P, NB, D], F32, R_H)
        wo_hi = sb("wo_hi", [P, KT, HALF], F32R, R_QKV)
        wo_lo = sb("wo_lo", [P, KT, HALF], F32R)
        mix_hi = sb("mix_hi", [P, 2, KT, P], F32R)
        mix_lo = sb("mix_lo", [P, 2, KT, P], F32R)
        assert at[0] <= R_RING
        hs = sb("hs", [P, 2, D], F32, R_RING)
        h32 = sb("h32", [P, KT, P], F32)
        h_squares = sb("h_squares", [P, D], F32)
        wo_raw = sb("wo_raw", [P, 2, HALF], F32)
        hn2_hi = sb("hn2_hi", [P, KT, SEQ], F32R, R_HN)
        hn2_lo = sb("hn2_lo", [P, KT, SEQ], F32R)

        a_hi = sb("a_hi", [P, FT, SEQ], F32R, R_MIX)
        a_lo = sb("a_lo", [P, FT, SEQ], F32R)
        w1_hi = sb("w1_hi", [P, FT, D], F32R, R_QKV)
        w1_lo = sb("w1_lo", [P, FT, D], F32R)
        w2_hi = sb("w2_hi", [P, FT, D], F32R)
        w2_lo = sb("w2_lo", [P, FT, D], F32R)
        m_raw = sb("m_raw", [P, 2, HALF], F32)
        act32 = sb("act32", [P, 2, HALF], F32)
        assert at[0] <= R_C
        g_row = sb("g_row", [P, D], F32, R_QKV)
        y = sb("y", [P, 2, D], F32)
        y_squares = sb("y_squares", [P, D], F32)

        ps = ctx.enter_context(nc.psum_tensor("ps", [P, 8, HALF], F32))
        c_scratch = nc.dram_tensor("c_scratch", (HEADS, 2, TOK), F32, kind="Internal").ap()

        s_par, s_consts, s_g = sem("par_loaded"), sem("consts_loaded"), sem("g_final_loaded")
        s_x = [sem(f"x_loaded{T}") for T in range(NB + 1)]
        s_wv = [sem(f"wv_loaded{i}") for i in range(4)]
        s_xr = [sem(f"x_again{i}") for i in range(NB)]
        s_w = [sem(f"w_loaded{i}") for i in range(2)]
        s_wo = [sem(f"wo_loaded{i}") for i in range(2)]
        s_m = [sem(f"mlp_w_loaded{i}") for i in range(2)]
        s_c = [sem(f"c_rows_loaded{i}") for i in range(2)]
        s_cst = sem("c_stored")
        s_out = [sem(f"out_stored{i}") for i in range(2)]
        masks_ready, pool_init = sem("masks_ready"), sem("pool_init")
        ss_done, ms_done, std_done, rstd_done, xs_done = (sem(n) for n in ("ss_done", "ms_done", "std_done", "rstd_done", "xs_done"))
        tr_done, hn32_done, hnhi_done, hnlo_done = (sem(n) for n in ("tr_done", "hn32_done", "hnhi_done", "hnlo_done"))
        wvhi_done, wvlo_done, v_done, v_evac = (sem(n) for n in ("wvhi_done", "wvlo_done", "v_done", "v_evac"))
        whi_done, wlo_done, proj_done, proj_evac = (sem(n) for n in ("whi_done", "wlo_done", "proj_done", "proj_evac"))
        lf_act, lf_dve, lft_done, lft_evac, cq_tr, cq_evac = (sem(n) for n in ("lf_act", "lf_dve", "lft_done", "lft_evac", "cq_tr", "cq_evac"))
        sig_done, glu_done, cu_done, conv_step, sc_step, pad_done = (sem(n) for n in ("sig_done", "glu_done", "cu_done", "conv_step", "sc_step", "pad_done"))
        scc_done = sem("scc_done")
        ln_tr, ln_dve, ln_sqrt, ln_norm, ln_back = (sem(n) for n in ("ln_tr", "ln_dve", "ln_sqrt", "ln_norm", "ln_back"))
        z_done, zsig_done, silu_done, shi_done, slo_done = (sem(n) for n in ("z_done", "zsig_done", "silu_done", "shi_done", "slo_done"))
        pw_done, pw_evac = sem("pw_done"), sem("pw_evac")
        att_init, qk_hi, qk_dup, qk_lo, qk_lo2, v_ready = (sem(n) for n in ("att_init", "qk_hi", "qk_dup", "qk_lo", "qk_lo2", "v_ready"))
        mx_mm, mx_red, r_step, rt_done, r_ready = (sem(n) for n in ("mx_mm", "mx_red", "r_step", "rt_done", "r_ready"))
        sc_done, exp_done, pv_done = (sem(n) for n in ("sc_done", "exp_done", "pv_done"))
        o_ln, o_inv, o_step, o_evac = (sem(n) for n in ("o_ln", "o_inv", "o_step", "o_evac"))
        wohi_done, wolo_done, wo_used, mixhi_done, mixlo_done = (sem(n) for n in ("wohi_done", "wolo_done", "wo_used", "mixhi_done", "mixlo_done"))
        out_done, h_evac = sem("out_done"), sem("h_evac")
        ss2, ms2, std2, rstd2, hs_done = (sem(n) for n in ("ss2_done", "ms2_done", "std2_done", "rstd2_done", "hs_done"))
        tr2, h32_done, h2hi_done, h2lo_done = (sem(n) for n in ("tr2_done", "h32_done", "h2hi_done", "h2lo_done"))
        mwhi_done, mwlo_done, m1_done, relu_done, asq_done, ahi_done, alo_done = (
            sem(n) for n in ("mwhi_done", "mwlo_done", "m1_done", "relu_done", "asq_done", "ahi_done", "alo_done"))
        ss3, ms3, std3, rstd3, y_done = (sem(n) for n in ("ss3_done", "ms3_done", "std3_done", "rstd3_done", "y_done"))

        def x_tile(T):
            return x_meta[:, :] if T == 0 else x_in[:, T - 1, :]

        def banks(n):
            return 3 * (n % 2)

        def pair_of(n):
            return (n - N_EARLY) // 2

        block = ctx.enter_context(nc.Block())

        @block.sync
        def _(sp):
            sp.dma_start(x_meta[:, :], meta).then_inc(s_x[0], 16)
            sp.dma_start(x_in[:, 0, :], x[0:P, :]).then_inc(s_x[1], 16)
            sp.dma_start(prm[:, :], par).then_inc(s_par, 16)
            sp.dma_start(ident[:, :], consts[:, 0, :]).then_inc(s_consts, 16)
            sp.dma_start(consts_f[:, :, :], consts).then_inc(s_consts, 16)
            for i in range(4):
                sp.dma_start(wv_raw[:, 2 * i:2 * i + 2, :], w_vf[:, 2 * i:2 * i + 2, :]).then_inc(s_wv[i], 16)
                sp.dma_start(x_in[:, i + 1, :], x[P * (i + 1):P * (i + 2), :]).then_inc(s_x[i + 2], 16)
            for T in range(6, NB + 1):
                sp.dma_start(x_tile(T), x[P * (T - 1):P * T, :]).then_inc(s_x[T], 16)

            def load_w(n, slot):
                if isinstance(n, int) and n < 2:
                    sp.wait_ge(wvlo_done, 4)
                else:
                    sp.wait_ge(wlo_done, n - 1)
                sp.dma_start(w_raw[:, slot, :], w_proj[n]).then_inc(s_w[slot], 16)

            for n in range(N_EARLY):
                load_w(n, n % 2)
                if n == 6:
                    sp.wait_ge(lf_dve, 12)
                    sp.dma_start(c_scratch[:, 0, :], c_hi[:, :].bitcast(F32)).then_inc(s_cst, 16)
                    sp.dma_start(c_scratch[:, 1, :], c_lo[:, :].bitcast(F32)).then_inc(s_cst, 16)
            with sp.Fori(0, 4) as p:
                load_w(N_EARLY + 2 * p, 0)
                load_w(N_EARLY + 2 * p + 1, 1)
            sp.wait_ge(wlo_done, N_PROJ - 1)
            sp.dma_start(w_raw[:, 0, 0:2 * D_CONF], w_pw).then_inc(s_w[0], 16)

            sp.wait_ge(slo_done, 2)
            for i in range(NB):
                sp.dma_start(h[:, i, :], x[P * i:P * (i + 1), :]).then_inc(s_xr[i], 16)

            def load_c(g, s):
                sp.dma_start(km[s][HD:HD + 2, :].bitcast(F32), c_scratch[g]).then_inc(s_c[s], 16)

            sp.wait_ge(s_cst, 32)
            sp.wait_ge(att_init, 2)
            load_c(0, 0)
            load_c(1, 1)
            with sp.Fori(0, 3) as p:
                for s in range(2):
                    sp.wait_ge(pv_done, NU * (2 * p + s + 1))
                    load_c(2 * p + s + 2, s)

            sp.wait_ge(pv_done, NU * HEADS)
            for b in range(2):
                for k in range(KT):
                    w = KT * b + k
                    if w >= 2:
                        sp.wait_ge(wolo_done, w - 1)
                    sp.dma_start(wo_raw[:, w % 2, :], w_out[P * k:P * (k + 1), HALF * b:HALF * (b + 1)]).then_inc(s_wo[w % 2], 16)

            def load_m(r, slot, src):
                sp.wait_ge(mwlo_done, r - 1)
                sp.dma_start(m_raw[:, slot, :], src).then_inc(s_m[slot], 16)

            def load_w1(q, first=False):
                for i in range(2 * FT):
                    src = w1[FT * q + i // 2, :, HALF * (i % 2):HALF * (i % 2 + 1)]
                    if first and i < 2:
                        sp.dma_start(m_raw[:, i % 2, :], src).then_inc(s_m[i % 2], 16)
                    else:
                        load_m(16 * q + i, i % 2, src)

            def load_w2(q):
                for i in range(2 * FT):
                    load_m(16 * q + 8 + i, i % 2, w2[FT * q + i // 2, :, HALF * (i % 2):HALF * (i % 2 + 1)])

            sp.wait_ge(h2lo_done, NB)
            load_w1(0, True)
            with sp.Fori(0, CH - 1) as q:
                load_w2(q)
                load_w1(q + 1)
            load_w2(CH - 1)
            sp.wait_ge(m1_done, 2 * FT * CH)
            sp.dma_start(g_row[:, :], g_fin).then_inc(s_g, 16)
            for t in range(NB):
                sp.wait_ge(y_done, t + 1)
                sp.dma_start(out[P * t:P * (t + 1), :], y[:, t % 2, :]).then_inc(s_out[t % 2], 16)
            for i in range(2):
                sp.wait_ge(s_out[i], 16 * NB // 2)

        @block.gpsimd
        def _(pool):
            nc.gpsimd.memset(f_raw[:, :, :], 0.0).then_inc(pool_init, 1)
            pool.wait_ge(pool_init, 1)
            pool.wait_ge(wvlo_done, 4)
            nc.gpsimd.memset(v_raw[:, 0, :], 0.0).then_inc(pool_init, 1)
            pool.wait_ge(proj_done, N_PROJ)
            def fill(i, dst, value):
                if i:
                    pool.wait_ge(att_init, i)
                nc.gpsimd.memset(dst, value).then_inc(att_init, 1)

            fills = [(km[0][HD:HD + 4, :], 1.0), (km[1][HD:HD + 4, :], 1.0), (qm[0][HD:HD + 4, :], 1.0), (qm[1][HD:HD + 4, :], 1.0),
                     (v_one[0][:, :, HD:P], 1.0), (v_one[1][:, :, 0:HD], 1.0),
                     (r_pad[:, :, :], 0.0), (r_pad[:, :, HD:HD + 2], 1.0)]
            assert len(fills) == N_FILLS
            for i, (dst, value) in enumerate(fills):
                fill(i, dst.bitcast(F32), value)

            def prep(g, p, s):
                rows, cols = slice(HD * s, HD * (s + 1)), slice(HD * s, HD * (s + 1))
                if not isinstance(g, int) or g >= 2:
                    pool.wait_ge(pv_done, NU * (g - 1))
                if not isinstance(g, int) or g >= 1:
                    pool.wait_ge(qk_lo2, g)
                nc.gpsimd.tensor_copy(v_one[s][:, :, cols], v_raw[:, :, bass.ds(p * P + s * HD, HD)]).then_inc(v_ready, 1)
                pool.wait_ge(qk_hi, g + 1)
                pool.wait_ge(v_ready, g + 1)
                raw = (q_raw, k_raw)[s][rows, bass.ds(p, 1), :].rearrange("p a c -> p (a c)")
                hi = qm[0][0:HD, :] if s == 0 else kx[1][HD:P, :]
                lo = qx[0][0:HD, :] if s == 0 else kx[1][HD:P, :]
                nc.gpsimd.tensor_tensor(lo, raw, hi.bitcast(F32), ALU.subtract).then_inc(qk_lo2, 1)

            pool.wait_ge(att_init, N_FILLS)
            pool.wait_ge(proj_evac, N_PROJ - N_EARLY)
            prep(0, 0, 0)
            prep(1, 0, 1)
            with pool.Fori(1, 4) as p:
                prep(2 * p, p, 0)
                prep(2 * p + 1, p, 1)

        @block.scalar
        def _(act):
            def square(T):
                rows = cols_of(T)[1]
                act.wait_ge(s_x[T], 16)
                if T:
                    act.wait_ge(ss_done, T)
                nc.scalar.activation(squares[0:rows, :], x_tile(T), ACT.Square,
                                     accum_out=sumsq[0:rows, T:T + 1]).then_inc(ss_done, 1)

            def root(T):
                rows = cols_of(T)[1]
                act.wait_ge(ms_done, T + 1)
                nc.scalar.activation(std[0:rows, T:T + 1], meansq[0:rows, T:T + 1], ACT.Sqrt).then_inc(std_done, 1)

            def evac_v(T):
                rows = cols_of(T)[1]
                b = 4 + 2 * (T % 2)
                if T == 0:
                    act.wait_ge(pool_init, 2)
                act.wait_ge(v_done, T + 1)
                nc.scalar.activation(v_raw[0:rows, T, 0:VF // 2], ps[0:rows, b, 0:VF // 2], ACT.Copy)
                nc.scalar.activation(v_raw[0:rows, T, VF // 2:D_ATTN], ps[0:rows, b + 1, 0:D_ATTN - VF // 2], ACT.Copy)
                nc.scalar.activation(f_raw[0:rows, T, :], ps[0:rows, b + 1, D_ATTN - VF // 2:VF // 2],
                                     ACT.Copy).then_inc(v_evac, 1)

            square(0)
            root(0)
            for T in range(NB + 1):
                if T < NB:
                    square(T + 1)
                    root(T + 1)
                if T == 0:
                    for i in range(4):
                        act.wait_ge(s_wv[i], 16)
                        nc.scalar.activation(wv_hi[:, 2 * i:2 * i + 2, :], wv_raw[:, 2 * i:2 * i + 2, :],
                                             ACT.Copy).then_inc(wvhi_done, 1)
                k0, rows = cols_of(T)
                act.wait_ge(hn32_done, T + 1)
                nc.scalar.activation(hn_hi[:, :, k0:k0 + rows], hn32[T % 2][:, :, 0:rows], ACT.Copy).then_inc(hnhi_done, 1)
                if T >= 2:
                    evac_v(T - 2)

            def split_hi(n, slot, size=D):
                act.wait_ge(s_w[slot], 16 * (n // 2 + 1) if isinstance(n, int) else n * 8 + 16 - 8 * slot)
                act.wait_ge(proj_done, n - 1) if not isinstance(n, int) or n >= 2 else None
                dst = w_hi[:, slot, :, :].rearrange("p k c -> p (k c)")
                nc.scalar.activation(dst[:, 0:size], w_raw[:, slot, 0:size], ACT.Copy).then_inc(whi_done, 1)

            split_hi(0, 0)
            evac_v(NB - 1)
            split_hi(1, 1)
            evac_v(NB)

            nc.scalar.preload_act_table_set("natural_log_exp_and_others")
            act.wait_ge(lf_dve, 1)
            nc.scalar.activation(lf[1][:, :, :], lf[0][:, :, :], ACT.Abs).then_inc(lf_act, 1)
            act.wait_ge(lf_act, 1)
            nc.scalar.activation(lf[2][:, :, :], lf[1][:, :, :], ACT.Exp, scale=-1.0).then_inc(lf_act, 1)
            act.wait_ge(lf_dve, 2)
            nc.scalar.activation(lf[4][:, :, :], lf[3][:, :, :], ACT.Ln).then_inc(lf_act, 1)

            def from_banks(n, dst, func):
                b = banks(n)
                act.wait_ge(proj_done, n + 1)
                c0 = ALL_TOKENS[0][1]
                nc.scalar.activation(dst[:, 0:c0], ps[:, b, 0:c0], func)
                return nc.scalar.activation(dst[:, c0:TOK].rearrange("p (b c) -> p b c", b=2),
                                            ps[:, b + 1:b + 3, 0:ALL_TOKENS[1][1]], func)

            for n in range(N_EARLY):
                kind, j = ORDER[n]
                if kind == GATE:
                    act.wait_ge(xs_done, NB + 1)
                    if j:
                        act.wait_ge(glu_done, j)
                    from_banks(n, sig_gate, ACT.Sigmoid).then_inc(sig_done, 1)
                elif kind == SC_C:
                    if j:
                        act.wait_ge(cu_done, j)
                    from_banks(n, sc_c, ACT.Copy).then_inc(scc_done, 1)
                split_hi(n + 2, n % 2)

            def evac_q(n, p):
                act.wait_ge(proj_done, n + 1)
                act.wait_ge(s_cst, 32)
                act.wait_ge(cq_evac, 1)
                nc.scalar.activation(q_raw[:, bass.ds(p, 1), :].rearrange("p a (b c) -> p (a b) c", b=2), ps[:, 0:2, :], ACT.Copy,
                                     scale=float(HD) ** -0.5).then_inc(proj_evac, 1)

            def evac_k(n, p):
                act.wait_ge(proj_done, n + 1)
                c0 = ALL_TOKENS[0][1]
                dst = k_raw[:, bass.ds(p, 1), :].rearrange("p a c -> p (a c)")
                nc.scalar.activation(dst[:, 0:c0], ps[:, 3, 0:c0], ACT.Copy)
                nc.scalar.activation(dst[:, c0:TOK].rearrange("p (b c) -> p b c", b=2),
                                     ps[:, 4:6, 0:ALL_TOKENS[1][1]], ACT.Copy).then_inc(proj_evac, 1)

            with act.Fori(0, 3) as p:
                n = N_EARLY + 2 * p
                evac_q(n, p)
                split_hi(n + 2, 0)
                evac_k(n + 1, p)
                split_hi(n + 3, 1)

            def ln_root(r):
                act.wait_ge(ln_dve, 3 * r + 2)
                nc.scalar.activation(ln_std[:, 4 * r:4 * r + 4], ln_rstd[:, 4 * r:4 * r + 4], ACT.Sqrt).then_inc(ln_sqrt, 1)

            ln_root(0)
            evac_q(N_PROJ - 2, 3)
            split_hi(N_PROJ, 0, 2 * D_CONF)
            ln_root(1)
            evac_k(N_PROJ - 1, 3)
            for j in range(2):
                act.wait_ge(ln_back, j + 1)
                nc.scalar.activation(z[:, j, :].rearrange("p (b c) -> p b c", b=2), ps[:, 6:8, :], ACT.Identity, scale=prm[:, LN_G + j:LN_G + j + 1],
                                     bias=prm[:, LN_B + j:LN_B + j + 1]).then_inc(z_done, 1)
                act.wait_ge(z_done, j + 1)
                nc.scalar.activation(silu[:, j, :], z[:, j, :], ACT.Sigmoid).then_inc(zsig_done, 1)

            def prep(g, p, s, step):
                rows = slice(HD * s, HD * (s + 1))
                k = k_raw[rows, bass.ds(p, 1), :].rearrange("p a c -> p (a c)")
                if step == 0:
                    if not isinstance(g, int) or g >= 2:
                        act.wait_ge(pv_done, NU * (g - 1))
                    nc.scalar.activation(qm[s][0:HD, :], q_raw[rows, bass.ds(p, 1), :].rearrange("p a c -> p (a c)"), ACT.Copy)
                elif s == 0:
                    nc.scalar.activation(km[s][0:HD, :], k, ACT.Copy).then_inc(qk_hi, 1)
                else:
                    nc.scalar.activation(km[s][0:HD, :], k, ACT.Copy)
                    nc.scalar.activation(kx[s][HD:P, :], k, ACT.Copy).then_inc(qk_hi, 1)

            def r_rows(g, s):
                act.wait_ge(rt_done, g + 1)
                nc.scalar.activation(qm[s][HD:HD + 4, :].rearrange("p (b c) -> p b c", b=2), ps[HD:HD + 4, 2:4, :], ACT.Copy).then_inc(r_ready, 1)

            def invert(g, s, ci):
                C = 2 * g + ci
                last = NU * g + (NB + 1 if ci == 0 else NU)
                sums = slice(HD, P) if s == 0 else slice(0, HD)
                act.wait_ge(pv_done, last)
                if not isinstance(g, int) or C > 0:
                    act.wait_ge(o_evac, C)
                nc.scalar.activation(o_r0[sums, :], ps[sums, 6 + ci, :], ACT.Ln).then_inc(o_ln, 1)
                act.wait_ge(o_ln, C + 1)
                nc.scalar.activation(o_r0[sums, :], o_r0[sums, :], ACT.Exp, scale=-1.0).then_inc(o_inv, 1)

            def head(g, p, s, nxt):
                for u in range(NU):
                    U, b = NU * g + u, (NU * s + u) % RING
                    _, rows, _, n, _ = unit(u)
                    act.wait_ge(sc_done, U + 1)
                    if not isinstance(U, int) or U >= RING:
                        act.wait_ge(pv_done, U - RING + 1)
                    nc.scalar.activation(p32[0:rows, b, 0:n], ps[0:rows, (NU * s + u) % 2, 0:n], ACT.Exp).then_inc(exp_done, 1)
                    if nxt is not None:
                        if u in (0, 1):
                            prep(*nxt, u)
                        if u == 12:
                            r_rows(nxt[0], nxt[2])
                    if u == 11:
                        invert(g, s, 0)
                invert(g, s, 1)

            act.wait_ge(att_init, N_FILLS)
            act.wait_ge(proj_evac, N_PROJ - N_EARLY)
            act.wait_ge(proj_done, N_PROJ)
            nc.scalar.preload_act_table_set("natural_log_exp_and_others")
            prep(0, 0, 0, 0)
            prep(0, 0, 0, 1)
            for j in range(2):
                act.wait_ge(silu_done, j + 1)
                nc.scalar.activation(s_hi[:, j, :], silu[:, j, :], ACT.Copy).then_inc(shi_done, 1)
            r_rows(0, 0)
            for o in range(2):
                act.wait_ge(pw_done, o + 1)
                nc.scalar.activation(mix[:, 4 + o, :].rearrange("p (b c) -> p b c", b=2), ps[:, 6:8, :], ACT.Identity,
                                     bias=prm[:, B_PW + o:B_PW + o + 1]).then_inc(pw_evac, 1)
            head(0, 0, 0, (1, 0, 1))
            head(1, 0, 1, (2, 1, 0))
            with act.Fori(1, 3) as p:
                head(2 * p, p, 0, (2 * p + 1, p, 1))
                head(2 * p + 1, p, 1, (2 * p + 2, p + 1, 0))
            head(6, 3, 0, (7, 3, 1))
            head(7, 3, 1, None)

            def wo_split(w):
                act.wait_ge(s_wo[w % 2], 16 * (w // 2 + 1))
                if w < KT:
                    act.wait_ge(pv_done, NU * HEADS)
                elif w < 2 * KT - 1:
                    act.wait_ge(wo_used, (KT - 1) * (NB - 1) + w - KT + 1)
                else:
                    act.wait_ge(out_done, NB)
                nc.scalar.activation(wo_hi[:, w % KT, :], wo_raw[:, w % 2, :], ACT.Copy).then_inc(wohi_done, 1)

            def mix_split(v, t, slot):
                if not isinstance(v, int) or v >= 2:
                    act.wait_ge(out_done, v - 1)
                else:
                    act.wait_ge(o_evac, 2 * HEADS)
                nc.scalar.activation(mix_hi[:, slot, :, :], mix[:, :, bass.ds(t * P, P)], ACT.Copy).then_inc(mixhi_done, 1)

            def h_square(t):
                act.wait_ge(h_evac, NB + t + 1)
                if not isinstance(t, int) or t >= 1:
                    act.wait_ge(ss2, t)
                nc.scalar.activation(h_squares[:, :], h[:, bass.ds(t, 1), :].rearrange("p a c -> p (a c)"), ACT.Square,
                                     accum_out=sumsq[:, bass.ds(t, 1)]).then_inc(ss2, 1)
                act.wait_ge(ms2, t + 1)
                nc.scalar.activation(std[:, bass.ds(t, 1)], meansq[:, bass.ds(t, 1)], ACT.Sqrt).then_inc(std2, 1)

            def h_high(t):
                act.wait_ge(h32_done, t + 1)
                nc.scalar.activation(hn2_hi[:, :, bass.ds(t * P, P)], h32[:, :, :], ACT.Copy).then_inc(h2hi_done, 1)

            mix_split(0, 0, 0)
            for w in range(KT):
                wo_split(w)
            mix_split(1, 1, 1)
            with act.Fori(0, 3) as i:
                mix_split(2 * i + 2, 2 * i + 2, 0)
                mix_split(2 * i + 3, 2 * i + 3, 1)
            mix_split(NB, 0, 0)
            for w in range(KT, 2 * KT):
                wo_split(w)
            mix_split(NB + 1, 1, 1)
            h_square(0)
            with act.Fori(0, 3) as i:
                mix_split(NB + 2 * i + 2, 2 * i + 2, 0)
                h_square(2 * i + 1)
                h_high(2 * i)
                mix_split(NB + 2 * i + 3, 2 * i + 3, 1)
                h_square(2 * i + 2)
                h_high(2 * i + 1)
            h_square(NB - 1)
            h_high(NB - 2)
            h_high(NB - 1)

            def mw_split(r, dst, slot):
                act.wait_ge(s_m[slot], 8 * r + 16 - 8 * slot)
                nc.scalar.activation(dst, m_raw[:, slot, :], ACT.Copy).then_inc(mwhi_done, 1)

            def w1_split(q, i):
                mw_split(16 * q + i, w1_hi[:, i // 2, HALF * (i % 2):HALF * (i % 2 + 1)], i % 2)

            def w2_split(q, i):
                if i == 0:
                    act.wait_ge(out_done, 2 * NB + NB * q)
                mw_split(16 * q + 8 + i, w2_hi[:, i // 2, HALF * (i % 2):HALF * (i % 2 + 1)], i % 2)

            def hidden(q, i):
                G = 8 * q + i
                act.wait_ge(m1_done, G + 1)
                if i >= 2:
                    act.wait_ge(alo_done, G - 1)
                nc.scalar.activation(act32[:, i % 2, :], ps[:, i % 4, :], ACT.Relu).then_inc(relu_done, 1)
                w2_split(q, i)
                act.wait_ge(asq_done, G + 1)
                nc.scalar.activation(a_hi[:, i % 4, HALF * (i // 4):HALF * (i // 4 + 1)], act32[:, i % 2, :],
                                     ACT.Copy).then_inc(ahi_done, 1)

            for i in range(8):
                w1_split(0, i)
            with act.Fori(0, CH - 1) as q:
                for i in range(8):
                    hidden(q, i)
                for i in range(8):
                    if i == 0:
                        act.wait_ge(m1_done, 8 * q + 8)
                    w1_split(q + 1, i)
            for i in range(8):
                hidden(CH - 1, i)
            for t in range(NB):
                act.wait_ge(h_evac, 2 * NB + NB * (CH - 1) + t + 1)
                if t:
                    act.wait_ge(ss3, t)
                nc.scalar.activation(y_squares[:, :], h[:, t, :], ACT.Square, accum_out=sumsq[:, t:t + 1]).then_inc(ss3, 1)
                act.wait_ge(ms3, t + 1)
                nc.scalar.activation(std[:, t:t + 1], meansq[:, t:t + 1], ACT.Sqrt).then_inc(std3, 1)

        @block.vector
        def _(dve):
            def g_of(first, n):
                return prm[:, first:first + KT].unsqueeze(2).broadcast_to([P, KT, n])

            dve.wait_ge(s_consts, 32)
            nc.vector.tensor_copy(identb[:, :], consts_f[:, 0, :])
            nc.vector.tensor_copy(mask_qk[:, :], consts_f[:, 1, :])
            nc.vector.tensor_copy(mask_kq[:, :], consts_f[:, 2, :]).then_inc(masks_ready, 1)

            def mean_square(T):
                rows = cols_of(T)[1]
                dve.wait_ge(ss_done, T + 1)
                nc.vector.tensor_scalar(meansq[0:rows, T:T + 1], sumsq[0:rows, T:T + 1], 1.0 / D, EPS,
                                        ALU.mult, ALU.add).then_inc(ms_done, 1)

            def scale_x(T):
                rows = cols_of(T)[1]
                dve.wait_ge(std_done, T + 1)
                nc.vector.reciprocal(rstd[0:rows, T:T + 1], std[0:rows, T:T + 1]).then_inc(rstd_done, 1)
                dve.wait_ge(rstd_done, T + 1)
                if T >= 2:
                    dve.wait_ge(tr_done, T - 1)
                nc.vector.tensor_scalar(xs[0:rows, T % 2, :], x_tile(T), rstd[0:rows, T:T + 1], None,
                                        ALU.mult).then_inc(xs_done, 1)

            mean_square(0)
            scale_x(0)
            for T in range(NB + 1):
                if T < NB:
                    mean_square(T + 1)
                    scale_x(T + 1)
                if T == 0:
                    dve.wait_ge(s_par, 16)
                k0, rows = cols_of(T)
                dve.wait_ge(tr_done, T + 1)
                if T >= 2:
                    dve.wait_ge(hnlo_done, T - 1)
                b = 2 * (T % 2)
                nc.vector.tensor_tensor(hn32[T % 2][:, :, 0:rows],
                                        ps[:, b:b + 2, :].rearrange("p b (k c) -> p (b k) c", c=P)[:, :, 0:rows],
                                        g_of(G1, rows), ALU.mult).then_inc(hn32_done, 1)
                if T == 0:
                    dve.wait_ge(masks_ready, 1)
                    for i in range(4):
                        dve.wait_ge(wvhi_done, i + 1)
                        nc.vector.tensor_tensor(wv_lo[:, 2 * i:2 * i + 2, :], wv_raw[:, 2 * i:2 * i + 2, :],
                                                wv_hi[:, 2 * i:2 * i + 2, :].bitcast(F32), ALU.subtract).then_inc(wvlo_done, 1)
                dve.wait_ge(hnhi_done, T + 1)
                nc.vector.tensor_tensor(hn_lo[:, :, k0:k0 + rows], hn32[T % 2][:, :, 0:rows],
                                        hn_hi[:, :, k0:k0 + rows].bitcast(F32), ALU.subtract).then_inc(hnlo_done, 1)

            def split_lo(n, slot, size=D):
                dve.wait_ge(whi_done, n + 1)
                hi = w_hi[:, slot, :, :].rearrange("p k c -> p (k c)").bitcast(F32)
                lo = w_lo[:, slot, :, :].rearrange("p k c -> p (k c)")
                nc.vector.tensor_tensor(lo[:, 0:size], w_raw[:, slot, 0:size], hi[:, 0:size], ALU.subtract).then_inc(wlo_done, 1)

            split_lo(0, 0)
            split_lo(1, 1)
            dve.wait_ge(xs_done, NB + 1)
            nc.vector.memset(glu[0][:, 0:PAD], 0.0)
            nc.vector.memset(glu[1][:, 0:PAD], 0.0).then_inc(pad_done, 1)
            dve.wait_ge(v_evac, NB + 1)
            step = [0]

            def chain(ins):
                ins.then_inc(lf_dve, 1)
                step[0] += 1

            chain(nc.vector.tensor_tensor(lf[0][:, :, :], f_raw[:, :, :],
                                          prm[:, B_F:B_F + HEADS].unsqueeze(1).broadcast_to([P, NB + 1, HEADS]), ALU.add))
            dve.wait_ge(lf_act, 2)
            chain(nc.vector.tensor_scalar(lf[3][:, :, :], lf[2][:, :, :], 1.0, None, ALU.add))
            dve.wait_ge(lf_dve, 2)
            chain(nc.vector.tensor_scalar(lf[5][:, :, :], lf[3][:, :, :], 1.0, None, ALU.subtract))
            dve.wait_ge(lf_dve, 3)
            chain(nc.vector.tensor_tensor(lf[6][:, :, :], lf[2][:, :, :], lf[5][:, :, :], ALU.subtract))
            chain(nc.vector.reciprocal(lf[7][:, :, :], lf[3][:, :, :]))
            dve.wait_ge(lf_dve, 5)
            chain(nc.vector.tensor_tensor(lf[8][:, :, :], lf[6][:, :, :], lf[7][:, :, :], ALU.mult))
            dve.wait_ge(lf_dve, 6)
            dve.wait_ge(lf_act, 3)
            chain(nc.vector.tensor_tensor(lf[9][:, :, :], lf[8][:, :, :], lf[4][:, :, :], ALU.add))
            dve.wait_ge(lf_dve, 7)
            chain(nc.vector.scalar_tensor_tensor(lf[6][:, :, :].rearrange("p t h -> p (t h)"),
                                                 lf[0][:, :, :].rearrange("p t h -> p (t h)"), 0.0,
                                                 lf[9][:, :, :].rearrange("p t h -> p (t h)"), ALU.min, ALU.subtract))

            def projected(n, dst, other):
                b = banks(n)
                dve.wait_ge(proj_done, n + 1)
                c0 = ALL_TOKENS[0][1]
                two = "p (b c) -> p b c"
                nc.vector.tensor_tensor(dst[:, 0:c0], ps[:, b, 0:c0], other[:, 0:c0], ALU.mult)
                return nc.vector.tensor_tensor(dst[:, c0:TOK].rearrange(two, b=2), ps[:, b + 1:b + 3, 0:ALL_TOKENS[1][1]],
                                               other[:, c0:TOK].rearrange(two, b=2), ALU.mult)

            def conv_first(j):
                nc.vector.tensor_scalar(dw[:, j, :], glu[j][:, 0:SEQ], prm[:, W_DW + CONF_K * j:W_DW + CONF_K * j + 1],
                                        prm[:, B_DW + j:B_DW + j + 1], ALU.mult, ALU.add).then_inc(conv_step, 1)

            def conv_tap(j, k):
                dve.wait_ge(conv_step, CONF_K * j + k)
                nc.vector.scalar_tensor_tensor(dw[:, j, :], glu[j][:, bass.ds(k, SEQ)], prm[:, bass.ds(W_DW + CONF_K * j + k, 1)],
                                               dw[:, j, :], ALU.mult, ALU.add).then_inc(conv_step, 1)

            for n in range(N_EARLY):
                kind, j = ORDER[n]
                if kind == CONF_A:
                    dve.wait_ge(pad_done, 1)
                    dve.wait_ge(sig_done, j + 1)
                    projected(n, glu[j][:, PAD:PAD + TOK], sig_gate).then_inc(glu_done, 1)
                elif kind == SC_U:
                    dve.wait_ge(scc_done, j + 1)
                    if j:
                        dve.wait_ge(sc_step, 4)
                    projected(n, sc_cu, sc_c).then_inc(cu_done, 1)
                    dve.wait_ge(cu_done, j + 1)
                    for k in range(SC_K):
                        w = prm[:, W_SC + SC_K * j + k:W_SC + SC_K * j + k + 1]
                        src = sc_cu[:, META - SC_K + 1 + k:META - SC_K + 1 + k + SEQ]
                        if k == 0:
                            nc.vector.tensor_scalar(mix[:, 6 + j, :], src, w, None, ALU.mult).then_inc(sc_step, 1)
                        else:
                            dve.wait_ge(sc_step, 4 * j + k)
                            nc.vector.scalar_tensor_tensor(mix[:, 6 + j, :], src, w, mix[:, 6 + j, :],
                                                           ALU.mult, ALU.add).then_inc(sc_step, 1)
                elif kind == SC_B:
                    dve.wait_ge(sc_step, 4 * j + SC_K)
                    dve.wait_ge(proj_done, n + 1)
                    b = banks(n)
                    view = mix[:, 6 + j, :].rearrange("p (b c) -> p b c", b=2)
                    nc.vector.tensor_tensor(view, ps[:, b:b + 2, :], view, ALU.mult).then_inc(sc_step, 1)
                split_lo(n + 2, n % 2)
                if n == 1:
                    dve.wait_ge(lft_done, 1)
                    nc.vector.tensor_copy(lf_t[:, 0:400], ps[0:HEADS, 6, 0:400])
                    nc.vector.tensor_copy(lf_t[:, 400:912], ps[0:HEADS, 7, :]).then_inc(lft_evac, 1)
                    dve.wait_ge(lft_done, 2)
                    nc.vector.tensor_copy(lf_t[:, 912:TOK], ps[0:HEADS, 6, 0:P]).then_inc(lft_evac, 1)
                    dve.wait_ge(lft_evac, 2)
                    chain(nc.vector.tensor_tensor_scan(c_t[:, :], lf_t[:, :], lf_t[:, :], 0.0, ALU.add, ALU.bypass))
                    dve.wait_ge(lf_dve, 9)
                    chain(nc.vector.tensor_scalar(c_neg[:, :], c_t[:, :], -1.0, None, ALU.mult))
                    dve.wait_ge(lf_dve, 10)
                    dve.wait_ge(v_done, NB + 1)
                    chain(nc.vector.tensor_copy(c_hi[:, :], c_neg[:, :]))
                    dve.wait_ge(lf_dve, 11)
                    chain(nc.vector.tensor_tensor(c_lo[:, :], c_neg[:, :], c_hi[:, :].bitcast(F32), ALU.subtract))
                if n == 4:
                    dve.wait_ge(cq_tr, 1)
                    nc.vector.tensor_copy(c_q[:, :, :].rearrange("p h t -> p t h"),
                                          ps[:, 6, 0:NB * HEADS].rearrange("p (t h) -> p t h", h=HEADS)).then_inc(cq_evac, 1)
                if n == 4:
                    dve.wait_ge(glu_done, 2)
                    conv_first(0)
                if n >= 4:
                    for i in range(5):
                        conv_tap(0, 5 * (n - 4) + i + 1)
            conv_first(1)
            with dve.Fori(0, 3) as p:
                for i in range(2):
                    split_lo(N_EARLY + 2 * p + 2 + i, i)
                    for k in range(5):
                        conv_tap(1, 10 * p + 5 * i + k + 1)

            def ln_statistics(r):
                dve.wait_ge(ln_tr, r + 1)
                view = ps[:, 6:8, :].rearrange("p b (t c) -> p (b t) c", c=D_CONF)
                for i in range(4):
                    ins = nc.vector.bn_stats(ln_stats[:, 4 * r + i, :], view[:, i, :])
                ins.then_inc(ln_dve, 1)
                dve.wait_ge(ln_dve, 3 * r + 1)
                for i in range(4):
                    nc.vector.bn_aggr(ln_mv[:, 4 * r + i, :], ln_stats[:, 4 * r + i, :]).then_inc(ln_norm, 1)
                dve.wait_ge(ln_norm, 8 * r + 4)
                nc.vector.tensor_scalar(ln_rstd[:, 4 * r:4 * r + 4], ln_mv[:, 4 * r:4 * r + 4, 1], EPS, None,
                                        ALU.add).then_inc(ln_dve, 1)
                dve.wait_ge(ln_sqrt, r + 1)
                nc.vector.reciprocal(ln_rstd[:, 4 * r:4 * r + 4], ln_std[:, 4 * r:4 * r + 4]).then_inc(ln_dve, 1)
                dve.wait_ge(ln_dve, 3 * r + 3)
                for i in range(4):
                    t = 4 * r + i
                    nc.vector.tensor_scalar(normed[:, t, :], view[:, i, :], ln_mv[:, t, 0:1], ln_rstd[:, t:t + 1],
                                            ALU.subtract, ALU.mult).then_inc(ln_norm, 1)

            dve.wait_ge(conv_step, 2 * CONF_K)
            ln_statistics(0)
            ln_statistics(1)
            split_lo(N_PROJ, 0, 2 * D_CONF)

            def prep(g, p, s, step):
                rows = slice(HD * s, HD * (s + 1))
                q = q_raw[rows, bass.ds(p, 1), :].rearrange("p a c -> p (a c)")
                k = k_raw[rows, bass.ds(p, 1), :].rearrange("p a c -> p (a c)")
                if step == 0:
                    dve.wait_ge(qk_hi, g + 1)
                    nc.vector.tensor_copy(qx[s][HD:P, :], q).then_inc(qk_dup, 1)
                elif step == 1:
                    nc.vector.tensor_copy(kx[s][0:HD, :], k)
                elif s == 0:
                    nc.vector.tensor_tensor(kx[s][HD:P, :], k, km[s][0:HD, :].bitcast(F32), ALU.subtract).then_inc(qk_lo, 1)
                else:
                    dve.wait_ge(qk_dup, g + 1)
                    nc.vector.tensor_tensor(qx[s][0:HD, :], q, qx[s][HD:P, :].bitcast(F32), ALU.subtract).then_inc(qk_lo, 1)

            def row_max(g, s, m):
                _, _, w, parts = MAXES[m]
                G, b = NM * g + m, 2 + 2 * ((NM * s + m) % 2)
                dve.wait_ge(mx_mm, G + 1)
                nc.vector.tensor_reduce(mx[:, m:m + 1], ps[:, b:b + parts, 0:w], AX.XY if parts > 1 else AX.X,
                                        ALU.max).then_inc(mx_red, 1)

            def shift(g, hd):
                def nxt(ins, i):
                    ins.then_inc(r_step, 1)
                    dve.wait_ge(r_step, 6 * g + i + 1)

                dve.wait_ge(mx_red, NM * (g + 1))
                nxt(nc.vector.tensor_tensor(mx[:, 7:8], mx[:, 7:8], mx[:, 8:9], ALU.max), 0)
                c = c_q[:, bass.ds(hd, 1), :].rearrange("p a t -> p (a t)")
                nxt(nc.vector.tensor_tensor(m_q[:, :], mx[:, 0:NB], c, ALU.add), 1)
                nxt(nc.vector.tensor_tensor(r_q[:, :], c, m_q[:, :], ALU.subtract), 2)
                nxt(nc.vector.tensor_copy(r_hi[:, :], r_q[:, :]), 3)
                if not isinstance(g, int) or g >= 1:
                    dve.wait_ge(rt_done, g)
                nxt(nc.vector.tensor_copy(r_pad[:, :, HD + 2], r_hi[:, :].bitcast(F32)), 4)
                nxt(nc.vector.tensor_tensor(r_pad[:, :, HD + 3], r_q[:, :], r_hi[:, :].bitcast(F32), ALU.subtract), 5)

            def finish(g, p, s, ci):
                C, c = 2 * g + ci, 1 - ci
                o, sums = (slice(0, HD), slice(HD, P)) if s == 0 else (slice(HD, P), slice(0, HD))
                dve.wait_ge(o_inv, C + 1)
                nc.vector.tensor_tensor(o_t[sums, :], ps[sums, 6 + ci, :], o_r0[sums, :], ALU.mult).then_inc(o_step, 1)
                dve.wait_ge(o_step, 2 * C + 1)
                nc.vector.scalar_tensor_tensor(o_r1[o, :], o_t[sums, :], 2.0, o_r0[sums, :], ALU.subtract, ALU.mult).then_inc(o_step, 1)
                dve.wait_ge(o_step, 2 * C + 2)
                nc.vector.scalar_tensor_tensor(mix[o, bass.ds(p, 1), HALF * c:HALF * (c + 1)].rearrange("p a c -> p (a c)"),
                                               ps[o, 6 + ci, :], -1.0, o_r1[o, :], ALU.mult, ALU.mult).then_inc(o_evac, 1)

            def head(g, p, s, nxt):
                for u in range(NU):
                    if nxt is not None:
                        if u < 3:
                            prep(*nxt, u)
                        for m in (2 * (u - 4), 2 * (u - 4) + 1):
                            if u >= 4 and m < NM:
                                row_max(nxt[0], nxt[2], m)
                        if u == 9:
                            shift(nxt[0], nxt[0])
                    if u == 12:
                        finish(g, p, s, 0)
                finish(g, p, s, 1)

            for i in range(3):
                if i == 0:
                    dve.wait_ge(att_init, N_FILLS)
                prep(0, 0, 0, i)
            for j in range(2):
                dve.wait_ge(zsig_done, j + 1)
                nc.vector.tensor_tensor(silu[:, j, :], z[:, j, :], silu[:, j, :], ALU.mult).then_inc(silu_done, 1)
                dve.wait_ge(shi_done, j + 1)
                nc.vector.tensor_tensor(s_lo[:, j, :], silu[:, j, :], s_hi[:, j, :].bitcast(F32), ALU.subtract).then_inc(slo_done, 1)
            for m in range(NM):
                row_max(0, 0, m)
            shift(0, 0)
            dve.wait_ge(pw_done, 2)
            head(0, 0, 0, (1, 0, 1))
            head(1, 0, 1, (2, 1, 0))
            with dve.Fori(1, 3) as p:
                head(2 * p, p, 0, (2 * p + 1, p, 1))
                head(2 * p + 1, p, 1, (2 * p + 2, p + 1, 0))
            head(6, 3, 0, (7, 3, 1))
            head(7, 3, 1, None)

            def wo_split(w):
                dve.wait_ge(wohi_done, w + 1)
                nc.vector.tensor_tensor(wo_lo[:, w % KT, :], wo_raw[:, w % 2, :], wo_hi[:, w % KT, :].bitcast(F32),
                                        ALU.subtract).then_inc(wolo_done, 1)

            def mix_split(v, t, slot):
                dve.wait_ge(mixhi_done, v + 1)
                nc.vector.tensor_tensor(mix_lo[:, slot, :, :], mix[:, :, bass.ds(t * P, P)],
                                        mix_hi[:, slot, :, :].bitcast(F32), ALU.subtract).then_inc(mixlo_done, 1)

            def residual(v, t, c, slot):
                dve.wait_ge(out_done, v + 1)
                dst = h[:, bass.ds(t, 1), HALF * c:HALF * (c + 1)].rearrange("p a c -> p (a c)")
                nc.vector.tensor_tensor(dst, ps[:, slot, :], dst, ALU.add).then_inc(h_evac, 1)

            def h_scale(t, slot):
                dve.wait_ge(ss2, t + 1)
                nc.vector.tensor_scalar(meansq[:, bass.ds(t, 1)], sumsq[:, bass.ds(t, 1)], 1.0 / D, EPS,
                                        ALU.mult, ALU.add).then_inc(ms2, 1)
                dve.wait_ge(std2, t + 1)
                nc.vector.reciprocal(rstd[:, bass.ds(t, 1)], std[:, bass.ds(t, 1)]).then_inc(rstd2, 1)
                dve.wait_ge(rstd2, t + 1)
                nc.vector.tensor_scalar(hs[:, slot, :], h[:, bass.ds(t, 1), :].rearrange("p a c -> p (a c)"),
                                        rstd[:, bass.ds(t, 1)], None, ALU.mult).then_inc(hs_done, 1)

            def h_split(t, slot):
                dve.wait_ge(tr2, t + 1)
                if isinstance(t, int) and t == NB - 1:
                    dve.wait_ge(h2lo_done, t)
                b = 4 + 2 * slot
                nc.vector.tensor_tensor(h32[:, :, :], ps[:, b:b + 2, :].rearrange("p b (k c) -> p (b k) c", c=P),
                                        g_of(G2, P), ALU.mult).then_inc(h32_done, 1)
                dve.wait_ge(h2hi_done, t + 1)
                nc.vector.tensor_tensor(hn2_lo[:, :, bass.ds(t * P, P)], h32[:, :, :],
                                        hn2_hi[:, :, bass.ds(t * P, P)].bitcast(F32), ALU.subtract).then_inc(h2lo_done, 1)

            for i in range(NB):
                dve.wait_ge(s_xr[i], 16)
            mix_split(0, 0, 0)
            for w in range(KT):
                wo_split(w)
            mix_split(1, 1, 1)
            residual(0, 0, 0, 0)
            with dve.Fori(0, 3) as i:
                mix_split(2 * i + 2, 2 * i + 2, 0)
                residual(2 * i + 1, 2 * i + 1, 0, 1)
                mix_split(2 * i + 3, 2 * i + 3, 1)
                residual(2 * i + 2, 2 * i + 2, 0, 0)
            mix_split(NB, 0, 0)
            residual(NB - 1, NB - 1, 0, 1)
            for w in range(KT, 2 * KT):
                wo_split(w)
            mix_split(NB + 1, 1, 1)
            residual(NB, 0, 1, 0)
            h_scale(0, 0)
            with dve.Fori(0, 3) as i:
                mix_split(NB + 2 * i + 2, 2 * i + 2, 0)
                residual(NB + 2 * i + 1, 2 * i + 1, 1, 1)
                h_scale(2 * i + 1, 1)
                h_split(2 * i, 0)
                mix_split(NB + 2 * i + 3, 2 * i + 3, 1)
                residual(NB + 2 * i + 2, 2 * i + 2, 1, 0)
                h_scale(2 * i + 2, 0)
                h_split(2 * i + 1, 1)
            residual(2 * NB - 1, NB - 1, 1, 1)
            h_scale(NB - 1, 1)
            h_split(NB - 2, 0)
            h_split(NB - 1, 1)

            def mw_split(r, lo, hi, slot):
                dve.wait_ge(mwhi_done, r + 1)
                nc.vector.tensor_tensor(lo, m_raw[:, slot, :], hi.bitcast(F32), ALU.subtract).then_inc(mwlo_done, 1)

            def w1_split(q, i):
                c = slice(HALF * (i % 2), HALF * (i % 2 + 1))
                mw_split(16 * q + i, w1_lo[:, i // 2, c], w1_hi[:, i // 2, c], i % 2)

            def w2_split(q, i):
                c = slice(HALF * (i % 2), HALF * (i % 2 + 1))
                mw_split(16 * q + 8 + i, w2_lo[:, i // 2, c], w2_hi[:, i // 2, c], i % 2)

            def hidden(q, i):
                G = 8 * q + i
                dve.wait_ge(relu_done, G + 1)
                nc.vector.tensor_tensor(act32[:, i % 2, :], act32[:, i % 2, :], act32[:, i % 2, :], ALU.mult).then_inc(asq_done, 1)
                w2_split(q, i)
                dve.wait_ge(ahi_done, G + 1)
                c = slice(HALF * (i // 4), HALF * (i // 4 + 1))
                nc.vector.tensor_tensor(a_lo[:, i % 4, c], act32[:, i % 2, :], a_hi[:, i % 4, c].bitcast(F32),
                                        ALU.subtract).then_inc(alo_done, 1)

            def accumulate(q, t):
                b = 4 + 2 * (t % 2)
                dve.wait_ge(out_done, 2 * NB + NB * q + t + 1)
                dst = h[:, t, :].rearrange("p (b c) -> p b c", b=2)
                nc.vector.tensor_tensor(dst, ps[:, b:b + 2, :], dst, ALU.add).then_inc(h_evac, 1)

            for i in range(8):
                w1_split(0, i)
            with dve.Fori(0, CH - 1) as q:
                for i in range(8):
                    hidden(q, i)
                for t in range(NB):
                    w1_split(q + 1, t)
                    accumulate(q, t)
            for i in range(8):
                hidden(CH - 1, i)

            def output(t):
                dve.wait_ge(ss3, t + 1)
                nc.vector.tensor_scalar(meansq[:, t:t + 1], sumsq[:, t:t + 1], 1.0 / D, EPS, ALU.mult, ALU.add).then_inc(ms3, 1)
                dve.wait_ge(std3, t + 1)
                nc.vector.reciprocal(rstd[:, t:t + 1], std[:, t:t + 1]).then_inc(rstd3, 1)
                dve.wait_ge(rstd3, t + 1)
                if t >= 2:
                    dve.wait_ge(s_out[t % 2], 16 * (t // 2))
                nc.vector.scalar_tensor_tensor(y[:, t % 2, :], h[:, t, :], rstd[:, t:t + 1], g_row[:, :],
                                               ALU.mult, ALU.mult).then_inc(y_done, 1)

            for t in range(NB):
                accumulate(CH - 1, t)
                if t == 0:
                    dve.wait_ge(s_g, 16)
                output(t)

        @block.tensor
        def _(pe):
            def three(dst, stat, mov, first, last):
                nc.tensor.matmul(dst, stat[0], mov[0], start=first, stop=False)
                nc.tensor.matmul(dst, stat[0], mov[1], start=False, stop=False)
                return nc.tensor.matmul(dst, stat[1], mov[0], start=False, stop=last)

            def transpose_x(T):
                rows = cols_of(T)[1]
                pe.wait_ge(xs_done, T + 1)
                if T >= 2:
                    pe.wait_ge(hn32_done, T - 1)
                for k in range(KT):
                    ins = nc.tensor.transpose(ps[:, 2 * (T % 2) + k // 4, P * (k % 4):P * (k % 4) + rows],
                                              xs[0:rows, T % 2, P * k:P * (k + 1)], ident[0:rows, 0:rows])
                ins.then_inc(tr_done, 1)

            def project_v(T):
                k0, rows = cols_of(T)
                pe.wait_ge(hnlo_done, T + 1)
                pe.wait_ge(wvlo_done, 4)
                if T >= 2:
                    pe.wait_ge(v_evac, T - 1)
                b = 4 + 2 * (T % 2)
                n = VF // 2
                for i in range(2):
                    for k in range(KT):
                        ins = three(ps[0:rows, b + i, 0:n], (hn_hi[:, k, k0:k0 + rows], hn_lo[:, k, k0:k0 + rows]),
                                    (wv_hi[:, k, n * i:n * (i + 1)], wv_lo[:, k, n * i:n * (i + 1)]), k == 0, k == KT - 1)
                ins.then_inc(v_done, 1)

            pe.wait_ge(s_consts, 32)
            transpose_x(0)
            for T in range(NB + 1):
                if T < NB:
                    transpose_x(T + 1)
                project_v(T)

            def project(n, slot, tokens):
                pe.wait_ge(wlo_done, n + 1)
                for k in range(KT):
                    stat = (w_hi[:, slot, k, :], w_lo[:, slot, k, :])
                    for a, b_ in ((0, 0), (0, 1), (1, 0)):
                        for i, (c0, width) in enumerate(tokens):
                            mov = (hn_hi, hn_lo)[b_][:, k, c0:c0 + width]
                            ins = nc.tensor.matmul(ps[:, 3 * slot + i, 0:width], stat[a], mov,
                                                   start=(k == 0 and a + b_ == 0), stop=(k == KT - 1 and a == 1))
                ins.then_inc(proj_done, 1)

            for n in range(N_EARLY):
                kind, j = ORDER[n]
                if n == 1:
                    pe.wait_ge(v_evac, NB + 1)
                elif n >= 2:
                    before, jb = ORDER[n - 2]
                    if before == GATE:
                        pe.wait_ge(sig_done, jb + 1)
                    elif before == CONF_A:
                        pe.wait_ge(glu_done, jb + 1)
                    elif before == SC_C:
                        pe.wait_ge(scc_done, jb + 1)
                    elif before == SC_U:
                        pe.wait_ge(cu_done, jb + 1)
                    else:
                        pe.wait_ge(sc_step, 4 * jb + 4)
                project(n, n % 2, REAL_TOKENS if kind == SC_B else ALL_TOKENS)
                if n == 1:
                    pe.wait_ge(lf_dve, 8)
                    for T in range(NB + 1):
                        k0, rows = cols_of(T)
                        b, c0 = (6, k0) if T < 4 else (7, k0 - 400)
                        if T == NB:
                            ins.then_inc(lft_done, 1)
                            pe.wait_ge(lft_evac, 1)
                            b, c0 = 6, 0
                        ins = nc.tensor.transpose(ps[0:HEADS, b, c0:c0 + rows], lf[6][0:rows, T, :], ident[0:rows, 0:rows])
                    ins.then_inc(lft_done, 1)
                if n == 3:
                    pe.wait_ge(lf_dve, 9)
                    pe.wait_ge(lft_evac, 2)
                    for t in range(NB):
                        ins = nc.tensor.transpose(ps[:, 6, HEADS * t:HEADS * (t + 1)],
                                                  c_t[:, META + P * t:META + P * (t + 1)], ident[0:HEADS, 0:HEADS])
                    ins.then_inc(cq_tr, 1)

            def ln_transposes(r):
                pe.wait_ge(conv_step, 2 * CONF_K)
                if r == 0:
                    pe.wait_ge(cq_evac, 1)
                else:
                    pe.wait_ge(ln_norm, 8)
                for i in range(4):
                    t = 4 * r + i
                    for j in range(2):
                        c0 = D_CONF * (i % 2) + P * j
                        ins = nc.tensor.transpose(ps[:, 6 + i // 2, c0:c0 + P], dw[:, j, P * t:P * (t + 1)], ident[:, :])
                ins.then_inc(ln_tr, 1)

            def queries(n):
                if isinstance(n, int) and n == N_EARLY:
                    pe.wait_ge(cu_done, 2)
                elif not isinstance(n, int) or n > N_EARLY:
                    pe.wait_ge(proj_evac, n - N_EARLY - 1)
                project(n, 0, REAL_TOKENS)

            def keys(n):
                if isinstance(n, int) and n == N_EARLY + 1:
                    pe.wait_ge(sc_step, 8)
                else:
                    pe.wait_ge(proj_evac, n - N_EARLY - 1)
                project(n, 1, ALL_TOKENS)

            queries(N_EARLY)
            keys(N_EARLY + 1)
            with pe.Fori(1, 3) as p:
                queries(N_EARLY + 2 * p)
                keys(N_EARLY + 2 * p + 1)
            ln_transposes(0)
            queries(N_PROJ - 2)
            ln_transposes(1)
            keys(N_PROJ - 1)
            for j in range(2):
                if j == 0:
                    pe.wait_ge(ln_norm, 16)
                else:
                    pe.wait_ge(z_done, 1)
                for t in range(NB):
                    ins = nc.tensor.transpose(ps[:, 6 + t // 4, P * (t % 4):P * (t % 4 + 1)],
                                              normed[:, t, P * j:P * (j + 1)], ident[:, :])
                ins.then_inc(ln_back, 1)

            def row_max(g, s, m):
                block_, c0, w, parts = MAXES[m]
                G, b = NM * g + m, 2 + 2 * ((NM * s + m) % 2)
                if m == 0:
                    pe.wait_ge(qk_hi, g + 1)
                    pe.wait_ge(s_c[s], 16 * (g // 2 + 1) if isinstance(g, int) else 8 * g + 16 - 8 * s)
                    if not isinstance(g, int) or g >= 1:
                        pe.wait_ge(r_ready, g)
                if not isinstance(G, int) or G >= 2:
                    pe.wait_ge(mx_red, G - 1)
                last = c0 + w * parts == META + P * (block_ + 1)
                for i in range(parts):
                    masked = last and i == parts - 1
                    a = c0 + w * i
                    ins = nc.tensor.matmul(ps[:, b + i, 0:w], qm[s][0:HD + 2, P * block_:P * (block_ + 1)],
                                           km[s][0:HD + 2, a:a + w], start=True, stop=not masked)
                    if masked:
                        ins = nc.tensor.matmul(ps[:, b + i, w - P:w], identb[:, :], mask_qk[:, :], start=False, stop=True)
                ins.then_inc(mx_mm, 1)

            def r_transposes(g):
                pe.wait_ge(r_step, 6 * g + 6)
                for t in range(NB):
                    ins = nc.tensor.transpose(ps[0:HD + 4, 2 + t // 4, P * (t % 4):P * (t % 4 + 1)], r_pad[:, t, :], ident[:, :])
                ins.then_inc(rt_done, 1)

            def scores(g, s, u):
                U, b = NU * g + u, (NU * s + u) % 2
                k0, rows, q0, n, diagonal = unit(u)
                if u == 0:
                    pe.wait_ge(qk_lo, g + 1)
                    pe.wait_ge(qk_lo2, g + 1)
                    pe.wait_ge(r_ready, g + 1)
                if not isinstance(U, int) or U >= 2:
                    pe.wait_ge(exp_done, U - 1)
                dst = ps[0:rows, b, 0:n]
                nc.tensor.matmul(dst, km[s][0:HD + 4, k0:k0 + rows], qm[s][0:HD + 4, q0:q0 + n], start=True, stop=False)
                ins = nc.tensor.matmul(dst, kx[s][:, k0:k0 + rows], qx[s][:, q0:q0 + n], start=False, stop=not diagonal)
                if diagonal:
                    ins = nc.tensor.matmul(ps[:, b, 0:P], identb[:, :], mask_kq[:, :], start=False, stop=True)
                ins.then_inc(sc_done, 1)

            def weigh(g, s, u):
                U, b = NU * g + u, (NU * s + u) % RING
                _, rows, q0, n, _ = unit(u)
                c, T = UNITS[u]
                ci = 1 - c
                pe.wait_ge(exp_done, U + 1)
                if u == 0:
                    pe.wait_ge(v_ready, g + 1)
                if T == 0:
                    if isinstance(g, int) and g == 0:
                        pe.wait_ge(pw_evac, 2)
                    else:
                        pe.wait_ge(o_evac, 2 * g + ci - 1)
                last = T == UNITS[NB][1] if c == 1 else T == UNITS[NU - 1][1]
                c0 = q0 - HALF * c
                ins = nc.tensor.matmul(ps[:, 6 + ci, c0:c0 + n], v_one[s][0:rows, T, :], p32[0:rows, b, 0:n],
                                       start=T == 0, stop=last)
                ins.then_inc(pv_done, 1)

            def head(g, s, nxt):
                for u in range(NU):
                    scores(g, s, u)
                    if nxt is not None:
                        for m in (2 * (u - 4), 2 * (u - 4) + 1):
                            if u >= 4 and m < NM:
                                row_max(nxt[0], nxt[1], m)
                        if u == 12:
                            r_transposes(nxt[0])
                    if u >= LAG:
                        weigh(g, s, u - LAG)
                for u in range(NU - LAG, NU):
                    weigh(g, s, u)

            def pointwise(o):
                pe.wait_ge(slo_done, 2)
                pe.wait_ge(wlo_done, N_PROJ + 1)
                if o:
                    pe.wait_ge(pw_evac, 1)
                for k in range(2):
                    c0 = D_CONF * k + P * o
                    stat = [w[:, 0, :, :].rearrange("p k c -> p (k c)")[:, c0:c0 + P] for w in (w_hi, w_lo)]
                    for i in range(2):
                        c = slice(HALF * i, HALF * (i + 1))
                        ins = three(ps[:, 6 + i, :], stat, (s_hi[:, k, c], s_lo[:, k, c]), k == 0, k == 1)
                ins.then_inc(pw_done, 1)

            pe.wait_ge(att_init, N_FILLS)
            pe.wait_ge(proj_evac, N_PROJ - N_EARLY)
            for m in range(NM):
                row_max(0, 0, m)
            pe.wait_ge(z_done, 2)
            r_transposes(0)
            pointwise(0)
            pointwise(1)
            head(0, 0, (1, 1))
            head(1, 1, (2, 0))
            with pe.Fori(1, 3) as p:
                head(2 * p, 0, (2 * p + 1, 1))
                head(2 * p + 1, 1, (2 * p + 2, 0))
            head(6, 0, (7, 1))
            head(7, 1, None)

            def project_out(v, b, slot):
                pe.wait_ge(mixlo_done, v + 1)
                if not isinstance(v, int) or v >= 2:
                    pe.wait_ge(h_evac, v - 1)
                for k in range(KT):
                    pe.wait_ge(wolo_done, KT * b + k + 1)
                    ins = three(ps[:, slot, :], (mix_hi[:, slot, k, :], mix_lo[:, slot, k, :]),
                                (wo_hi[:, k, :], wo_lo[:, k, :]), k == 0, k == KT - 1)
                    if b == 0 and k < KT - 1:
                        ins.then_inc(wo_used, 1)
                ins.then_inc(out_done, 1)

            def transpose_h(t, slot):
                pe.wait_ge(hs_done, t + 1)
                if not isinstance(t, int) or t >= 2:
                    pe.wait_ge(h32_done, t - 1)
                for k in range(KT):
                    ins = nc.tensor.transpose(ps[:, 4 + 2 * slot + k // 4, P * (k % 4):P * (k % 4 + 1)],
                                              hs[:, slot, P * k:P * (k + 1)], ident[:, :])
                ins.then_inc(tr2, 1)

            pe.wait_ge(o_evac, 2 * HEADS)
            project_out(0, 0, 0)
            project_out(1, 0, 1)
            with pe.Fori(1, 4) as i:
                project_out(2 * i, 0, 0)
                project_out(2 * i + 1, 0, 1)
            project_out(NB, 1, 0)
            project_out(NB + 1, 1, 1)
            transpose_h(0, 0)
            project_out(NB + 2, 1, 0)
            transpose_h(1, 1)
            with pe.Fori(1, 3) as i:
                project_out(NB + 2 * i + 1, 1, 1)
                transpose_h(2 * i, 0)
                project_out(NB + 2 * i + 2, 1, 0)
                transpose_h(2 * i + 1, 1)
            project_out(2 * NB - 1, 1, 1)
            transpose_h(NB - 2, 0)
            transpose_h(NB - 1, 1)

            def mlp(q):
                for i in range(2 * FT):
                    f, half = i % FT, i // FT
                    if half == 0:
                        pe.wait_ge(mwlo_done, 16 * q + 2 * f + 2)
                    else:
                        pe.wait_ge(relu_done, 8 * q + i - 3)
                    c = slice(HALF * half, HALF * (half + 1))
                    for k in range(KT):
                        w = slice(P * k, P * (k + 1))
                        ins = three(ps[:, f, :], (w1_hi[:, f, w], w1_lo[:, f, w]), (hn2_hi[:, k, c], hn2_lo[:, k, c]),
                                    k == 0, k == KT - 1)
                    ins.then_inc(m1_done, 1)
                for t in range(NB):
                    b = 4 + 2 * (t % 2)
                    if t % 4 == 0:
                        pe.wait_ge(alo_done, 8 * q + t + 4)
                    pe.wait_ge(h_evac, 2 * NB + NB * q + t - 1)
                    for f in range(FT):
                        if t == 0:
                            pe.wait_ge(mwlo_done, 16 * q + 8 + 2 * f + 2)
                        a = (a_hi[:, f, P * t:P * (t + 1)], a_lo[:, f, P * t:P * (t + 1)])
                        for i in range(2):
                            c = slice(HALF * i, HALF * (i + 1))
                            ins = three(ps[:, b + i, :], a, (w2_hi[:, f, c], w2_lo[:, f, c]), f == 0, f == FT - 1)
                    ins.then_inc(out_done, 1)

            pe.wait_ge(h2lo_done, NB)
            with pe.Fori(0, CH - 1) as q:
                mlp(q)
            mlp(CH - 1)


def kernel(x, meta_tokens, mix_norm_g, w_in, b_forget, w_conf_dw, b_conf_dw, conf_ln_g, conf_ln_b, w_conf_pw,
           b_conf_pw, w_sc_conv, w_out, mlp_norm_g, w_mlp1, w_mlp2, final_norm_g):
    import concourse.bacc as bacc
    from concourse.bass_utils import run_bass_kernel_spmd

    def tiles(a):
        a = np.asarray(a)
        return a.reshape(-1, P, *a.shape[1:]).swapaxes(0, 1)

    win = tiles(w_in[0])
    par = np.concatenate([
        tiles(mix_norm_g[0]), tiles(mlp_norm_g[0]), tiles(b_conf_dw[0]),
        tiles(np.asarray(w_conf_dw[0]).T).reshape(P, -1), tiles(conf_ln_g[0]), tiles(conf_ln_b[0]), tiles(b_conf_pw[0]),
        tiles(np.asarray(w_sc_conv[0]).T).reshape(P, -1), np.broadcast_to(np.asarray(b_forget[0]), (P, HEADS))], axis=1)
    row, col = np.arange(P)[:, None], np.arange(P)[None, :]
    hidden = -1e30
    consts = np.stack([np.eye(P), np.where(col > row, hidden, 0.0), np.where(row > col, hidden, 0.0)], 1).astype(np.float32)
    arrays = {
        "x": np.asarray(x)[0], "meta": np.asarray(meta_tokens), "par": par, "consts": consts,
        "w_vf": win[:, :, 2 * D_ATTN:2 * D_ATTN + VF],
        "w_proj": np.stack([win[:, :, FIRST_COL[kind] + P * j:FIRST_COL[kind] + P * (j + 1)].reshape(P, -1)
                            for kind, j in ORDER]),
        "w_pw": tiles(w_conf_pw[0]).reshape(P, -1), "w_out": np.asarray(w_out[0]),
        "w1": np.asarray(w_mlp1[0]).reshape(KT, P, FF // P, P).transpose(2, 1, 0, 3).reshape(FF // P, P, D),
        "w2": np.asarray(w_mlp2[0]).reshape(FF // P, P, D),
        "g_fin": np.broadcast_to(np.asarray(final_norm_g), (P, D)),
    }
    nc = bacc.Bacc("TRN2", target_bir_lowering=False, num_devices=1)
    arrays = {f"in_{n}": np.ascontiguousarray(a) for n, a in arrays.items()}
    ins = [nc.dram_tensor(n, a.shape, mybir.dt.from_np(a.dtype), kind="ExternalInput").ap() for n, a in arrays.items()]
    out = nc.dram_tensor("out", (SEQ, D), F32, kind="ExternalOutput").ap()
    build(nc, *ins, out)
    r = run_bass_kernel_spmd(nc, [arrays], core_ids=[0])
    return r.results[0]["out"].reshape(1, SEQ, D)
```

```python
from contextlib import ExitStack

import numpy as np

import concourse.bass as bass
from concourse import mybir

F32 = mybir.dt.float32
F32R = mybir.dt.float32r
BF16 = mybir.dt.bfloat16
ALU = mybir.AluOpType
ACT = mybir.ActivationFunctionType
AX = mybir.AxisListType

P = 128
D = 1024
SEQ = 1024
META = 16
TOK = SEQ + META
HEADS = 8
HD = 64
D_ATTN = HEADS * HD
D_CONF = 256
CONF_K = 31
SC_K = 3
FF = 4096
EPS = 1e-6
KT = D // P
NB = SEQ // P
VF = D_ATTN + HEADS
HALF = 512
CH = FF // HALF
FT = HALF // P

G1, G2 = 0, 8
B_DW, W_DW = 16, 18
LN_G, LN_B = W_DW + 2 * CONF_K, W_DW + 2 * CONF_K + 2
B_PW = LN_B + 2
W_SC = B_PW + 2
B_F = W_SC + 2 * SC_K
N_PAR = B_F + HEADS

GATE, CONF_A, SC_B, SC_C, SC_U, Q, K = range(7)
ORDER = [(GATE, 0), (CONF_A, 0), (GATE, 1), (CONF_A, 1)] \
    + [(kind, j) for j in range(2) for kind in (SC_C, SC_U, SC_B)] \
    + [(kind, p) for p in range(4) for kind in (Q, K)]
FIRST_COL = {Q: 0, K: D_ATTN, CONF_A: 3 * D_ATTN + HEADS, GATE: 3 * D_ATTN + HEADS + D_CONF,
             SC_B: 3 * D_ATTN + HEADS + 2 * D_CONF, SC_C: 3 * D_ATTN + HEADS + 3 * D_CONF,
             SC_U: 3 * D_ATTN + HEADS + 4 * D_CONF}
N_PROJ = len(ORDER)
N_EARLY = 10

LATE = 12
_first = [(0, k) for k in range(10)]
_turns = [(j, k) for k in range(CONF_K - LATE) for j in (1, 0)]
_turns = [t for t in _turns if t not in _first]
EARLY_TAPS = [[]] * 2 + [_first[0:5], _first[5:10]] + [_turns[5 * i:5 * i + 5] for i in range(5)] + [_turns[25:]]

ALL_TOKENS = [(0, 352), (352, 344), (696, 344)]
REAL_TOKENS = [(META, HALF), (META + HALF, HALF)]

UNITS = [(0, 0), (0, 1), (0, 2), (0, 3), (1, 0), (0, 4)] + [(1, T) for T in range(1, NB + 1)]
NU = len(UNITS)
LAST = (UNITS.index((0, NB // 2)), NU - 1)
RING = 4
N_FILLS = 8
R_FILLS = 6
LAG = 2
MAXES = [(0, 0, 144, 1), (1, 0, 272, 1), (2, 0, 400, 1), (3, 0, 264, 2), (4, 0, 328, 2), (5, 0, 392, 2),
         (6, 0, 456, 2), (7, 0, 348, 2), (7, 696, 344, 1)]
NM = len(MAXES)
MAX_STEPS = {5: (0,), 6: (1, 2), 7: (3, 4), 8: (5, 6), 9: (7, 8)}


def cols_of(T):
    return (0, META) if T == 0 else (META + P * (T - 1), P)


def unit(u):
    c, T = UNITS[u]
    k0, rows = cols_of(T)
    ahead = max(0, T - 1 - 4 * c)
    q0 = HALF * c + P * ahead
    return k0, rows, q0, HALF * (c + 1) - q0, T >= 1 and T - 1 >= 4 * c


def build(nc, x, meta, par, consts, w_vf, w_proj, w_pw, w_out, w1, w2, g_fin, out):
    with ExitStack() as ctx:
        base = 16512
        at = [base]

        def sb(name, shape, dt, offset=None):
            if offset is not None:
                at[0] = offset
            size = 4 if dt != BF16 else 2
            for n in shape[1:]:
                size *= n
            t = nc.alloc_sbuf_tensor_at(name, shape, dt, offset=at[0])
            at[0] += -(-size // 32) * 32
            assert at[0] <= 229344, (name, at[0])
            return t

        def sem(name):
            return ctx.enter_context(nc.semaphore(name))

        R_HN = base
        R_MIX = R_HN + 2 * KT * TOK * 4
        R_H = R_MIX + KT * SEQ * 4
        R_QKV = R_H + KT * SEQ * 4
        R_RING = R_QKV + 2 * 4 * (SEQ + META) * 4 - 4 * META * 4 + (NB + 1) * D_ATTN * 4
        R_C = R_RING + 6 * 4096

        ident = sb("ident", [P, P], F32, R_C)
        identb = sb("identb", [P, P], BF16)
        mask_qk = sb("mask_qk", [P, P], BF16)
        mask_kq = sb("mask_kq", [P, P], BF16)
        prm = sb("prm", [P, N_PAR], F32)
        sumsq = sb("sumsq", [P, 12], F32)
        eps = sb("eps", [P, 1], F32)
        std = sb("std", [P, 12], F32)
        rstd = sb("rstd", [P, 12], F32)
        f_raw = sb("f_raw", [P, NB + 1, HEADS], F32)
        c_q = sb("c_q", [P, HEADS, NB], F32)
        mx = sb("mx", [P, NM], F32)
        m_q = sb("m_q", [P, NB], F32)
        r_q = sb("r_q", [P, NB], F32)
        r_hi = sb("r_hi", [P, NB], F32R)

        hn_hi = sb("hn_hi", [P, KT, TOK], F32R, R_HN)
        hn_lo = sb("hn_lo", [P, KT, TOK], F32R)
        x_in = sb("x_in", [P, NB, D], F32, R_H)
        x_meta = sb("x_meta", [META, D], F32, R_QKV)
        xs = sb("xs", [P, 2, D], F32)
        squares = sb("squares", [P, D], F32)
        wv_hi = sb("wv_hi", [P, KT, VF], F32R, R_QKV + 16384)
        wv_lo = sb("wv_lo", [P, KT, VF], F32R, R_MIX)
        hn32 = sb("hn32", [P, KT, P], F32, R_MIX + 16640)
        hn32b = sb("hn32b", [P, KT, P], F32)
        consts_f = sb("consts_f", [P, 3, P], F32)
        wv_raw = sb("wv_raw", [P, KT, VF], F32, R_RING)
        w_raw = sb("w_raw", [P, 2, D], F32, R_RING)
        w_hi = sb("w_hi", [P, 2, KT, P], F32R)
        w_lo = sb("w_lo", [P, 2, KT, P], F32R)
        q_raw = sb("q_raw", [P, 4, SEQ], F32, R_QKV)
        k_raw = sb("k_raw", [P, 4, TOK], F32)
        v_raw = sb("v_raw", [P, NB + 1, D_ATTN], F32)
        hn32 = [hn32, hn32b]
        lf = [sb(f"lf{i}", [P, NB + 1, HEADS], F32, R_QKV + 16384 + i * 288) for i in range(10)]
        lf_t = sb("lf_t", [HEADS, TOK], F32, R_QKV)
        c_t = sb("c_t", [HEADS, TOK], F32)
        c_neg = sb("c_neg", [HEADS, TOK], F32)
        c_hi = sb("c_hi", [HEADS, TOK], F32R, R_MIX)
        c_lo = sb("c_lo", [HEADS, TOK], F32R)
        PAD = CONF_K - 1 - META
        GLU = -(-(PAD + TOK) * 4 // 32) * 32
        glu = [sb("glu0", [P, PAD + TOK], F32, R_H), sb("glu1", [P, PAD + TOK], F32)]
        sig_gate = sb("sig_gate", [P, TOK], F32)
        sc_c = sb("sc_c", [P, TOK], F32)
        sc_cu = sb("sc_cu", [P, TOK], F32)
        dw = sb("dw", [P, 2, SEQ], F32)
        z = sb("z", [P, 2, SEQ], F32, R_H)
        normed = sb("normed", [P, NB, D_CONF], F32, R_H + 2 * GLU)
        silu = sb("silu", [P, 2, SEQ], F32, R_H + 2 * GLU + 3 * TOK * 4)
        ln_stats = sb("ln_stats", [P, NB, 6], F32)
        ln_mv = sb("ln_mv", [P, NB, 2], F32)
        ln_std = sb("ln_std", [P, NB], F32)
        ln_rstd = sb("ln_rstd", [P, NB], F32)
        s_hi = sb("s_hi", [P, 2, SEQ], F32R, R_MIX)
        s_lo = sb("s_lo", [P, 2, SEQ], F32R)
        mix = sb("mix", [P, KT, SEQ], F32, R_MIX)
        assert PAD >= 0 and R_H + KT * SEQ * 4 == R_QKV

        qm = [sb(f"qm{s}", [P, SEQ], F32R, R_HN if s == 0 else None) for s in range(2)]
        qx = [sb(f"qx{s}", [P, SEQ], F32R) for s in range(2)]
        km = [sb(f"km{s}", [P, TOK], F32R) for s in range(2)]
        kx = [sb(f"kx{s}", [P, TOK], F32R) for s in range(2)]
        v_one = [sb(f"v_one{s}", [P, NB + 1, P], F32) for s in range(2)]
        o_r0 = sb("o_r0", [P, HALF], F32)
        o_t = sb("o_t", [P, HALF], F32)
        o_r1 = sb("o_r1", [P, HALF], F32)
        r_pad = sb("r_pad", [P, NB, HD + 4], F32)
        p32 = sb("p32", [P, RING, HALF], F32, R_RING)

        h = sb("h", [P, NB, D], F32, R_H)
        wo_hi = sb("wo_hi", [P, KT, HALF], F32R, R_QKV)
        wo_lo = sb("wo_lo", [P, KT, HALF], F32R)
        mix_parts = sb("mix_parts", [P, 2, 2, KT, P], F32R)
        assert at[0] <= R_RING
        hs = sb("hs", [P, 2, D], F32, R_RING)
        h32 = sb("h32", [P, KT, P], F32)
        h_squares = sb("h_squares", [P, D], F32)
        wo_raw = [sb("wo_raw0", [P, 4, HALF], F32), sb("wo_raw1", [P, KT, HALF], F32, R_RING)]
        hn2_hi = sb("hn2_hi", [P, KT, SEQ], F32R, R_HN)
        hn2_lo = sb("hn2_lo", [P, KT, SEQ], F32R)

        a_hi = sb("a_hi", [P, FT, SEQ], F32R, R_MIX)
        a_lo = sb("a_lo", [P, FT, SEQ], F32R)
        w1_first = sb("w1_first", [P, 2 * FT, HALF], F32, R_MIX)
        w2_hi = sb("w2_hi", [P, FT, D], F32R, R_QKV)
        w2_lo = sb("w2_lo", [P, FT, D], F32R)
        w1_parts = sb("w1_parts", [P, FT, 2, D], F32R)
        act32 = sb("act32", [P, 2, HALF], F32)
        m_raw = sb("m_raw", [P, 2, HALF], F32)
        assert at[0] <= R_C
        g_row = sb("g_row", [P, D], F32, R_QKV + 2 * FT * D * 4)
        y = sb("y", [P, 2, D], F32)
        y_squares = sb("y_squares", [P, D], F32)

        ps = ctx.enter_context(nc.psum_tensor("ps", [P, 8, HALF], F32))
        c_scratch = nc.dram_tensor("c_scratch", (HEADS, 2, TOK), F32, kind="Internal").ap()

        s_par, s_consts, s_masks, s_g = sem("par_loaded"), sem("ident_loaded"), sem("masks_loaded"), sem("g_final_loaded")
        s_x = [sem(f"x_loaded{T}") for T in range(NB + 1)]
        s_wv = [sem(f"wv_loaded{i}") for i in range(4)]
        s_xr = [sem(f"x_again{i}") for i in range(NB)]
        s_w = [sem(f"w_loaded{i}") for i in range(2)]
        s_wo = [sem(f"wo_loaded{i}") for i in range(4 + KT)]
        s_w1f = [sem(f"w1_first_loaded{i}") for i in range(2 * FT)]
        s_m = [sem(f"mlp_w_loaded{i}") for i in range(2)]
        s_c = [sem(f"c_rows_loaded{i}") for i in range(2)]
        s_cst = sem("c_stored")
        s_out = [sem(f"out_stored{i}") for i in range(2)]
        masks_ready, pool_init, eps_ready = sem("masks_ready"), sem("pool_init"), sem("eps_ready")
        ss_done, std_done, rstd_done, xs_done = (sem(n) for n in ("ss_done", "std_done", "rstd_done", "xs_done"))
        tr_done, hn32_done, hnhi_done, hnlo_done = (sem(n) for n in ("tr_done", "hn32_done", "hnhi_done", "hnlo_done"))
        wvhi_done, wvlo_done, v_done, v_evac = (sem(n) for n in ("wvhi_done", "wvlo_done", "v_done", "v_evac"))
        whi_done, wlo_done, proj_done, proj_evac = (sem(n) for n in ("whi_done", "wlo_done", "proj_done", "proj_evac"))
        lf_act, lf_dve, lft_done, lft_evac, cq_tr, cq_evac = (sem(n) for n in ("lf_act", "lf_dve", "lft_done", "lft_evac", "cq_tr", "cq_evac"))
        sig_done, glu_done, cu_done, conv_step, sc_step, pad_done = (sem(n) for n in ("sig_done", "glu_done", "cu_done", "conv_step0", "sc_step", "pad_done"))
        scc_done = sem("scc_done")
        conv_step = [conv_step, sem("conv_step1")]
        ln_tr, ln_dve, ln_sqrt, ln_norm, ln_back = (sem(n) for n in ("ln_tr", "ln_dve", "ln_sqrt", "ln_norm", "ln_back"))
        z_done, zsig_done, silu_done, shi_done, slo_done = (sem(n) for n in ("z_done", "zsig_done", "silu_done", "shi_done", "slo_done"))
        pw_done, pw_evac = sem("pw_done"), sem("pw_evac")
        att_init, qk_hi, qk_dup, k_dup, qk_lo, qk_lo2, v_ready = (sem(n) for n in ("att_init", "qk_hi", "qk_dup", "k_dup", "qk_lo", "qk_lo2", "v_ready"))
        mx_mm, mx_red, r_step, rt_done, r_ready = (sem(n) for n in ("mx_mm", "mx_red", "r_step", "rt_done", "r_ready"))
        sc_done, exp_done, pv_done = (sem(n) for n in ("sc_done", "exp_done", "pv_done"))
        o_ln, o_inv, o_step, o_evac = (sem(n) for n in ("o_ln", "o_inv", "o_step", "o_evac"))
        wohi_done, wolo_done, wo_used, mixhi_done, mixlo_done = (sem(n) for n in ("wohi_done", "wolo_done", "wo_used", "mixhi_done", "mixlo_done"))
        out_done, h_evac = sem("out_done"), sem("h_evac")
        ss2, std2, rstd2, hs_done = (sem(n) for n in ("ss2_done", "std2_done", "rstd2_done", "hs_done"))
        tr2, h32_done, h2hi_done, h2lo_done = (sem(n) for n in ("tr2_done", "h32_done", "h2hi_done", "h2lo_done"))
        mwhi_done, mwlo_done, m1_done, relu_done, asq_done, ahi_done, alo_done = (
            sem(n) for n in ("mwhi_done", "mwlo_done", "m1_done", "relu_done", "asq_done", "ahi_done", "alo_done"))
        ss3, std3, rstd3, y_done = (sem(n) for n in ("ss3_done", "std3_done", "rstd3_done", "y_done"))

        def x_tile(T):
            return x_meta[:, :] if T == 0 else x_in[:, T - 1, :]

        def banks(n):
            return 3 * (n % 2)

        def wo_buffer(w):
            return (wo_raw[0][:, w % 4, :], w % 4) if w < KT else (wo_raw[1][:, w - KT, :], 4 + w - KT)

        block = ctx.enter_context(nc.Block())

        @block.sync
        def _(sp):
            sp.dma_start(x_meta[:, :], meta).then_inc(s_x[0], 16)
            sp.dma_start(ident[:, :], consts[:, 0, :]).then_inc(s_consts, 16)
            sp.dma_start(prm[:, :], par).then_inc(s_par, 16)
            for i in range(4):
                sp.dma_start(wv_raw[:, 2 * i:2 * i + 2, :], w_vf[:, 2 * i:2 * i + 2, :]).then_inc(s_wv[i], 16)
                if i == 1:
                    sp.dma_start(x_tile(1), x[0:P, :]).then_inc(s_x[1], 16)
            for T in range(2, NB + 1):
                sp.dma_start(x_tile(T), x[P * (T - 1):P * T, :]).then_inc(s_x[T], 16)
                if T == 2:
                    sp.dma_start(consts_f[:, :, :], consts).then_inc(s_masks, 16)

            def load_w(n, slot):
                if isinstance(n, int) and n < 2:
                    sp.wait_ge(wvlo_done, 4)
                else:
                    sp.wait_ge(wlo_done, n - 1)
                sp.dma_start(w_raw[:, slot, :], w_proj[n]).then_inc(s_w[slot], 16)

            for n in range(N_EARLY):
                load_w(n, n % 2)
                if n == 6:
                    sp.wait_ge(lf_dve, 12)
                    sp.dma_start(c_scratch[:, 0, :], c_hi[:, :].bitcast(F32)).then_inc(s_cst, 16)
                    sp.dma_start(c_scratch[:, 1, :], c_lo[:, :].bitcast(F32)).then_inc(s_cst, 16)
            with sp.Fori(0, 4) as p:
                load_w(N_EARLY + 2 * p, 0)
                load_w(N_EARLY + 2 * p + 1, 1)
            sp.wait_ge(wlo_done, N_PROJ - 1)
            sp.dma_start(w_raw[:, 0, 0:2 * D_CONF], w_pw).then_inc(s_w[0], 16)

            def load_c(g, s):
                sp.dma_start(km[s][HD:HD + 2, :].bitcast(F32), c_scratch[g]).then_inc(s_c[s], 16)

            sp.wait_ge(s_cst, 32)
            sp.wait_ge(att_init, 1)
            load_c(0, 0)
            sp.wait_ge(att_init, 3)
            load_c(1, 1)
            sp.wait_ge(slo_done, 2)
            for i in range(NB):
                sp.dma_start(h[:, i, :], x[P * i:P * (i + 1), :]).then_inc(s_xr[i], 16)
            with sp.Fori(0, 3) as p:
                for s in range(2):
                    sp.wait_ge(sc_done, NU * (2 * p + s + 1))
                    load_c(2 * p + s + 2, s)

            for w in range(2 * KT):
                b, k = w // KT, w % KT
                buf, i = wo_buffer(w)
                if 4 <= w < KT:
                    sp.wait_ge(wolo_done, w - 3)
                elif w == KT:
                    sp.wait_ge(pv_done, NU * HEADS)
                sp.dma_start(buf, w_out[P * k:P * (k + 1), HALF * b:HALF * (b + 1)]).then_inc(s_wo[i], 16)

            sp.wait_ge(mixlo_done, 2 * NB)
            for i in range(2 * FT):
                sp.dma_start(w1_first[:, i, :], w1[i // 2, :, HALF * (i % 2):HALF * (i % 2 + 1)]).then_inc(s_w1f[i], 16)

            def load_m(r, slot, src):
                sp.wait_ge(mwlo_done, r - 1)
                sp.dma_start(m_raw[:, slot, :], src).then_inc(s_m[slot], 16)

            def load_w1(q):
                for i in range(2 * FT):
                    load_m(16 * q + i, i % 2, w1[FT * q + i // 2, :, HALF * (i % 2):HALF * (i % 2 + 1)])

            def load_w2(q):
                for i in range(2 * FT):
                    load_m(16 * q + 8 + i, i % 2, w2[FT * q + i // 2, :, HALF * (i % 2):HALF * (i % 2 + 1)])

            with sp.Fori(0, CH - 1) as q:
                load_w2(q)
                load_w1(q + 1)
            load_w2(CH - 1)
            sp.wait_ge(m1_done, 2 * FT * CH)
            sp.dma_start(g_row[:, :], g_fin).then_inc(s_g, 16)
            for t in range(NB):
                sp.wait_ge(y_done, t + 1)
                sp.dma_start(out[P * t:P * (t + 1), :], y[:, t % 2, :]).then_inc(s_out[t % 2], 16)
            for i in range(2):
                sp.wait_ge(s_out[i], 16 * NB // 2)

        @block.gpsimd
        def _(pool):
            nc.gpsimd.memset(f_raw[:, :, :], 0.0).then_inc(pool_init, 1)
            pool.wait_ge(pool_init, 1)
            pool.wait_ge(wvlo_done, 4)
            nc.gpsimd.memset(v_raw[:, 0, :], 0.0).then_inc(pool_init, 1)
            pool.wait_ge(proj_done, N_PROJ)
            def fill(i, dst, value):
                if i:
                    pool.wait_ge(att_init, i)
                nc.gpsimd.memset(dst, value).then_inc(att_init, 1)

            fills = [(km[0][HD:HD + 4, :], 1.0), (qm[0][HD:HD + 4, :], 1.0), (km[1][HD:HD + 4, :], 1.0), (qm[1][HD:HD + 4, :], 1.0),
                     (r_pad[:, :, :], 0.0), (r_pad[:, :, HD:HD + 2], 1.0),
                     (v_one[0][:, :, HD:P], 1.0), (v_one[1][:, :, 0:HD], 1.0)]
            assert len(fills) == N_FILLS
            for i, (dst, value) in enumerate(fills):
                fill(i, dst.bitcast(F32), value)

            def prep(g, p, s):
                rows, cols = slice(HD * s, HD * (s + 1)), slice(HD * s, HD * (s + 1))
                if not isinstance(g, int) or g >= 2:
                    pool.wait_ge(pv_done, NU * (g - 1))
                if not isinstance(g, int) or g >= 1:
                    pool.wait_ge(qk_lo2, g)
                nc.gpsimd.tensor_copy(v_one[s][:, :, cols], v_raw[:, :, bass.ds(p * P + s * HD, HD)]).then_inc(v_ready, 1)
                pool.wait_ge(qk_hi, g + 1)
                pool.wait_ge(k_dup, g + 1)
                pool.wait_ge(v_ready, g + 1)
                raw = (q_raw, k_raw)[s][rows, bass.ds(p, 1), :].rearrange("p a c -> p (a c)")
                hi = qm[0][0:HD, :] if s == 0 else kx[1][HD:P, :]
                lo = qx[0][0:HD, :] if s == 0 else kx[1][HD:P, :]
                nc.gpsimd.tensor_tensor(lo, raw, hi.bitcast(F32), ALU.subtract).then_inc(qk_lo2, 1)

            pool.wait_ge(att_init, N_FILLS)
            pool.wait_ge(proj_evac, N_PROJ - N_EARLY)
            prep(0, 0, 0)
            prep(1, 0, 1)
            with pool.Fori(1, 4) as p:
                prep(2 * p, p, 0)
                prep(2 * p + 1, p, 1)

        @block.scalar
        def _(act):
            def square(T):
                rows = cols_of(T)[1]
                act.wait_ge(s_x[T], 16)
                if T:
                    act.wait_ge(ss_done, T)
                nc.scalar.activation(squares[0:rows, :], x_tile(T), ACT.Square,
                                     accum_out=sumsq[0:rows, T:T + 1]).then_inc(ss_done, 1)

            def root(T):
                rows = cols_of(T)[1]
                act.wait_ge(ss_done, T + 1)
                nc.scalar.activation(std[0:rows, T:T + 1], sumsq[0:rows, T:T + 1], ACT.Sqrt, scale=1.0 / D,
                                     bias=eps[0:rows, :]).then_inc(std_done, 1)

            def evac_v(T):
                rows = cols_of(T)[1]
                b = 4 + 2 * (T % 2)
                if T == 0:
                    act.wait_ge(pool_init, 2)
                act.wait_ge(v_done, T + 1)
                nc.scalar.activation(v_raw[0:rows, T, 0:VF // 2], ps[0:rows, b, 0:VF // 2], ACT.Copy)
                nc.scalar.activation(v_raw[0:rows, T, VF // 2:D_ATTN], ps[0:rows, b + 1, 0:D_ATTN - VF // 2], ACT.Copy)
                nc.scalar.activation(f_raw[0:rows, T, :], ps[0:rows, b + 1, D_ATTN - VF // 2:VF // 2],
                                     ACT.Copy).then_inc(v_evac, 1)

            def split_wv(i):
                act.wait_ge(s_wv[i], 16)
                nc.scalar.activation(wv_hi[:, 2 * i:2 * i + 2, :], wv_raw[:, 2 * i:2 * i + 2, :], ACT.Copy).then_inc(wvhi_done, 1)

            def split_hn(T):
                k0, rows = cols_of(T)
                act.wait_ge(hn32_done, T + 1)
                nc.scalar.activation(hn_hi[:, :, k0:k0 + rows], hn32[T % 2][:, :, 0:rows], ACT.Copy).then_inc(hnhi_done, 1)

            nc.scalar.preload_act_table_set("sqrt_and_others")
            act.wait_ge(eps_ready, 1)
            square(0)
            root(0)
            split_wv(0)
            split_hn(0)
            split_wv(1)
            square(1)
            root(1)
            split_wv(2)
            split_wv(3)
            for T in range(1, NB + 1):
                if T < NB:
                    square(T + 1)
                    root(T + 1)
                split_hn(T)
                if T >= 2:
                    evac_v(T - 2)

            def split_hi(n, slot, size=D):
                act.wait_ge(s_w[slot], 16 * (n // 2 + 1) if isinstance(n, int) else n * 8 + 16 - 8 * slot)
                act.wait_ge(proj_done, n - 1) if not isinstance(n, int) or n >= 2 else None
                dst = w_hi[:, slot, :, :].rearrange("p k c -> p (k c)")
                nc.scalar.activation(dst[:, 0:size], w_raw[:, slot, 0:size], ACT.Copy).then_inc(whi_done, 1)

            split_hi(0, 0)
            evac_v(NB - 1)
            split_hi(1, 1)
            evac_v(NB)

            nc.scalar.preload_act_table_set("natural_log_exp_and_others")
            act.wait_ge(lf_dve, 1)
            nc.scalar.activation(lf[1][:, :, :], lf[0][:, :, :], ACT.Abs).then_inc(lf_act, 1)
            act.wait_ge(lf_act, 1)
            nc.scalar.activation(lf[2][:, :, :], lf[1][:, :, :], ACT.Exp, scale=-1.0).then_inc(lf_act, 1)
            act.wait_ge(lf_dve, 2)
            nc.scalar.activation(lf[4][:, :, :], lf[3][:, :, :], ACT.Ln).then_inc(lf_act, 1)

            def from_banks(n, dst, func):
                b = banks(n)
                act.wait_ge(proj_done, n + 1)
                c0 = ALL_TOKENS[0][1]
                nc.scalar.activation(dst[:, 0:c0], ps[:, b, 0:c0], func)
                return nc.scalar.activation(dst[:, c0:TOK].rearrange("p (b c) -> p b c", b=2),
                                            ps[:, b + 1:b + 3, 0:ALL_TOKENS[1][1]], func)

            for n in range(N_EARLY):
                kind, j = ORDER[n]
                if kind == GATE:
                    act.wait_ge(xs_done, NB + 1)
                    if j:
                        act.wait_ge(glu_done, j)
                    from_banks(n, sig_gate, ACT.Sigmoid).then_inc(sig_done, 1)
                elif kind == SC_C:
                    if j:
                        act.wait_ge(cu_done, j)
                    from_banks(n, sc_c, ACT.Copy).then_inc(scc_done, 1)
                split_hi(n + 2, n % 2)

            def evac_q(n, p):
                act.wait_ge(proj_done, n + 1)
                act.wait_ge(s_cst, 32)
                act.wait_ge(cq_evac, 1)
                nc.scalar.activation(q_raw[:, bass.ds(p, 1), :].rearrange("p a (b c) -> p (a b) c", b=2), ps[:, 0:2, :], ACT.Copy,
                                     scale=float(HD) ** -0.5).then_inc(proj_evac, 1)

            def evac_k(n, p):
                act.wait_ge(proj_done, n + 1)
                c0 = ALL_TOKENS[0][1]
                dst = k_raw[:, bass.ds(p, 1), :].rearrange("p a c -> p (a c)")
                nc.scalar.activation(dst[:, 0:c0], ps[:, 3, 0:c0], ACT.Copy)
                nc.scalar.activation(dst[:, c0:TOK].rearrange("p (b c) -> p b c", b=2),
                                     ps[:, 4:6, 0:ALL_TOKENS[1][1]], ACT.Copy).then_inc(proj_evac, 1)

            with act.Fori(0, 2) as p:
                n = N_EARLY + 2 * p
                evac_q(n, p)
                split_hi(n + 2, 0)
                evac_k(n + 1, p)
                split_hi(n + 3, 1)

            def ln_root(r):
                act.wait_ge(ln_dve, 3 * r + 2)
                nc.scalar.activation(ln_std[:, 4 * r:4 * r + 4], ln_rstd[:, 4 * r:4 * r + 4], ACT.Sqrt).then_inc(ln_sqrt, 1)

            def swish_sigmoid(j):
                act.wait_ge(ln_back, j + 1)
                nc.scalar.activation(z[:, j, :].rearrange("p (b c) -> p b c", b=2), ps[:, 6:8, :], ACT.Identity, scale=prm[:, LN_G + j:LN_G + j + 1],
                                     bias=prm[:, LN_B + j:LN_B + j + 1]).then_inc(z_done, 1)
                act.wait_ge(z_done, j + 1)
                nc.scalar.activation(silu[:, j, :], z[:, j, :], ACT.Sigmoid).then_inc(zsig_done, 1)

            def swish_hi(j):
                act.wait_ge(silu_done, j + 1)
                nc.scalar.activation(s_hi[:, j, :], silu[:, j, :], ACT.Copy).then_inc(shi_done, 1)

            evac_q(N_PROJ - 4, 2)
            split_hi(N_PROJ - 2, 0)
            ln_root(0)
            evac_k(N_PROJ - 3, 2)
            split_hi(N_PROJ - 1, 1)
            ln_root(1)
            evac_q(N_PROJ - 2, 3)
            split_hi(N_PROJ, 0, 2 * D_CONF)
            for j in range(2):
                swish_sigmoid(j)
                swish_hi(j)
            evac_k(N_PROJ - 1, 3)

            def prep(g, p, s, step):
                rows = slice(HD * s, HD * (s + 1))
                k = k_raw[rows, bass.ds(p, 1), :].rearrange("p a c -> p (a c)")
                if step == 0:
                    if not isinstance(g, int) or g >= 2:
                        act.wait_ge(sc_done, NU * (g - 1))
                    nc.scalar.activation(qm[s][0:HD, :], q_raw[rows, bass.ds(p, 1), :].rearrange("p a c -> p (a c)"), ACT.Copy)
                else:
                    nc.scalar.activation(km[s][0:HD, :], k, ACT.Copy).then_inc(qk_hi, 1)

            def r_rows(g, s):
                act.wait_ge(rt_done, g + 1)
                nc.scalar.activation(qm[s][HD:HD + 4, :].rearrange("p (b c) -> p b c", b=2), ps[HD:HD + 4, 2:4, :], ACT.Copy).then_inc(r_ready, 1)

            def invert(g, s, c):
                C = 2 * g + c
                last = NU * g + LAST[c] + 1
                sums = slice(HD, P) if s == 0 else slice(0, HD)
                act.wait_ge(pv_done, last)
                if not isinstance(g, int) or C > 0:
                    act.wait_ge(o_evac, C)
                nc.scalar.activation(o_r0[sums, :], ps[sums, 6 + c, :], ACT.Ln).then_inc(o_ln, 1)
                act.wait_ge(o_ln, C + 1)
                nc.scalar.activation(o_r0[sums, :], o_r0[sums, :], ACT.Exp, scale=-1.0).then_inc(o_inv, 1)

            def wo_split(w):
                buf, i = wo_buffer(w)
                act.wait_ge(s_wo[i], 16 * (w // 4 + 1) if w < KT else 16)
                if w == 0:
                    act.wait_ge(v_ready, HEADS)
                    act.wait_ge(qk_hi, HEADS)
                    act.wait_ge(qk_lo, HEADS)
                    act.wait_ge(qk_lo2, HEADS)
                elif w >= KT:
                    act.wait_ge(wo_used, (KT - 1) * (NB - 1) + w - KT + 1) if w < 2 * KT - 1 else act.wait_ge(out_done, NB)
                nc.scalar.activation(wo_hi[:, w % KT, :], buf, ACT.Copy).then_inc(wohi_done, 1)

            def mix_split(v, t, slot):
                if not isinstance(v, int) or v >= 2:
                    act.wait_ge(out_done, v - 1)
                if isinstance(v, int) and v == 0:
                    act.wait_ge(o_evac, 2 * HEADS - 1)
                elif isinstance(v, int) and v == 2:
                    act.wait_ge(o_evac, 2 * HEADS)
                nc.scalar.activation(mix_parts[:, slot, 0, :, :], mix[:, :, bass.ds(t * P, P)], ACT.Copy).then_inc(mixhi_done, 1)

            def head(g, s, nxt):
                for u in range(NU):
                    U, b = NU * g + u, (NU * s + u) % RING
                    _, rows, _, n, _ = unit(u)
                    act.wait_ge(sc_done, U + 1)
                    if not isinstance(U, int) or U >= RING:
                        act.wait_ge(pv_done, U - RING + 1)
                    nc.scalar.activation(p32[0:rows, b, 0:n], ps[0:rows, (NU * s + u) % 2, 0:n], ACT.Exp).then_inc(exp_done, 1)
                    if nxt is not None:
                        if u in (0, 3):
                            prep(*nxt, u // 3)
                        if u == 12:
                            r_rows(nxt[0], nxt[2])
                    if u == LAG and not (isinstance(g, int) and g == 0):
                        invert(g - 1, 1 - s, 1)
                    if u == LAST[0] + LAG + 1:
                        invert(g, s, 0)
                    if nxt is None:
                        if u < KT:
                            wo_split(u)
                        elif u in (11, 12):
                            mix_split(u - 11, u - 11, u - 11)

            act.wait_ge(proj_evac, N_PROJ - N_EARLY)
            act.wait_ge(proj_done, N_PROJ)
            prep(0, 0, 0, 0)
            prep(0, 0, 0, 1)
            nc.scalar.preload_act_table_set("natural_log_exp_and_others")
            for o in range(2):
                act.wait_ge(pw_done, o + 1)
                b = 6 - 6 * o
                nc.scalar.activation(mix[:, 4 + o, :].rearrange("p (b c) -> p b c", b=2), ps[:, b:b + 2, :], ACT.Identity,
                                     bias=prm[:, B_PW + o:B_PW + o + 1]).then_inc(pw_evac, 1)
            act.wait_ge(att_init, 4)
            r_rows(0, 0)
            head(0, 0, (1, 0, 1))
            head(1, 1, (2, 1, 0))
            with act.Fori(1, 3) as p:
                head(2 * p, 0, (2 * p + 1, p, 1))
                head(2 * p + 1, 1, (2 * p + 2, p + 1, 0))
            head(6, 0, (7, 3, 1))
            head(7, 1, None)
            invert(7, 1, 1)

            def h_square(t):
                act.wait_ge(h_evac, NB + t + 1)
                if not isinstance(t, int) or t >= 1:
                    act.wait_ge(ss2, t)
                nc.scalar.activation(h_squares[:, :], h[:, bass.ds(t, 1), :].rearrange("p a c -> p (a c)"), ACT.Square,
                                     accum_out=sumsq[:, bass.ds(t, 1)]).then_inc(ss2, 1)
                act.wait_ge(ss2, t + 1)
                nc.scalar.activation(std[:, bass.ds(t, 1)], sumsq[:, bass.ds(t, 1)], ACT.Sqrt, scale=1.0 / D,
                                     bias=eps[:, :]).then_inc(std2, 1)

            def h_high(t):
                act.wait_ge(h32_done, t + 1)
                nc.scalar.activation(hn2_hi[:, :, bass.ds(t * P, P)], h32[:, :, :], ACT.Copy).then_inc(h2hi_done, 1)

            mix_split(2, 2, 0)
            mix_split(3, 3, 1)
            with act.Fori(1, 3) as i:
                mix_split(2 * i + 2, 2 * i + 2, 0)
                mix_split(2 * i + 3, 2 * i + 3, 1)
            mix_split(NB, 0, 0)
            for w in range(KT, 2 * KT):
                wo_split(w)
            mix_split(NB + 1, 1, 1)
            act.wait_ge(wolo_done, 2 * KT)

            def normalize(t, slot):
                if not isinstance(t, int) or t < NB - 2:
                    mix_split(NB + t + 2, t + 2, slot)
                h_square(t)
                if not isinstance(t, int) or t >= 1:
                    h_high(t - 1)

            normalize(0, 0)
            normalize(1, 1)
            with act.Fori(1, 3) as i:
                normalize(2 * i, 0)
                normalize(2 * i + 1, 1)
            normalize(NB - 2, 0)

            def mw_split(r, dst, slot):
                act.wait_ge(s_m[slot], 8 * (r - 8) + 16 - 8 * slot)
                nc.scalar.activation(dst, m_raw[:, slot, :], ACT.Copy).then_inc(mwhi_done, 1)

            def w1_split(q, i):
                mw_split(16 * q + i, w1_parts[:, i // 2, 0, HALF * (i % 2):HALF * (i % 2 + 1)], i % 2)

            def w2_split(q, i):
                if i == 0:
                    act.wait_ge(out_done, 2 * NB + NB * q)
                mw_split(16 * q + 8 + i, w2_hi[:, i // 2, HALF * (i % 2):HALF * (i % 2 + 1)], i % 2)

            def hidden(q, i):
                G = 8 * q + i
                act.wait_ge(m1_done, G + 1)
                if i >= 2:
                    act.wait_ge(alo_done, G - 1)
                nc.scalar.activation(act32[:, i % 2, :], ps[:, i % 4, :], ACT.Relu).then_inc(relu_done, 1)
                w2_split(q, i)
                act.wait_ge(asq_done, G + 1)
                nc.scalar.activation(a_hi[:, i % 4, HALF * (i // 4):HALF * (i // 4 + 1)], act32[:, i % 2, :],
                                     ACT.Copy).then_inc(ahi_done, 1)

            def w1_first_split(i):
                act.wait_ge(s_w1f[i], 16)
                if i == 0:
                    act.wait_ge(out_done, 2 * NB - 1)
                elif i == 2:
                    act.wait_ge(out_done, 2 * NB)
                elif i == 4:
                    act.wait_ge(tr2, NB)
                    act.wait_ge(h2lo_done, NB)
                    act.wait_ge(ss2, NB)
                nc.scalar.activation(w1_parts[:, i // 2, 0, HALF * (i % 2):HALF * (i % 2 + 1)], w1_first[:, i, :],
                                     ACT.Copy).then_inc(mwhi_done, 1)

            w1_first_split(0)
            w1_first_split(1)
            h_square(NB - 1)
            h_high(NB - 2)
            w1_first_split(2)
            w1_first_split(3)
            h_high(NB - 1)
            for i in range(4, 8):
                w1_first_split(i)
            act.wait_ge(mwlo_done, 8)
            with act.Fori(0, CH - 1) as q:
                for i in range(8):
                    hidden(q, i)
                for i in range(8):
                    if i == 0:
                        act.wait_ge(m1_done, 8 * q + 8)
                    w1_split(q + 1, i)
            for i in range(8):
                hidden(CH - 1, i)
            for t in range(NB):
                act.wait_ge(h_evac, 2 * NB + NB * (CH - 1) + t + 1)
                if t:
                    act.wait_ge(ss3, t)
                nc.scalar.activation(y_squares[:, :], h[:, t, :], ACT.Square, accum_out=sumsq[:, t:t + 1]).then_inc(ss3, 1)
                act.wait_ge(ss3, t + 1)
                nc.scalar.activation(std[:, t:t + 1], sumsq[:, t:t + 1], ACT.Sqrt, scale=1.0 / D, bias=eps[:, :]).then_inc(std3, 1)

        @block.vector
        def _(dve):
            def g_of(first, n):
                return prm[:, first:first + KT].unsqueeze(2).broadcast_to([P, KT, n])

            def scale_x(T):
                rows = cols_of(T)[1]
                dve.wait_ge(std_done, T + 1)
                nc.vector.reciprocal(rstd[0:rows, T:T + 1], std[0:rows, T:T + 1]).then_inc(rstd_done, 1)
                dve.wait_ge(rstd_done, T + 1)
                if T >= 2:
                    dve.wait_ge(tr_done, T - 1)
                nc.vector.tensor_scalar(xs[0:rows, T % 2, :], x_tile(T), rstd[0:rows, T:T + 1], None,
                                        ALU.mult).then_inc(xs_done, 1)

            def gain(T):
                rows = cols_of(T)[1]
                if T == 0:
                    dve.wait_ge(s_par, 16)
                dve.wait_ge(tr_done, T + 1)
                if T >= 2:
                    dve.wait_ge(hnlo_done, T - 1)
                b = 2 * (T % 2)
                nc.vector.tensor_tensor(hn32[T % 2][:, :, 0:rows],
                                        ps[:, b:b + 2, :].rearrange("p b (k c) -> p (b k) c", c=P)[:, :, 0:rows],
                                        g_of(G1, rows), ALU.mult).then_inc(hn32_done, 1)

            def split_hn(T):
                k0, rows = cols_of(T)
                dve.wait_ge(hnhi_done, T + 1)
                nc.vector.tensor_tensor(hn_lo[:, :, k0:k0 + rows], hn32[T % 2][:, :, 0:rows],
                                        hn_hi[:, :, k0:k0 + rows].bitcast(F32), ALU.subtract).then_inc(hnlo_done, 1)

            def split_wv(i):
                dve.wait_ge(wvhi_done, i + 1)
                nc.vector.tensor_tensor(wv_lo[:, 2 * i:2 * i + 2, :], wv_raw[:, 2 * i:2 * i + 2, :],
                                        wv_hi[:, 2 * i:2 * i + 2, :].bitcast(F32), ALU.subtract).then_inc(wvlo_done, 1)

            nc.vector.memset(eps[:, :], EPS).then_inc(eps_ready, 1)
            scale_x(0)
            split_wv(0)
            gain(0)
            split_hn(0)
            split_wv(1)
            scale_x(1)
            split_wv(2)
            split_wv(3)
            for T in range(1, NB + 1):
                if T < NB:
                    scale_x(T + 1)
                gain(T)
                split_hn(T)
                if T == 3:
                    dve.wait_ge(s_masks, 16)
                    nc.vector.tensor_copy(identb[:, :], consts_f[:, 0, :])
                    nc.vector.tensor_copy(mask_qk[:, :], consts_f[:, 1, :])
                    nc.vector.tensor_copy(mask_kq[:, :], consts_f[:, 2, :]).then_inc(masks_ready, 1)

            def split_lo(n, slot, size=D):
                dve.wait_ge(whi_done, n + 1)
                hi = w_hi[:, slot, :, :].rearrange("p k c -> p (k c)").bitcast(F32)
                lo = w_lo[:, slot, :, :].rearrange("p k c -> p (k c)")
                nc.vector.tensor_tensor(lo[:, 0:size], w_raw[:, slot, 0:size], hi[:, 0:size], ALU.subtract).then_inc(wlo_done, 1)

            split_lo(0, 0)
            split_lo(1, 1)
            dve.wait_ge(xs_done, NB + 1)
            nc.vector.memset(glu[0][:, 0:PAD], 0.0)
            nc.vector.memset(glu[1][:, 0:PAD], 0.0).then_inc(pad_done, 1)
            dve.wait_ge(v_evac, NB + 1)
            step = [0]

            def chain(ins):
                ins.then_inc(lf_dve, 1)
                step[0] += 1

            chain(nc.vector.tensor_tensor(lf[0][:, :, :], f_raw[:, :, :],
                                          prm[:, B_F:B_F + HEADS].unsqueeze(1).broadcast_to([P, NB + 1, HEADS]), ALU.add))
            dve.wait_ge(lf_act, 2)
            chain(nc.vector.tensor_scalar(lf[3][:, :, :], lf[2][:, :, :], 1.0, None, ALU.add))
            dve.wait_ge(lf_dve, 2)
            chain(nc.vector.tensor_scalar(lf[5][:, :, :], lf[3][:, :, :], 1.0, None, ALU.subtract))
            dve.wait_ge(lf_dve, 3)
            chain(nc.vector.tensor_tensor(lf[6][:, :, :], lf[2][:, :, :], lf[5][:, :, :], ALU.subtract))
            chain(nc.vector.reciprocal(lf[7][:, :, :], lf[3][:, :, :]))
            dve.wait_ge(lf_dve, 5)
            chain(nc.vector.tensor_tensor(lf[8][:, :, :], lf[6][:, :, :], lf[7][:, :, :], ALU.mult))
            dve.wait_ge(lf_dve, 6)
            dve.wait_ge(lf_act, 3)
            chain(nc.vector.tensor_tensor(lf[9][:, :, :], lf[8][:, :, :], lf[4][:, :, :], ALU.add))
            dve.wait_ge(lf_dve, 7)
            chain(nc.vector.scalar_tensor_tensor(lf[6][:, :, :].rearrange("p t h -> p (t h)"),
                                                 lf[0][:, :, :].rearrange("p t h -> p (t h)"), 0.0,
                                                 lf[9][:, :, :].rearrange("p t h -> p (t h)"), ALU.min, ALU.subtract))

            def projected(n, dst, other):
                b = banks(n)
                dve.wait_ge(proj_done, n + 1)
                c0 = ALL_TOKENS[0][1]
                two = "p (b c) -> p b c"
                nc.vector.tensor_tensor(dst[:, 0:c0], ps[:, b, 0:c0], other[:, 0:c0], ALU.mult)
                return nc.vector.tensor_tensor(dst[:, c0:TOK].rearrange(two, b=2), ps[:, b + 1:b + 3, 0:ALL_TOKENS[1][1]],
                                               other[:, c0:TOK].rearrange(two, b=2), ALU.mult)

            def conv_tap(j, k):
                if isinstance(k, int) and k == 0:
                    nc.vector.tensor_scalar(dw[:, j, :], glu[j][:, 0:SEQ], prm[:, W_DW + CONF_K * j:W_DW + CONF_K * j + 1],
                                            prm[:, B_DW + j:B_DW + j + 1], ALU.mult, ALU.add).then_inc(conv_step[j], 1)
                else:
                    dve.wait_ge(conv_step[j], k)
                    nc.vector.scalar_tensor_tensor(dw[:, j, :], glu[j][:, bass.ds(k, SEQ)], prm[:, bass.ds(W_DW + CONF_K * j + k, 1)],
                                                   dw[:, j, :], ALU.mult, ALU.add).then_inc(conv_step[j], 1)

            for n in range(N_EARLY):
                kind, j = ORDER[n]
                if kind == CONF_A:
                    dve.wait_ge(pad_done, 1)
                    dve.wait_ge(sig_done, j + 1)
                    projected(n, glu[j][:, PAD:PAD + TOK], sig_gate).then_inc(glu_done, 1)
                elif kind == SC_U:
                    dve.wait_ge(scc_done, j + 1)
                    if j:
                        dve.wait_ge(sc_step, 4)
                    projected(n, sc_cu, sc_c).then_inc(cu_done, 1)
                    dve.wait_ge(cu_done, j + 1)
                    for k in range(SC_K):
                        w = prm[:, W_SC + SC_K * j + k:W_SC + SC_K * j + k + 1]
                        src = sc_cu[:, META - SC_K + 1 + k:META - SC_K + 1 + k + SEQ]
                        if k == 0:
                            nc.vector.tensor_scalar(mix[:, 6 + j, :], src, w, None, ALU.mult).then_inc(sc_step, 1)
                        else:
                            dve.wait_ge(sc_step, 4 * j + k)
                            nc.vector.scalar_tensor_tensor(mix[:, 6 + j, :], src, w, mix[:, 6 + j, :],
                                                           ALU.mult, ALU.add).then_inc(sc_step, 1)
                elif kind == SC_B:
                    dve.wait_ge(sc_step, 4 * j + SC_K)
                    dve.wait_ge(proj_done, n + 1)
                    b = banks(n)
                    view = mix[:, 6 + j, :].rearrange("p (b c) -> p b c", b=2)
                    nc.vector.tensor_tensor(view, ps[:, b:b + 2, :], view, ALU.mult).then_inc(sc_step, 1)
                split_lo(n + 2, n % 2)
                if n == 1:
                    dve.wait_ge(lft_done, 1)
                    nc.vector.tensor_copy(lf_t[:, 0:400], ps[0:HEADS, 6, 0:400])
                    nc.vector.tensor_copy(lf_t[:, 400:912], ps[0:HEADS, 7, :]).then_inc(lft_evac, 1)
                if n == 2:
                    dve.wait_ge(lft_done, 2)
                    nc.vector.tensor_copy(lf_t[:, 912:TOK], ps[0:HEADS, 6, 0:P]).then_inc(lft_evac, 1)
                    dve.wait_ge(lft_evac, 2)
                    chain(nc.vector.tensor_tensor_scan(c_t[:, :], lf_t[:, :], lf_t[:, :], 0.0, ALU.add, ALU.bypass))
                    dve.wait_ge(lf_dve, 9)
                    chain(nc.vector.tensor_scalar(c_neg[:, :], c_t[:, :], -1.0, None, ALU.mult))
                    dve.wait_ge(lf_dve, 10)
                    dve.wait_ge(v_done, NB + 1)
                    chain(nc.vector.tensor_copy(c_hi[:, :], c_neg[:, :]))
                    dve.wait_ge(lf_dve, 11)
                    chain(nc.vector.tensor_tensor(c_lo[:, :], c_neg[:, :], c_hi[:, :].bitcast(F32), ALU.subtract))
                if n == 4:
                    dve.wait_ge(cq_tr, 1)
                    nc.vector.tensor_copy(c_q[:, :, :].rearrange("p h t -> p t h"),
                                          ps[:, 6, 0:NB * HEADS].rearrange("p (t h) -> p t h", h=HEADS)).then_inc(cq_evac, 1)
                if n == 2:
                    dve.wait_ge(glu_done, 1)
                if n == 4:
                    dve.wait_ge(glu_done, 2)
                for j_, k in EARLY_TAPS[n]:
                    conv_tap(j_, k)
            with dve.Fori(0, 2) as p:
                for i in range(2):
                    split_lo(N_EARLY + 2 * p + 2 + i, i)
                    for k in range(LATE // 4):
                        for j in range(2):
                            conv_tap(j, CONF_K - LATE + LATE // 2 * p + LATE // 4 * i + k)

            def ln_statistics(r):
                dve.wait_ge(ln_tr, r + 1)
                view = ps[:, 6:8, :].rearrange("p b (t c) -> p (b t) c", c=D_CONF)
                for i in range(4):
                    ins = nc.vector.bn_stats(ln_stats[:, 4 * r + i, :], view[:, i, :])
                ins.then_inc(ln_dve, 1)
                dve.wait_ge(ln_dve, 3 * r + 1)
                for i in range(4):
                    nc.vector.bn_aggr(ln_mv[:, 4 * r + i, :], ln_stats[:, 4 * r + i, :]).then_inc(ln_norm, 1)
                dve.wait_ge(ln_norm, 8 * r + 4)
                nc.vector.tensor_scalar(ln_rstd[:, 4 * r:4 * r + 4], ln_mv[:, 4 * r:4 * r + 4, 1], EPS, None,
                                        ALU.add).then_inc(ln_dve, 1)
                dve.wait_ge(ln_sqrt, r + 1)
                nc.vector.reciprocal(ln_rstd[:, 4 * r:4 * r + 4], ln_std[:, 4 * r:4 * r + 4]).then_inc(ln_dve, 1)
                dve.wait_ge(ln_dve, 3 * r + 3)
                for i in range(4):
                    t = 4 * r + i
                    nc.vector.tensor_scalar(normed[:, t, :], view[:, i, :], ln_mv[:, t, 0:1], ln_rstd[:, t:t + 1],
                                            ALU.subtract, ALU.mult).then_inc(ln_norm, 1)

            def swish(j):
                dve.wait_ge(zsig_done, j + 1)
                nc.vector.tensor_tensor(silu[:, j, :], z[:, j, :], silu[:, j, :], ALU.mult).then_inc(silu_done, 1)
                dve.wait_ge(shi_done, j + 1)
                nc.vector.tensor_tensor(s_lo[:, j, :], silu[:, j, :], s_hi[:, j, :].bitcast(F32), ALU.subtract).then_inc(slo_done, 1)

            for j in range(2):
                dve.wait_ge(conv_step[j], CONF_K)
            split_lo(N_PROJ - 2, 0)
            ln_statistics(0)
            split_lo(N_PROJ - 1, 1)
            ln_statistics(1)
            split_lo(N_PROJ, 0, 2 * D_CONF)
            swish(0)
            swish(1)

            def prep(g, p, s, step):
                rows = slice(HD * s, HD * (s + 1))
                q = q_raw[rows, bass.ds(p, 1), :].rearrange("p a c -> p (a c)")
                k = k_raw[rows, bass.ds(p, 1), :].rearrange("p a c -> p (a c)")
                if step == 0:
                    if not isinstance(g, int) or g >= 2:
                        dve.wait_ge(sc_done, NU * (g - 1))
                    nc.vector.tensor_copy(qx[s][HD:P, :], q).then_inc(qk_dup, 1)
                elif step == 1:
                    ins = nc.vector.tensor_copy(kx[s][0:HD, :], k)
                    if s == 1:
                        ins = nc.vector.tensor_copy(kx[s][HD:P, :], k)
                    ins.then_inc(k_dup, 1)
                elif s == 0:
                    dve.wait_ge(qk_hi, g + 1)
                    nc.vector.tensor_tensor(kx[s][HD:P, :], k, km[s][0:HD, :].bitcast(F32), ALU.subtract).then_inc(qk_lo, 1)
                else:
                    dve.wait_ge(qk_dup, g + 1)
                    nc.vector.tensor_tensor(qx[s][0:HD, :], q, qx[s][HD:P, :].bitcast(F32), ALU.subtract).then_inc(qk_lo, 1)

            def row_max(g, s, m):
                _, _, w, parts = MAXES[m]
                G, b = NM * g + m, 2 + 2 * ((NM * s + m) % 2)
                dve.wait_ge(mx_mm, G + 1)
                nc.vector.tensor_reduce(mx[:, m:m + 1], ps[:, b:b + parts, 0:w], AX.XY if parts > 1 else AX.X,
                                        ALU.max).then_inc(mx_red, 1)

            def shift(g, hd):
                def nxt(ins, i):
                    ins.then_inc(r_step, 1)
                    dve.wait_ge(r_step, 6 * g + i + 1)

                dve.wait_ge(mx_red, NM * (g + 1))
                nxt(nc.vector.tensor_tensor(mx[:, 7:8], mx[:, 7:8], mx[:, 8:9], ALU.max), 0)
                c = c_q[:, bass.ds(hd, 1), :].rearrange("p a t -> p (a t)")
                nxt(nc.vector.tensor_tensor(m_q[:, :], mx[:, 0:NB], c, ALU.add), 1)
                nxt(nc.vector.tensor_tensor(r_q[:, :], c, m_q[:, :], ALU.subtract), 2)
                nxt(nc.vector.tensor_copy(r_hi[:, :], r_q[:, :]), 3)
                if not isinstance(g, int) or g >= 1:
                    dve.wait_ge(rt_done, g)
                nxt(nc.vector.tensor_copy(r_pad[:, :, HD + 2], r_hi[:, :].bitcast(F32)), 4)
                nxt(nc.vector.tensor_tensor(r_pad[:, :, HD + 3], r_q[:, :], r_hi[:, :].bitcast(F32), ALU.subtract), 5)

            def finish(g, p, s, c):
                C = 2 * g + c
                o, sums = (slice(0, HD), slice(HD, P)) if s == 0 else (slice(HD, P), slice(0, HD))
                dve.wait_ge(o_inv, C + 1)
                nc.vector.tensor_tensor(o_t[sums, :], ps[sums, 6 + c, :], o_r0[sums, :], ALU.mult).then_inc(o_step, 1)
                dve.wait_ge(o_step, 2 * C + 1)
                nc.vector.scalar_tensor_tensor(o_r1[o, :], o_t[sums, :], 2.0, o_r0[sums, :], ALU.subtract, ALU.mult).then_inc(o_step, 1)
                dve.wait_ge(o_step, 2 * C + 2)
                nc.vector.scalar_tensor_tensor(mix[o, bass.ds(p, 1), HALF * c:HALF * (c + 1)].rearrange("p a c -> p (a c)"),
                                               ps[o, 6 + c, :], -1.0, o_r1[o, :], ALU.mult, ALU.mult).then_inc(o_evac, 1)

            def wo_split(w):
                dve.wait_ge(wohi_done, w + 1)
                nc.vector.tensor_tensor(wo_lo[:, w % KT, :], wo_buffer(w)[0], wo_hi[:, w % KT, :].bitcast(F32),
                                        ALU.subtract).then_inc(wolo_done, 1)

            def mix_split(v, t, slot):
                dve.wait_ge(mixhi_done, v + 1)
                nc.vector.tensor_tensor(mix_parts[:, slot, 1, :, :], mix[:, :, bass.ds(t * P, P)],
                                        mix_parts[:, slot, 0, :, :].bitcast(F32), ALU.subtract).then_inc(mixlo_done, 1)

            def head(g, p, s, nxt):
                for u in range(NU):
                    if nxt is not None:
                        if u < 2:
                            prep(*nxt, u)
                        for m in MAX_STEPS.get(u, ()):
                            row_max(nxt[0], nxt[2], m)
                        if u == 9:
                            shift(nxt[0], nxt[0])
                    if u == LAG + 1 and not (isinstance(g, int) and g == 0):
                        finish(g - 1, p - 1 + s, 1 - s, 1)
                    if u == LAST[0] + LAG + 2:
                        finish(g, p, s, 0)
                    if nxt is not None and u == 11:
                        prep(*nxt, 2)
                    if nxt is None:
                        if u < KT:
                            wo_split(u)
                        elif u in (11, 12):
                            mix_split(u - 11, u - 11, u - 11)

            dve.wait_ge(proj_evac, N_PROJ - N_EARLY)
            for i in range(3):
                prep(0, 0, 0, i)
            for m in range(NM):
                row_max(0, 0, m)
            dve.wait_ge(att_init, R_FILLS)
            shift(0, 0)
            dve.wait_ge(pw_done, 2)
            head(0, 0, 0, (1, 0, 1))
            head(1, 0, 1, (2, 1, 0))
            with dve.Fori(1, 3) as p:
                head(2 * p, p, 0, (2 * p + 1, p, 1))
                head(2 * p + 1, p, 1, (2 * p + 2, p + 1, 0))
            head(6, 3, 0, (7, 3, 1))
            head(7, 3, 1, None)
            finish(7, 3, 1, 1)

            def residual(v, t, c, slot):
                dve.wait_ge(out_done, v + 1)
                dst = h[:, bass.ds(t, 1), HALF * c:HALF * (c + 1)].rearrange("p a c -> p (a c)")
                nc.vector.tensor_tensor(dst, ps[:, slot, :], dst, ALU.add).then_inc(h_evac, 1)

            def h_scale(t, slot):
                dve.wait_ge(std2, t + 1)
                nc.vector.reciprocal(rstd[:, bass.ds(t, 1)], std[:, bass.ds(t, 1)]).then_inc(rstd2, 1)
                dve.wait_ge(rstd2, t + 1)
                nc.vector.tensor_scalar(hs[:, slot, :], h[:, bass.ds(t, 1), :].rearrange("p a c -> p (a c)"),
                                        rstd[:, bass.ds(t, 1)], None, ALU.mult).then_inc(hs_done, 1)

            def h_gain(t, slot):
                dve.wait_ge(tr2, t + 1)
                if not isinstance(t, int) or t >= 1:
                    dve.wait_ge(h2lo_done, t)
                b = 4 + 2 * slot
                nc.vector.tensor_tensor(h32[:, :, :], ps[:, b:b + 2, :].rearrange("p b (k c) -> p (b k) c", c=P),
                                        g_of(G2, P), ALU.mult).then_inc(h32_done, 1)

            def h_low(t):
                dve.wait_ge(h2hi_done, t + 1)
                nc.vector.tensor_tensor(hn2_lo[:, :, bass.ds(t * P, P)], h32[:, :, :],
                                        hn2_hi[:, :, bass.ds(t * P, P)].bitcast(F32), ALU.subtract).then_inc(h2lo_done, 1)

            def next_pair(i):
                mix_split(2 * i + 2, 2 * i + 2, 0)
                residual(2 * i, 2 * i, 0, 0)
                mix_split(2 * i + 3, 2 * i + 3, 1)
                residual(2 * i + 1, 2 * i + 1, 0, 1)

            def normalize(t, slot):
                residual(NB + t, t, 1, slot)
                if not isinstance(t, int) or t < NB - 2:
                    mix_split(NB + t + 2, t + 2, slot)
                if not isinstance(t, int) or t >= 1:
                    h_gain(t - 1, 1 - slot)
                h_scale(t, slot)
                if not isinstance(t, int) or t >= 1:
                    h_low(t - 1)

            for i in range(NB):
                dve.wait_ge(s_xr[i], 16)
            next_pair(0)
            with dve.Fori(1, 3) as i:
                next_pair(i)
            mix_split(NB, 0, 0)
            residual(NB - 2, NB - 2, 0, 0)
            for w in range(KT, 2 * KT):
                wo_split(w)
            residual(NB - 1, NB - 1, 0, 1)
            mix_split(NB + 1, 1, 1)
            normalize(0, 0)
            normalize(1, 1)
            with dve.Fori(1, 3) as i:
                normalize(2 * i, 0)
                normalize(2 * i + 1, 1)
            normalize(NB - 2, 0)

            def mw_split(r, lo, hi, slot):
                dve.wait_ge(mwhi_done, r + 1)
                nc.vector.tensor_tensor(lo, m_raw[:, slot, :], hi.bitcast(F32), ALU.subtract).then_inc(mwlo_done, 1)

            def w1_split(q, i):
                c = slice(HALF * (i % 2), HALF * (i % 2 + 1))
                mw_split(16 * q + i, w1_parts[:, i // 2, 1, c], w1_parts[:, i // 2, 0, c], i % 2)

            def w2_split(q, i):
                c = slice(HALF * (i % 2), HALF * (i % 2 + 1))
                mw_split(16 * q + 8 + i, w2_lo[:, i // 2, c], w2_hi[:, i // 2, c], i % 2)

            def hidden(q, i):
                G = 8 * q + i
                dve.wait_ge(relu_done, G + 1)
                nc.vector.tensor_tensor(act32[:, i % 2, :], act32[:, i % 2, :], act32[:, i % 2, :], ALU.mult).then_inc(asq_done, 1)
                w2_split(q, i)
                dve.wait_ge(ahi_done, G + 1)
                c = slice(HALF * (i // 4), HALF * (i // 4 + 1))
                nc.vector.tensor_tensor(a_lo[:, i % 4, c], act32[:, i % 2, :], a_hi[:, i % 4, c].bitcast(F32),
                                        ALU.subtract).then_inc(alo_done, 1)

            def accumulate(q, t):
                b = 4 + 2 * (t % 2)
                dve.wait_ge(out_done, 2 * NB + NB * q + t + 1)
                dst = h[:, t, :].rearrange("p (b c) -> p b c", b=2)
                nc.vector.tensor_tensor(dst, ps[:, b:b + 2, :], dst, ALU.add).then_inc(h_evac, 1)

            def w1_first_split(i):
                dve.wait_ge(mwhi_done, i + 1)
                c = slice(HALF * (i % 2), HALF * (i % 2 + 1))
                nc.vector.tensor_tensor(w1_parts[:, i // 2, 1, c], w1_first[:, i, :], w1_parts[:, i // 2, 0, c].bitcast(F32),
                                        ALU.subtract).then_inc(mwlo_done, 1)

            w1_first_split(0)
            w1_first_split(1)
            normalize(NB - 1, 1)
            w1_first_split(2)
            w1_first_split(3)
            h_gain(NB - 1, 1)
            h_low(NB - 1)
            for i in range(4, 8):
                w1_first_split(i)
            with dve.Fori(0, CH - 1) as q:
                for i in range(8):
                    hidden(q, i)
                for t in range(NB):
                    w1_split(q + 1, t)
                    accumulate(q, t)
            for i in range(8):
                hidden(CH - 1, i)

            def output(t):
                dve.wait_ge(std3, t + 1)
                nc.vector.reciprocal(rstd[:, t:t + 1], std[:, t:t + 1]).then_inc(rstd3, 1)
                dve.wait_ge(rstd3, t + 1)
                if t >= 2:
                    dve.wait_ge(s_out[t % 2], 16 * (t // 2))
                nc.vector.scalar_tensor_tensor(y[:, t % 2, :], h[:, t, :], rstd[:, t:t + 1], g_row[:, :],
                                               ALU.mult, ALU.mult).then_inc(y_done, 1)

            for t in range(NB):
                accumulate(CH - 1, t)
                if t == 0:
                    dve.wait_ge(s_g, 16)
                output(t)

        @block.tensor
        def _(pe):
            def three(dst, stat, mov, first, last):
                nc.tensor.matmul(dst, stat[0], mov[0], start=first, stop=False)
                nc.tensor.matmul(dst, stat[0], mov[1], start=False, stop=False)
                return nc.tensor.matmul(dst, stat[1], mov[0], start=False, stop=last)

            def transpose_x(T):
                rows = cols_of(T)[1]
                pe.wait_ge(xs_done, T + 1)
                if T >= 2:
                    pe.wait_ge(hn32_done, T - 1)
                for k in range(KT):
                    ins = nc.tensor.transpose(ps[:, 2 * (T % 2) + k // 4, P * (k % 4):P * (k % 4) + rows],
                                              xs[0:rows, T % 2, P * k:P * (k + 1)], ident[0:rows, 0:rows])
                ins.then_inc(tr_done, 1)

            def project_v(T):
                k0, rows = cols_of(T)
                pe.wait_ge(hnlo_done, T + 1)
                if T >= 2:
                    pe.wait_ge(v_evac, T - 1)
                b = 4 + 2 * (T % 2)
                n = VF // 2
                for i in range(2):
                    for k in range(KT):
                        if T == 0 and i == 0:
                            pe.wait_ge(wvlo_done, k // 2 + 1)
                            if k == KT // 2:
                                transpose_x(1)
                        ins = three(ps[0:rows, b + i, 0:n], (hn_hi[:, k, k0:k0 + rows], hn_lo[:, k, k0:k0 + rows]),
                                    (wv_hi[:, k, n * i:n * (i + 1)], wv_lo[:, k, n * i:n * (i + 1)]), k == 0, k == KT - 1)
                ins.then_inc(v_done, 1)

            pe.wait_ge(s_consts, 16)
            transpose_x(0)
            project_v(0)
            for T in range(1, NB + 1):
                if T < NB:
                    transpose_x(T + 1)
                project_v(T)

            def project(n, slot, tokens, between=None):
                pe.wait_ge(wlo_done, n + 1)
                for k in range(KT):
                    if k == KT // 2 and between:
                        between()
                    stat = (w_hi[:, slot, k, :], w_lo[:, slot, k, :])
                    for a, b_ in ((0, 0), (0, 1), (1, 0)):
                        for i, (c0, width) in enumerate(tokens):
                            mov = (hn_hi, hn_lo)[b_][:, k, c0:c0 + width]
                            ins = nc.tensor.matmul(ps[:, 3 * slot + i, 0:width], stat[a], mov,
                                                   start=(k == 0 and a + b_ == 0), stop=(k == KT - 1 and a == 1))
                ins.then_inc(proj_done, 1)

            for n in range(N_EARLY):
                kind, j = ORDER[n]
                if n == 1:
                    pe.wait_ge(v_evac, NB + 1)
                elif n >= 2:
                    before, jb = ORDER[n - 2]
                    if before == GATE:
                        pe.wait_ge(sig_done, jb + 1)
                    elif before == CONF_A:
                        pe.wait_ge(glu_done, jb + 1)
                    elif before == SC_C:
                        pe.wait_ge(scc_done, jb + 1)
                    elif before == SC_U:
                        pe.wait_ge(cu_done, jb + 1)
                    else:
                        pe.wait_ge(sc_step, 4 * jb + 4)
                project(n, n % 2, REAL_TOKENS if kind == SC_B else ALL_TOKENS)
                if n == 1:
                    pe.wait_ge(lf_dve, 8)
                    for T in range(NB):
                        k0, rows = cols_of(T)
                        b, c0 = (6, k0) if T < 4 else (7, k0 - 400)
                        ins = nc.tensor.transpose(ps[0:HEADS, b, c0:c0 + rows], lf[6][0:rows, T, :], ident[0:rows, 0:rows])
                    ins.then_inc(lft_done, 1)
                if n == 2:
                    pe.wait_ge(lft_evac, 1)
                    nc.tensor.transpose(ps[0:HEADS, 6, 0:P], lf[6][:, NB, :], ident[:, :]).then_inc(lft_done, 1)
                if n == 3:
                    pe.wait_ge(lf_dve, 9)
                    pe.wait_ge(lft_evac, 2)
                    for t in range(NB):
                        ins = nc.tensor.transpose(ps[:, 6, HEADS * t:HEADS * (t + 1)],
                                                  c_t[:, META + P * t:META + P * (t + 1)], ident[0:HEADS, 0:HEADS])
                    ins.then_inc(cq_tr, 1)

            def ln_transposes(r):
                for j in range(2):
                    pe.wait_ge(conv_step[j], CONF_K)
                if r == 0:
                    pe.wait_ge(cq_evac, 1)
                else:
                    pe.wait_ge(ln_norm, 8)
                for i in range(4):
                    t = 4 * r + i
                    for j in range(2):
                        c0 = D_CONF * (i % 2) + P * j
                        ins = nc.tensor.transpose(ps[:, 6 + i // 2, c0:c0 + P], dw[:, j, P * t:P * (t + 1)], ident[:, :])
                ins.then_inc(ln_tr, 1)

            def queries(n):
                if isinstance(n, int) and n == N_EARLY:
                    pe.wait_ge(cu_done, 2)
                elif not isinstance(n, int) or n > N_EARLY:
                    pe.wait_ge(proj_evac, n - N_EARLY - 1)
                project(n, 0, REAL_TOKENS)

            def keys(n, between=None):
                if isinstance(n, int) and n == N_EARLY + 1:
                    pe.wait_ge(sc_step, 8)
                else:
                    pe.wait_ge(proj_evac, n - N_EARLY - 1)
                project(n, 1, ALL_TOKENS, between)

            queries(N_EARLY)
            keys(N_EARLY + 1)
            def ln_transposes_back(j):
                if j == 0:
                    pe.wait_ge(ln_norm, 16)
                else:
                    pe.wait_ge(z_done, 1)
                for t in range(NB):
                    ins = nc.tensor.transpose(ps[:, 6 + t // 4, P * (t % 4):P * (t % 4 + 1)],
                                              normed[:, t, P * j:P * (j + 1)], ident[:, :])
                ins.then_inc(ln_back, 1)

            queries(N_PROJ - 6)
            keys(N_PROJ - 5)
            queries(N_PROJ - 4)
            ln_transposes(0)
            keys(N_PROJ - 3)
            ln_transposes(1)
            queries(N_PROJ - 2)
            ln_transposes_back(0)
            keys(N_PROJ - 1, lambda: ln_transposes_back(1))

            def row_max(g, s, m):
                block_, c0, w, parts = MAXES[m]
                G, b = NM * g + m, 2 + 2 * ((NM * s + m) % 2)
                if m == 0:
                    pe.wait_ge(qk_hi, g + 1)
                    pe.wait_ge(s_c[s], 16 * (g // 2 + 1) if isinstance(g, int) else 8 * g + 16 - 8 * s)
                    if not isinstance(g, int) or g >= 1:
                        pe.wait_ge(r_ready, g)
                if not isinstance(G, int) or G >= 2:
                    pe.wait_ge(mx_red, G - 1)
                last = c0 + w * parts == META + P * (block_ + 1)
                for i in range(parts):
                    masked = last and i == parts - 1
                    a = c0 + w * i
                    ins = nc.tensor.matmul(ps[:, b + i, 0:w], qm[s][0:HD + 2, P * block_:P * (block_ + 1)],
                                           km[s][0:HD + 2, a:a + w], start=True, stop=not masked)
                    if masked:
                        ins = nc.tensor.matmul(ps[:, b + i, w - P:w], identb[:, :], mask_qk[:, :], start=False, stop=True)
                ins.then_inc(mx_mm, 1)

            def r_transposes(g):
                pe.wait_ge(r_step, 6 * g + 6)
                for t in range(NB):
                    ins = nc.tensor.transpose(ps[0:HD + 4, 2 + t // 4, P * (t % 4):P * (t % 4 + 1)], r_pad[:, t, :], ident[:, :])
                ins.then_inc(rt_done, 1)

            def scores(g, s, u):
                U, b = NU * g + u, (NU * s + u) % 2
                k0, rows, q0, n, diagonal = unit(u)
                if u == 0:
                    pe.wait_ge(qk_lo, g + 1)
                    pe.wait_ge(qk_lo2, g + 1)
                    pe.wait_ge(r_ready, g + 1)
                if not isinstance(U, int) or U >= 2:
                    pe.wait_ge(exp_done, U - 1)
                dst = ps[0:rows, b, 0:n]
                nc.tensor.matmul(dst, km[s][0:HD + 4, k0:k0 + rows], qm[s][0:HD + 4, q0:q0 + n], start=True, stop=False)
                ins = nc.tensor.matmul(dst, kx[s][:, k0:k0 + rows], qx[s][:, q0:q0 + n], start=False, stop=not diagonal)
                if diagonal:
                    ins = nc.tensor.matmul(ps[:, b, 0:P], identb[:, :], mask_kq[:, :], start=False, stop=True)
                ins.then_inc(sc_done, 1)

            def weigh(g, s, u):
                U, b = NU * g + u, (NU * s + u) % RING
                _, rows, q0, n, _ = unit(u)
                c, T = UNITS[u]
                pe.wait_ge(exp_done, U + 1)
                if u == 0:
                    pe.wait_ge(v_ready, g + 1)
                if T == 0:
                    if isinstance(g, int) and g == 0:
                        pe.wait_ge(pw_evac, 2)
                    else:
                        pe.wait_ge(o_evac, 2 * g + c - 1)
                c0 = q0 - HALF * c
                last = u == LAST[c]
                ins = nc.tensor.matmul(ps[:, 6 + c, c0:c0 + n], v_one[s][0:rows, T, :], p32[0:rows, b, 0:n],
                                       start=T == 0, stop=last)
                ins.then_inc(pv_done, 1)

            def head(g, s, nxt):
                for u in range(NU):
                    scores(g, s, u)
                    if nxt is not None:
                        for m in MAX_STEPS.get(u, ()):
                            row_max(nxt[0], nxt[1], m)
                        if u == 12:
                            r_transposes(nxt[0])
                    if u >= LAG:
                        weigh(g, s, u - LAG)
                    elif not (isinstance(g, int) and g == 0):
                        weigh(g - 1, 1 - s, NU - LAG + u)

            def pointwise(o):
                pe.wait_ge(slo_done, 2)
                pe.wait_ge(wlo_done, N_PROJ + 1)
                pe.wait_ge(z_done, 2)
                b = 6 - 6 * o
                for k in range(2):
                    c0 = D_CONF * k + P * o
                    stat = [w[:, 0, :, :].rearrange("p k c -> p (k c)")[:, c0:c0 + P] for w in (w_hi, w_lo)]
                    for i in range(2):
                        c = slice(HALF * i, HALF * (i + 1))
                        ins = three(ps[:, b + i, :], stat, (s_hi[:, k, c], s_lo[:, k, c]), k == 0, k == 1)
                ins.then_inc(pw_done, 1)

            pointwise(0)
            pointwise(1)
            pe.wait_ge(att_init, 2)
            pe.wait_ge(masks_ready, 1)
            pe.wait_ge(proj_evac, N_PROJ - N_EARLY)
            for m in range(NM):
                row_max(0, 0, m)
            r_transposes(0)
            pe.wait_ge(att_init, 4)
            pe.wait_ge(pw_evac, 2)
            head(0, 0, (1, 1))
            head(1, 1, (2, 0))
            with pe.Fori(1, 3) as p:
                head(2 * p, 0, (2 * p + 1, 1))
                head(2 * p + 1, 1, (2 * p + 2, 0))
            head(6, 0, (7, 1))
            head(7, 1, None)
            for u in range(NU - LAG, NU):
                weigh(7, 1, u)

            def project_out(v, b, slot):
                pe.wait_ge(mixlo_done, v + 1)
                if not isinstance(v, int) or v >= 2:
                    pe.wait_ge(h_evac, v - 1)
                for k in range(KT):
                    pe.wait_ge(wolo_done, KT * b + k + 1)
                    ins = three(ps[:, slot, :], (mix_parts[:, slot, 0, k, :], mix_parts[:, slot, 1, k, :]),
                                (wo_hi[:, k, :], wo_lo[:, k, :]), k == 0, k == KT - 1)
                    if b == 0 and k < KT - 1:
                        ins.then_inc(wo_used, 1)
                ins.then_inc(out_done, 1)

            def transpose_h(t, slot):
                pe.wait_ge(hs_done, t + 1)
                if not isinstance(t, int) or t >= 2:
                    pe.wait_ge(h32_done, t - 1)
                for k in range(KT):
                    ins = nc.tensor.transpose(ps[:, 4 + 2 * slot + k // 4, P * (k % 4):P * (k % 4 + 1)],
                                              hs[:, slot, P * k:P * (k + 1)], ident[:, :])
                ins.then_inc(tr2, 1)

            project_out(0, 0, 0)
            project_out(1, 0, 1)
            with pe.Fori(1, 4) as i:
                project_out(2 * i, 0, 0)
                project_out(2 * i + 1, 0, 1)
            project_out(NB, 1, 0)
            project_out(NB + 1, 1, 1)
            transpose_h(0, 0)
            project_out(NB + 2, 1, 0)
            transpose_h(1, 1)
            with pe.Fori(1, 3) as i:
                project_out(NB + 2 * i + 1, 1, 1)
                transpose_h(2 * i, 0)
                project_out(NB + 2 * i + 2, 1, 0)
                transpose_h(2 * i + 1, 1)
            project_out(2 * NB - 1, 1, 1)
            transpose_h(NB - 2, 0)

            def mlp(q):
                for i in range(2 * FT):
                    if isinstance(q, int) and q == 0 and i < 2:
                        if i == 0:
                            pe.wait_ge(h_evac, 2 * NB)
                            pe.wait_ge(h2lo_done, FT)
                        else:
                            transpose_h(NB - 1, 1)
                    f, half = i % FT, i // FT
                    if half == 0:
                        pe.wait_ge(mwlo_done, 16 * q + 2 * f + 2)
                    else:
                        pe.wait_ge(relu_done, 8 * q + i - 3)
                        if isinstance(q, int) and q == 0 and i == FT:
                            pe.wait_ge(h2lo_done, NB)
                    c = slice(HALF * half, HALF * (half + 1))
                    for k in range(KT):
                        w = slice(P * k, P * (k + 1))
                        ins = three(ps[:, f, :], (w1_parts[:, f, 0, w], w1_parts[:, f, 1, w]), (hn2_hi[:, k, c], hn2_lo[:, k, c]),
                                    k == 0, k == KT - 1)
                    ins.then_inc(m1_done, 1)
                for t in range(NB):
                    b = 4 + 2 * (t % 2)
                    if t % 4 == 0:
                        pe.wait_ge(alo_done, 8 * q + t + 4)
                    pe.wait_ge(h_evac, 2 * NB + NB * q + t - 1)
                    for f in range(FT):
                        if t == 0:
                            pe.wait_ge(mwlo_done, 16 * q + 8 + 2 * f + 2)
                        a = (a_hi[:, f, P * t:P * (t + 1)], a_lo[:, f, P * t:P * (t + 1)])
                        for i in range(2):
                            c = slice(HALF * i, HALF * (i + 1))
                            ins = three(ps[:, b + i, :], a, (w2_hi[:, f, c], w2_lo[:, f, c]), f == 0, f == FT - 1)
                    ins.then_inc(out_done, 1)

            mlp(0)
            with pe.Fori(1, CH - 1) as q:
                mlp(q)
            mlp(CH - 1)


def kernel(x, meta_tokens, mix_norm_g, w_in, b_forget, w_conf_dw, b_conf_dw, conf_ln_g, conf_ln_b, w_conf_pw,
           b_conf_pw, w_sc_conv, w_out, mlp_norm_g, w_mlp1, w_mlp2, final_norm_g):
    import concourse.bacc as bacc
    from concourse.bass_utils import run_bass_kernel_spmd

    def tiles(a):
        a = np.asarray(a)
        return a.reshape(-1, P, *a.shape[1:]).swapaxes(0, 1)

    win = tiles(w_in[0])
    par = np.concatenate([
        tiles(mix_norm_g[0]), tiles(mlp_norm_g[0]), tiles(b_conf_dw[0]),
        tiles(np.asarray(w_conf_dw[0]).T).reshape(P, -1), tiles(conf_ln_g[0]), tiles(conf_ln_b[0]), tiles(b_conf_pw[0]),
        tiles(np.asarray(w_sc_conv[0]).T).reshape(P, -1), np.broadcast_to(np.asarray(b_forget[0]), (P, HEADS))], axis=1)
    row, col = np.arange(P)[:, None], np.arange(P)[None, :]
    hidden = -1e30
    consts = np.stack([np.eye(P), np.where(col > row, hidden, 0.0), np.where(row > col, hidden, 0.0)], 1).astype(np.float32)
    arrays = {
        "x": np.asarray(x)[0], "meta": np.asarray(meta_tokens), "par": par, "consts": consts,
        "w_vf": win[:, :, 2 * D_ATTN:2 * D_ATTN + VF],
        "w_proj": np.stack([win[:, :, FIRST_COL[kind] + P * j:FIRST_COL[kind] + P * (j + 1)].reshape(P, -1)
                            for kind, j in ORDER]),
        "w_pw": tiles(w_conf_pw[0]).reshape(P, -1), "w_out": np.asarray(w_out[0]),
        "w1": np.asarray(w_mlp1[0]).reshape(KT, P, FF // P, P).transpose(2, 1, 0, 3).reshape(FF // P, P, D),
        "w2": np.asarray(w_mlp2[0]).reshape(FF // P, P, D),
        "g_fin": np.broadcast_to(np.asarray(final_norm_g), (P, D)),
    }
    nc = bacc.Bacc("TRN2", target_bir_lowering=False, num_devices=1)
    arrays = {f"in_{n}": np.ascontiguousarray(a) for n, a in arrays.items()}
    ins = [nc.dram_tensor(n, a.shape, mybir.dt.from_np(a.dtype), kind="ExternalInput").ap() for n, a in arrays.items()]
    out = nc.dram_tensor("out", (SEQ, D), F32, kind="ExternalOutput").ap()
    build(nc, *ins, out)
    r = run_bass_kernel_spmd(nc, [arrays], core_ids=[0])
    return r.results[0]["out"].reshape(1, SEQ, D)
```

```python
from contextlib import ExitStack

import numpy as np

import concourse.bass as bass
from concourse import mybir

F32 = mybir.dt.float32
F32R = mybir.dt.float32r
BF16 = mybir.dt.bfloat16
ALU = mybir.AluOpType
ACT = mybir.ActivationFunctionType
AX = mybir.AxisListType

P = 128
D = 1024
SEQ = 1024
META = 16
TOK = SEQ + META
HEADS = 8
HD = 64
D_ATTN = HEADS * HD
D_CONF = 256
CONF_K = 31
SC_K = 3
FF = 4096
EPS = 1e-6
KT = D // P
NB = SEQ // P
VF = D_ATTN + HEADS
HALF = 512
CH = FF // HALF
FT = HALF // P

G1, G2 = 0, 8
B_DW, W_DW = 16, 18
LN_G, LN_B = W_DW + 2 * CONF_K, W_DW + 2 * CONF_K + 2
B_PW = LN_B + 2
W_SC = B_PW + 2
B_F = W_SC + 2 * SC_K
N_PAR = B_F + HEADS

GATE, CONF_A, SC_B, SC_C, SC_U, Q, K = range(7)
ORDER = [(GATE, 0), (CONF_A, 0), (GATE, 1), (CONF_A, 1)] \
    + [(kind, j) for j in range(2) for kind in (SC_C, SC_U, SC_B)] \
    + [(kind, p) for p in range(4) for kind in (Q, K)]
FIRST_COL = {Q: 0, K: D_ATTN, CONF_A: 3 * D_ATTN + HEADS, GATE: 3 * D_ATTN + HEADS + D_CONF,
             SC_B: 3 * D_ATTN + HEADS + 2 * D_CONF, SC_C: 3 * D_ATTN + HEADS + 3 * D_CONF,
             SC_U: 3 * D_ATTN + HEADS + 4 * D_CONF}
N_PROJ = len(ORDER)
N_EARLY = 10

LATE = 12
first_taps = [(0, k) for k in range(10)]
taps_in_turn = [(j, k) for k in range(CONF_K - LATE) for j in (1, 0)]
taps_in_turn = [t for t in taps_in_turn if t not in first_taps]
EARLY_TAPS = [[]] * 2 + [first_taps[0:5], first_taps[5:10]] + [taps_in_turn[5 * i:5 * i + 5] for i in range(5)] + [taps_in_turn[25:]]

ALL_TOKENS = [(0, 352), (352, 344), (696, 344)]
REAL_TOKENS = [(META, HALF), (META + HALF, HALF)]

UNITS = [(0, 0), (0, 1), (0, 2), (0, 3), (1, 0), (0, 4)] + [(1, T) for T in range(1, NB + 1)]
NU = len(UNITS)
LAST = (UNITS.index((0, NB // 2)), NU - 1)
RING = 4
N_FILLS = 8
R_FILLS = 6
LAG = 2
MAXES = [(0, 0, 144, 1), (1, 0, 272, 1), (2, 0, 400, 1), (3, 0, 264, 2), (4, 0, 328, 2), (5, 0, 392, 2),
         (6, 0, 456, 2), (7, 0, 348, 2), (7, 696, 344, 1)]
NM = len(MAXES)
MAX_STEPS = {5: (0,), 6: (1, 2), 7: (3, 4), 8: (5, 6), 9: (7, 8)}
WO_UNITS = (0, 1, 2, 3, 6, 7, 8, 9)
R_UNIT = 11


TILES = [NB] + list(range(NB))


def cols_of(T):
    return P * T, min(P, TOK - P * T)


def out_parts(t):
    return [(0, D)] if t < NB - 1 else [(0, HALF), (HALF, D)]


def unit(u):
    c, T = UNITS[u]
    k0, rows = cols_of(T)
    q0 = max(HALF * c, k0 - META)
    n = HALF * (c + 1) - q0
    first = META + q0 - k0
    return k0, rows, q0, n, (first, min(P - first, n)) if first < P else None


def build(nc, x, meta, par, consts, w_vf, w_proj, w_pw, w_out, w1, w2, g_fin, out):
    with ExitStack() as ctx:
        base = 16512
        at = [base]

        def sb(name, shape, dt, offset=None):
            if offset is not None:
                at[0] = offset
            size = 4 if dt != BF16 else 2
            for n in shape[1:]:
                size *= n
            t = nc.alloc_sbuf_tensor_at(name, shape, dt, offset=at[0])
            at[0] += -(-size // 32) * 32
            assert at[0] <= 229344, (name, at[0])
            return t

        def sem(name):
            return ctx.enter_context(nc.semaphore(name))

        R_HN = base
        R_MIX = R_HN + 2 * KT * TOK * 4
        R_H = R_MIX + KT * SEQ * 4
        R_QKV = R_H + KT * SEQ * 4
        R_RING = R_QKV + 2 * 4 * (SEQ + META) * 4 - 4 * META * 4 + (NB + 1) * D_ATTN * 4
        R_C = R_RING + 6 * 4096

        ident = sb("ident", [P, P], F32, R_C)
        identb = sb("identb", [P, P], BF16)
        mask_qk = sb("mask_qk", [P, P], BF16)
        mask_kq = sb("mask_kq", [P, P], BF16)
        prm = sb("prm", [P, N_PAR], F32)
        sumsq = sb("sumsq", [P, 12], F32)
        eps = sb("eps", [P, 1], F32)
        std = sb("std", [P, 12], F32)
        rstd = sb("rstd", [P, 12], F32)
        f_raw = sb("f_raw", [P, NB + 1, HEADS], F32)
        c_q = sb("c_q", [P, HEADS, NB], F32)
        mx = sb("mx", [P, NM], F32)
        m_q = sb("m_q", [P, NB], F32)
        r_q = sb("r_q", [P, NB], F32)
        r_hi = sb("r_hi", [P, NB], F32R)

        hn_hi = sb("hn_hi", [P, KT, TOK], F32R, R_HN)
        hn_lo = sb("hn_lo", [P, KT, TOK], F32R)
        x_in = sb("x_in", [P, NB, D], F32, R_H)
        x_tail = sb("x_tail", [META, D], F32, R_QKV)
        xs = sb("xs", [P, 2, D], F32)
        squares = sb("squares", [P, D], F32)
        wv_hi = sb("wv_hi", [P, KT, VF], F32R, R_QKV + 16384)
        wv_lo = sb("wv_lo", [P, KT, VF], F32R, R_MIX)
        hn32 = sb("hn32", [P, KT, P], F32, R_MIX + 16640)
        hn32b = sb("hn32b", [P, KT, P], F32)
        consts_f = sb("consts_f", [P, 3, P], F32)
        wv_raw = sb("wv_raw", [P, KT, VF], F32, R_RING)
        w_raw = sb("w_raw", [P, 2, D], F32, R_RING)
        w_hi = sb("w_hi", [P, 2, KT, P], F32R)
        w_lo = sb("w_lo", [P, 2, KT, P], F32R)
        q_raw = sb("q_raw", [P, 4, SEQ], F32, R_QKV)
        k_raw = sb("k_raw", [P, 4, TOK], F32)
        v_raw = sb("v_raw", [P, NB + 1, D_ATTN], F32)
        hn32 = [hn32, hn32b]
        lf = [sb(f"lf{i}", [P, NB + 1, HEADS], F32, R_QKV + 16384 + i * 288) for i in range(10)]
        lf_t = sb("lf_t", [HEADS, TOK], F32, R_QKV)
        c_t = sb("c_t", [HEADS, TOK], F32)
        c_neg = sb("c_neg", [HEADS, TOK], F32)
        c_hi = sb("c_hi", [HEADS, TOK], F32R, R_MIX)
        c_lo = sb("c_lo", [HEADS, TOK], F32R)
        PAD = CONF_K - 1 - META
        GLU = -(-(PAD + TOK) * 4 // 32) * 32
        glu = [sb("glu0", [P, PAD + TOK], F32, R_H), sb("glu1", [P, PAD + TOK], F32)]
        sig_gate = sb("sig_gate", [P, TOK], F32)
        sc_c = sb("sc_c", [P, TOK], F32)
        sc_cu = sb("sc_cu", [P, TOK], F32)
        dw = sb("dw", [P, 2, SEQ], F32)
        z = sb("z", [P, 2, SEQ], F32, R_H)
        normed = sb("normed", [P, NB, D_CONF], F32, R_H + 2 * GLU)
        silu = sb("silu", [P, 2, SEQ], F32, R_H + 2 * GLU + 3 * TOK * 4)
        ln_stats = sb("ln_stats", [P, NB, 6], F32)
        ln_mv = sb("ln_mv", [P, NB, 2], F32)
        ln_std = sb("ln_std", [P, NB], F32)
        ln_rstd = sb("ln_rstd", [P, NB], F32)
        s_hi = sb("s_hi", [P, 2, SEQ], F32R, R_MIX)
        s_lo = sb("s_lo", [P, 2, SEQ], F32R)
        mix = sb("mix", [P, KT, SEQ], F32, R_MIX)
        assert PAD >= 0 and R_H + KT * SEQ * 4 == R_QKV

        qm = [sb(f"qm{s}", [P, SEQ], F32R, R_HN if s == 0 else None) for s in range(2)]
        qx = [sb(f"qx{s}", [P, SEQ], F32R) for s in range(2)]
        km = [sb(f"km{s}", [P, TOK], F32R) for s in range(2)]
        kx = [sb(f"kx{s}", [P, TOK], F32R) for s in range(2)]
        v_one = [sb(f"v_one{s}", [P, NB + 1, P], F32) for s in range(2)]
        o_r0 = sb("o_r0", [P, HALF], F32)
        o_t = sb("o_t", [P, HALF], F32)
        o_r1 = sb("o_r1", [P, HALF], F32)
        r_pad = sb("r_pad", [P, NB, HD + 4], F32)
        p32 = sb("p32", [P, RING, HALF], F32, R_RING)

        h = sb("h", [P, NB, D], F32, R_H)
        wo_hi = sb("wo_hi", [P, KT, HALF], F32R, R_QKV)
        wo_lo = sb("wo_lo", [P, KT, HALF], F32R)
        mix_parts = sb("mix_parts", [P, 2, 2, KT, P], F32R)
        assert at[0] <= R_RING
        hs = sb("hs", [P, 2, D], F32, R_RING)
        h32 = sb("h32", [P, KT, P], F32)
        h_squares = sb("h_squares", [P, D], F32)
        wo_raw = [sb("wo_raw0", [P, 4, HALF], F32), sb("wo_raw1", [P, KT, HALF], F32, R_RING)]
        hn2_hi = sb("hn2_hi", [P, KT, SEQ], F32R, R_HN)
        hn2_lo = sb("hn2_lo", [P, KT, SEQ], F32R)

        a_hi = sb("a_hi", [P, FT, SEQ], F32R, R_MIX)
        a_lo = sb("a_lo", [P, FT, SEQ], F32R)
        w1_first = sb("w1_first", [P, 2 * FT, HALF], F32, R_MIX)
        w2_hi = sb("w2_hi", [P, FT, D], F32R, R_QKV)
        w2_lo = sb("w2_lo", [P, FT, D], F32R)
        w1_parts = sb("w1_parts", [P, FT, 2, D], F32R)
        act32 = sb("act32", [P, 2, HALF], F32)
        m_raw = sb("m_raw", [P, 2, HALF], F32)
        assert at[0] <= R_C
        g_row = sb("g_row", [P, D], F32, R_QKV + 2 * FT * D * 4)
        y = sb("y", [P, 2, D], F32)
        y_squares = sb("y_squares", [P, D], F32)

        ps = ctx.enter_context(nc.psum_tensor("ps", [P, 8, HALF], F32))
        c_scratch = nc.dram_tensor("c_scratch", (HEADS, 2, TOK), F32, kind="Internal").ap()

        s_par, s_ident, s_masks, s_g = sem("par_loaded"), sem("ident_loaded"), sem("masks_loaded"), sem("g_final_loaded")
        s_x = [sem(f"x_loaded{T}") for T in range(NB + 1)]
        s_wv = [sem(f"wv_loaded{i}") for i in range(4)]
        s_x_again = [sem(f"x_again{i}") for i in range(NB)]
        s_w = [sem(f"w_loaded{i}") for i in range(2)]
        s_wo = [sem(f"wo_loaded{i}") for i in range(4 + KT)]
        s_w1_first = [sem(f"w1_first_loaded{i}") for i in range(2 * FT)]
        s_m = [sem(f"mlp_w_loaded{i}") for i in range(2)]
        s_c = [sem(f"c_rows_loaded{i}") for i in range(2)]
        s_c_stored = sem("c_stored")
        s_out = [sem(f"out_stored{i}") for i in range(2)]
        masks_ready, pool_init, eps_ready = sem("masks_ready"), sem("pool_init"), sem("eps_ready")
        ss_done, std_done, rstd_done, xs_done = (sem(n) for n in ("ss_done", "std_done", "rstd_done", "xs_done"))
        tr_done, hn32_done, hnhi_done, hnlo_done = (sem(n) for n in ("tr_done", "hn32_done", "hnhi_done", "hnlo_done"))
        wvhi_done, wvlo_done, v_done, v_evac = (sem(n) for n in ("wvhi_done", "wvlo_done", "v_done", "v_evac"))
        whi_done, wlo_done, proj_done, proj_evac = (sem(n) for n in ("whi_done", "wlo_done", "proj_done", "proj_evac"))
        lf_act, lf_dve, lft_done, lft_evac, cq_tr, cq_evac = (sem(n) for n in ("lf_act", "lf_dve", "lft_done", "lft_evac", "cq_tr", "cq_evac"))
        sig_done, glu_done, cu_done, conv_step, sc_step, pad_done = (sem(n) for n in ("sig_done", "glu_done", "cu_done", "conv_step0", "sc_step", "pad_done"))
        scc_done = sem("scc_done")
        conv_step = [conv_step, sem("conv_step1")]
        ln_tr, ln_dve, ln_sqrt, ln_norm, ln_back = (sem(n) for n in ("ln_tr", "ln_dve", "ln_sqrt", "ln_norm", "ln_back"))
        z_done, zsig_done, silu_done, shi_done, slo_done = (sem(n) for n in ("z_done", "zsig_done", "silu_done", "shi_done", "slo_done"))
        pw_done, pw_evac = sem("pw_done"), sem("pw_evac")
        att_init, act_hi, dve_hi, q_dup, k_dup, dve_lo, pool_lo, v_ready = (sem(n) for n in ("att_init", "act_hi", "dve_hi", "q_dup", "k_dup", "dve_lo", "pool_lo", "v_ready"))
        mx_mm, mx_red, r_step, rt_done, r_ready = (sem(n) for n in ("mx_mm", "mx_red", "r_step", "rt_done", "r_ready"))
        sc_done, exp_done, pv_done = (sem(n) for n in ("sc_done", "exp_done", "pv_done"))
        o_ln, o_inv, o_step, o_evac = (sem(n) for n in ("o_ln", "o_inv", "o_step", "o_evac"))
        wohi_done, wolo_done, wo_used, mixhi_done, mixlo_done = (sem(n) for n in ("wohi_done", "wolo_done", "wo_used", "mixhi_done", "mixlo_done"))
        out_done, h_evac = sem("out_done"), sem("h_evac")
        h_ss_done, h_std_done, h_rstd_done, h_scaled = (sem(n) for n in ("h_ss_done", "h_std_done", "h_rstd_done", "h_scaled"))
        h_tr_done, h32_done, h2hi_done, h2lo_done = (sem(n) for n in ("h_tr_done", "h32_done", "h2hi_done", "h2lo_done"))
        mwhi_done, mwlo_done, m1_done, relu_done, asq_done, ahi_done, alo_done = (
            sem(n) for n in ("mwhi_done", "mwlo_done", "m1_done", "relu_done", "asq_done", "ahi_done", "alo_done"))
        y_ss_done, y_std_done, y_rstd_done, y_done = (sem(n) for n in ("y_ss_done", "y_std_done", "y_rstd_done", "y_done"))

        def x_tile(T):
            return x_tail[:, :] if T == NB else x_in[:, T, :]

        def banks(n):
            return 3 * (n % 2)

        def wo_buffer(w):
            return (wo_raw[0][:, w % 4, :], w % 4) if w < KT else (wo_raw[1][:, w - KT, :], 4 + w - KT)

        block = ctx.enter_context(nc.Block())

        @block.sync
        def _(sp):
            def load_x(T):
                k0, rows = cols_of(T)
                sp.dma_start(x_tile(T), x[k0 - META:k0 - META + rows, :]).then_inc(s_x[T], 16)

            load_x(NB)
            sp.dma_start(ident[:, :], consts[:, 0, :]).then_inc(s_ident, 16)
            sp.dma_start(prm[:, :], par).then_inc(s_par, 16)
            sp.dma_start(x_in[0:META, 0, :], meta).then_inc(s_x[0], 16)
            for i in range(4):
                sp.dma_start(wv_raw[:, 2 * i:2 * i + 2, :], w_vf[:, 2 * i:2 * i + 2, :]).then_inc(s_wv[i], 16)
                if i == 1:
                    sp.dma_start(x_in[META:P, 0, :], x[0:P - META, :]).then_inc(s_x[0], 16)
            for T in range(1, NB):
                load_x(T)
                if T == 2:
                    sp.dma_start(consts_f[:, :, :], consts).then_inc(s_masks, 16)

            def load_w(n, slot):
                if isinstance(n, int) and n < 2:
                    sp.wait_ge(wvlo_done, 4)
                else:
                    sp.wait_ge(wlo_done, n - 1)
                sp.dma_start(w_raw[:, slot, :], w_proj[n]).then_inc(s_w[slot], 16)

            for n in range(N_EARLY):
                load_w(n, n % 2)
                if n == 6:
                    sp.wait_ge(lf_dve, 12)
                    sp.dma_start(c_scratch[:, 0, :], c_hi[:, :].bitcast(F32)).then_inc(s_c_stored, 16)
                    sp.dma_start(c_scratch[:, 1, :], c_lo[:, :].bitcast(F32)).then_inc(s_c_stored, 16)
            with sp.Fori(0, 4) as p:
                load_w(N_EARLY + 2 * p, 0)
                load_w(N_EARLY + 2 * p + 1, 1)
            sp.wait_ge(wlo_done, N_PROJ - 1)
            sp.dma_start(w_raw[:, 0, 0:2 * D_CONF], w_pw).then_inc(s_w[0], 16)

            def load_c(g, s):
                sp.dma_start(km[s][HD:HD + 2, :].bitcast(F32), c_scratch[g]).then_inc(s_c[s], 16)

            sp.wait_ge(s_c_stored, 32)
            sp.wait_ge(att_init, 1)
            load_c(0, 0)
            sp.wait_ge(att_init, 3)
            load_c(1, 1)
            sp.wait_ge(slo_done, 2)
            for i in range(NB):
                sp.dma_start(h[:, i, :], x[P * i:P * (i + 1), :]).then_inc(s_x_again[i], 16)
            with sp.Fori(0, 3) as p:
                for s in range(2):
                    sp.wait_ge(sc_done, NU * (2 * p + s + 1))
                    load_c(2 * p + s + 2, s)

            for w in range(2 * KT):
                b, k = w // KT, w % KT
                buf, i = wo_buffer(w)
                if 4 <= w < KT:
                    sp.wait_ge(wolo_done, w - 3)
                elif w == KT:
                    sp.wait_ge(pv_done, NU * HEADS)
                sp.dma_start(buf, w_out[P * k:P * (k + 1), HALF * b:HALF * (b + 1)]).then_inc(s_wo[i], 16)

            sp.wait_ge(mixlo_done, 2 * NB)
            for i in range(2 * FT):
                sp.dma_start(w1_first[:, i, :], w1[i // 2, :, HALF * (i % 2):HALF * (i % 2 + 1)]).then_inc(s_w1_first[i], 16)

            def load_m(r, slot, src):
                sp.wait_ge(mwlo_done, r - 1)
                sp.dma_start(m_raw[:, slot, :], src).then_inc(s_m[slot], 16)

            def load_w1(q):
                for i in range(2 * FT):
                    load_m(16 * q + i, i % 2, w1[FT * q + i // 2, :, HALF * (i % 2):HALF * (i % 2 + 1)])

            def load_w2(q):
                for i in range(2 * FT):
                    load_m(16 * q + 8 + i, i % 2, w2[FT * q + i // 2, :, HALF * (i % 2):HALF * (i % 2 + 1)])

            with sp.Fori(0, CH - 1) as q:
                load_w2(q)
                load_w1(q + 1)
            load_w2(CH - 1)
            sp.wait_ge(m1_done, 2 * FT * CH)
            sp.dma_start(g_row[:, :], g_fin).then_inc(s_g, 16)
            for t in range(NB):
                for i, (c0, c1) in enumerate(out_parts(t)):
                    sp.wait_ge(y_done, t + 1 + i)
                    sp.dma_start(out[P * t:P * (t + 1), c0:c1], y[:, t % 2, c0:c1]).then_inc(s_out[t % 2], 16)
            for i in range(2):
                sp.wait_ge(s_out[i], 16 * (NB // 2 + i))

        @block.gpsimd
        def _(pool):
            nc.gpsimd.memset(f_raw[:, NB, :], 0.0).then_inc(pool_init, 1)
            pool.wait_ge(pool_init, 1)
            nc.gpsimd.memset(v_raw[:, NB, :], 0.0).then_inc(pool_init, 1)
            pool.wait_ge(proj_done, N_PROJ)

            def fill(i, dst, value):
                if i:
                    pool.wait_ge(att_init, i)
                nc.gpsimd.memset(dst, value).then_inc(att_init, 1)

            fills = [(km[0][HD:HD + 4, :], 1.0), (qm[0][HD:HD + 4, :], 1.0), (km[1][HD:HD + 4, :], 1.0), (qm[1][HD:HD + 4, :], 1.0),
                     (r_pad[:, :, :], 0.0), (r_pad[:, :, HD:HD + 2], 1.0),
                     (v_one[0][:, :, HD:P], 1.0), (v_one[1][:, :, 0:HD], 1.0)]
            assert len(fills) == N_FILLS
            for i, (dst, value) in enumerate(fills):
                fill(i, dst.bitcast(F32), value)

            def prep(g, p, s):
                rows, cols = slice(HD * s, HD * (s + 1)), slice(HD * s, HD * (s + 1))
                if not isinstance(g, int) or g >= 2:
                    pool.wait_ge(pv_done, NU * (g - 1))
                if not isinstance(g, int) or g >= 1:
                    pool.wait_ge(pool_lo, g)
                nc.gpsimd.tensor_copy(v_one[s][:, :, cols], v_raw[:, :, bass.ds(p * P + s * HD, HD)]).then_inc(v_ready, 1)
                pool.wait_ge(dve_hi, g + 1)
                pool.wait_ge(k_dup, g + 1)
                pool.wait_ge(v_ready, g + 1)
                raw = (q_raw, k_raw)[s][rows, bass.ds(p, 1), :].rearrange("p a c -> p (a c)")
                hi = qm[0][0:HD, :] if s == 0 else kx[1][HD:P, :]
                lo = qx[0][0:HD, :] if s == 0 else kx[1][HD:P, :]
                nc.gpsimd.tensor_tensor(lo, raw, hi.bitcast(F32), ALU.subtract).then_inc(pool_lo, 1)

            pool.wait_ge(att_init, N_FILLS)
            pool.wait_ge(proj_evac, N_PROJ - N_EARLY)
            prep(0, 0, 0)
            prep(1, 0, 1)
            with pool.Fori(1, 4) as p:
                prep(2 * p, p, 0)
                prep(2 * p + 1, p, 1)

        @block.scalar
        def _(act):
            def square(i):
                T = TILES[i]
                rows = cols_of(T)[1]
                act.wait_ge(s_x[T], 16 if T else 32)
                if i:
                    act.wait_ge(ss_done, i)
                nc.scalar.activation(squares[0:rows, :], x_tile(T), ACT.Square,
                                     accum_out=sumsq[0:rows, T:T + 1]).then_inc(ss_done, 1)

            def root(i):
                T = TILES[i]
                rows = cols_of(T)[1]
                act.wait_ge(ss_done, i + 1)
                nc.scalar.activation(std[0:rows, T:T + 1], sumsq[0:rows, T:T + 1], ACT.Sqrt, scale=1.0 / D,
                                     bias=eps[0:rows, :]).then_inc(std_done, 1)

            def evac_v(i):
                T = TILES[i]
                rows = cols_of(T)[1]
                b = 4 + 2 * (i % 2)
                if T == NB:
                    act.wait_ge(pool_init, 2)
                act.wait_ge(v_done, i + 1)
                nc.scalar.activation(v_raw[0:rows, T, 0:VF // 2], ps[0:rows, b, 0:VF // 2], ACT.Copy)
                nc.scalar.activation(v_raw[0:rows, T, VF // 2:D_ATTN], ps[0:rows, b + 1, 0:D_ATTN - VF // 2], ACT.Copy)
                nc.scalar.activation(f_raw[0:rows, T, :], ps[0:rows, b + 1, D_ATTN - VF // 2:VF // 2],
                                     ACT.Copy).then_inc(v_evac, 1)

            def split_wv(i):
                act.wait_ge(s_wv[i], 16)
                nc.scalar.activation(wv_hi[:, 2 * i:2 * i + 2, :], wv_raw[:, 2 * i:2 * i + 2, :], ACT.Copy).then_inc(wvhi_done, 1)

            def split_hn(i):
                k0, rows = cols_of(TILES[i])
                act.wait_ge(hn32_done, i + 1)
                nc.scalar.activation(hn_hi[:, :, k0:k0 + rows], hn32[i % 2][:, :, 0:rows], ACT.Copy).then_inc(hnhi_done, 1)

            nc.scalar.preload_act_table_set("sqrt_and_others")
            act.wait_ge(eps_ready, 1)
            square(0)
            root(0)
            split_wv(0)
            split_hn(0)
            split_wv(1)
            square(1)
            root(1)
            split_wv(2)
            split_wv(3)
            for i in range(1, NB + 1):
                if i < NB:
                    square(i + 1)
                    root(i + 1)
                split_hn(i)
                if i >= 2:
                    evac_v(i - 2)

            def split_hi(n, slot, size=D):
                act.wait_ge(s_w[slot], 16 * (n // 2 + 1) if isinstance(n, int) else n * 8 + 16 - 8 * slot)
                act.wait_ge(proj_done, n - 1) if not isinstance(n, int) or n >= 2 else None
                dst = w_hi[:, slot, :, :].rearrange("p k c -> p (k c)")
                nc.scalar.activation(dst[:, 0:size], w_raw[:, slot, 0:size], ACT.Copy).then_inc(whi_done, 1)

            split_hi(0, 0)
            evac_v(NB - 1)
            split_hi(1, 1)
            evac_v(NB)

            nc.scalar.preload_act_table_set("natural_log_exp_and_others")
            act.wait_ge(lf_dve, 1)
            nc.scalar.activation(lf[1][:, :, :], lf[0][:, :, :], ACT.Abs).then_inc(lf_act, 1)
            act.wait_ge(lf_act, 1)
            nc.scalar.activation(lf[2][:, :, :], lf[1][:, :, :], ACT.Exp, scale=-1.0).then_inc(lf_act, 1)
            act.wait_ge(lf_dve, 2)
            nc.scalar.activation(lf[4][:, :, :], lf[3][:, :, :], ACT.Ln).then_inc(lf_act, 1)

            def from_banks(n, dst, func):
                b = banks(n)
                act.wait_ge(proj_done, n + 1)
                c0 = ALL_TOKENS[0][1]
                nc.scalar.activation(dst[:, 0:c0], ps[:, b, 0:c0], func)
                return nc.scalar.activation(dst[:, c0:TOK].rearrange("p (b c) -> p b c", b=2),
                                            ps[:, b + 1:b + 3, 0:ALL_TOKENS[1][1]], func)

            for n in range(N_EARLY):
                kind, j = ORDER[n]
                if kind == GATE:
                    act.wait_ge(xs_done, NB + 1)
                    if j:
                        act.wait_ge(glu_done, j)
                    from_banks(n, sig_gate, ACT.Sigmoid).then_inc(sig_done, 1)
                elif kind == SC_C:
                    if j:
                        act.wait_ge(cu_done, j)
                    from_banks(n, sc_c, ACT.Copy).then_inc(scc_done, 1)
                split_hi(n + 2, n % 2)

            def evac_q(n, p):
                act.wait_ge(proj_done, n + 1)
                act.wait_ge(s_c_stored, 32)
                act.wait_ge(cq_evac, 1)
                nc.scalar.activation(q_raw[:, bass.ds(p, 1), :].rearrange("p a (b c) -> p (a b) c", b=2), ps[:, 0:2, :], ACT.Copy,
                                     scale=float(HD) ** -0.5).then_inc(proj_evac, 1)

            def evac_k(n, p):
                act.wait_ge(proj_done, n + 1)
                c0 = ALL_TOKENS[0][1]
                dst = k_raw[:, bass.ds(p, 1), :].rearrange("p a c -> p (a c)")
                nc.scalar.activation(dst[:, 0:c0], ps[:, 3, 0:c0], ACT.Copy)
                nc.scalar.activation(dst[:, c0:TOK].rearrange("p (b c) -> p b c", b=2),
                                     ps[:, 4:6, 0:ALL_TOKENS[1][1]], ACT.Copy).then_inc(proj_evac, 1)

            with act.Fori(0, 2) as p:
                n = N_EARLY + 2 * p
                evac_q(n, p)
                split_hi(n + 2, 0)
                evac_k(n + 1, p)
                split_hi(n + 3, 1)

            def ln_root(r):
                act.wait_ge(ln_dve, 3 * r + 2)
                nc.scalar.activation(ln_std[:, 4 * r:4 * r + 4], ln_rstd[:, 4 * r:4 * r + 4], ACT.Sqrt).then_inc(ln_sqrt, 1)

            def swish_sigmoid(j):
                act.wait_ge(ln_back, j + 1)
                nc.scalar.activation(z[:, j, :].rearrange("p (b c) -> p b c", b=2), ps[:, 6:8, :], ACT.Identity, scale=prm[:, LN_G + j:LN_G + j + 1],
                                     bias=prm[:, LN_B + j:LN_B + j + 1]).then_inc(z_done, 1)
                act.wait_ge(z_done, j + 1)
                nc.scalar.activation(silu[:, j, :], z[:, j, :], ACT.Sigmoid).then_inc(zsig_done, 1)

            def swish_hi(j):
                act.wait_ge(silu_done, j + 1)
                nc.scalar.activation(s_hi[:, j, :], silu[:, j, :], ACT.Copy).then_inc(shi_done, 1)

            evac_q(N_PROJ - 4, 2)
            split_hi(N_PROJ - 2, 0)
            ln_root(0)
            evac_k(N_PROJ - 3, 2)
            split_hi(N_PROJ - 1, 1)
            ln_root(1)
            evac_q(N_PROJ - 2, 3)
            split_hi(N_PROJ, 0, 2 * D_CONF)
            for j in range(2):
                swish_sigmoid(j)
                swish_hi(j)
            evac_k(N_PROJ - 1, 3)

            def prep(g, p, s):
                rows = slice(HD * s, HD * (s + 1))
                dst, src = (qm[1], q_raw) if s else (km[0], k_raw)
                if not isinstance(g, int) or g >= 2:
                    act.wait_ge(sc_done, NU * (g - 1))
                nc.scalar.activation(dst[0:HD, :], src[rows, bass.ds(p, 1), :].rearrange("p a c -> p (a c)"), ACT.Copy).then_inc(act_hi, 1)

            def r_rows(g, s):
                act.wait_ge(rt_done, g + 1)
                nc.scalar.activation(qm[s][HD:HD + 4, :].rearrange("p (b c) -> p b c", b=2), ps[HD:HD + 4, 2:4, :], ACT.Copy).then_inc(r_ready, 1)

            def invert(g, s, c):
                C = 2 * g + c
                last = NU * g + LAST[c] + 1
                sums = slice(HD, P) if s == 0 else slice(0, HD)
                act.wait_ge(pv_done, last)
                if not isinstance(g, int) or C > 0:
                    act.wait_ge(o_evac, C)
                nc.scalar.activation(o_r0[sums, :], ps[sums, 6 + c, :], ACT.Ln).then_inc(o_ln, 1)
                act.wait_ge(o_ln, C + 1)
                nc.scalar.activation(o_r0[sums, :], o_r0[sums, :], ACT.Exp, scale=-1.0).then_inc(o_inv, 1)

            def wo_split(w):
                buf, i = wo_buffer(w)
                act.wait_ge(s_wo[i], 16 * (w // 4 + 1) if w < KT else 16)
                if w == 0:
                    act.wait_ge(v_ready, HEADS)
                    act.wait_ge(act_hi, HEADS)
                    act.wait_ge(dve_hi, HEADS)
                    act.wait_ge(dve_lo, HEADS)
                    act.wait_ge(pool_lo, HEADS)
                elif w >= KT:
                    act.wait_ge(wo_used, (KT - 1) * (NB - 1) + w - KT + 1) if w < 2 * KT - 1 else act.wait_ge(out_done, NB)
                nc.scalar.activation(wo_hi[:, w % KT, :], buf, ACT.Copy).then_inc(wohi_done, 1)

            def mix_split(v, t, slot):
                if not isinstance(v, int) or v >= 2:
                    act.wait_ge(out_done, v - 1)
                if isinstance(v, int) and v == 0:
                    act.wait_ge(o_evac, 2 * HEADS - 1)
                elif isinstance(v, int) and v == 2:
                    act.wait_ge(o_evac, 2 * HEADS)
                nc.scalar.activation(mix_parts[:, slot, 0, :, :], mix[:, :, bass.ds(t * P, P)], ACT.Copy).then_inc(mixhi_done, 1)

            def head(g, s, nxt):
                for u in range(NU):
                    U, b = NU * g + u, (NU * s + u) % RING
                    _, rows, _, n, _ = unit(u)
                    act.wait_ge(sc_done, U + 1)
                    if not isinstance(U, int) or U >= RING:
                        act.wait_ge(pv_done, U - RING + 1)
                    nc.scalar.activation(p32[0:rows, b, 0:n], ps[0:rows, (NU * s + u) % 2, 0:n], ACT.Exp).then_inc(exp_done, 1)
                    if nxt is not None:
                        if u == 0:
                            prep(*nxt)
                        if u == R_UNIT:
                            r_rows(nxt[0], nxt[2])
                    if u == LAG - 1 and not (isinstance(g, int) and g == 0):
                        invert(g - 1, 1 - s, 1)
                    if u == LAST[0] + LAG + 1:
                        invert(g, s, 0)
                    if nxt is None:
                        if u in WO_UNITS:
                            wo_split(WO_UNITS.index(u))
                        elif u in (11, 12):
                            mix_split(u - 11, u - 11, u - 11)

            act.wait_ge(proj_evac, N_PROJ - N_EARLY)
            act.wait_ge(proj_done, N_PROJ)
            prep(0, 0, 0)
            nc.scalar.preload_act_table_set("natural_log_exp_and_others")
            for o in range(2):
                act.wait_ge(pw_done, o + 1)
                b = 6 - 6 * o
                nc.scalar.activation(mix[:, 4 + o, :].rearrange("p (b c) -> p b c", b=2), ps[:, b:b + 2, :], ACT.Identity,
                                     bias=prm[:, B_PW + o:B_PW + o + 1]).then_inc(pw_evac, 1)
            act.wait_ge(att_init, 4)
            r_rows(0, 0)
            head(0, 0, (1, 0, 1))
            head(1, 1, (2, 1, 0))
            with act.Fori(1, 3) as p:
                head(2 * p, 0, (2 * p + 1, p, 1))
                head(2 * p + 1, 1, (2 * p + 2, p + 1, 0))
            head(6, 0, (7, 3, 1))
            head(7, 1, None)
            invert(7, 1, 1)

            def h_square(t):
                act.wait_ge(h_evac, NB + t + 1)
                if not isinstance(t, int) or t >= 1:
                    act.wait_ge(h_ss_done, t)
                nc.scalar.activation(h_squares[:, :], h[:, bass.ds(t, 1), :].rearrange("p a c -> p (a c)"), ACT.Square,
                                     accum_out=sumsq[:, bass.ds(t, 1)]).then_inc(h_ss_done, 1)
                act.wait_ge(h_ss_done, t + 1)
                nc.scalar.activation(std[:, bass.ds(t, 1)], sumsq[:, bass.ds(t, 1)], ACT.Sqrt, scale=1.0 / D,
                                     bias=eps[:, :]).then_inc(h_std_done, 1)

            def h_high(t):
                act.wait_ge(h32_done, t + 1)
                nc.scalar.activation(hn2_hi[:, :, bass.ds(t * P, P)], h32[:, :, :], ACT.Copy).then_inc(h2hi_done, 1)

            mix_split(2, 2, 0)
            mix_split(3, 3, 1)
            with act.Fori(1, 3) as i:
                mix_split(2 * i + 2, 2 * i + 2, 0)
                mix_split(2 * i + 3, 2 * i + 3, 1)
            mix_split(NB, 0, 0)
            for w in range(KT, 2 * KT):
                wo_split(w)
            mix_split(NB + 1, 1, 1)
            act.wait_ge(wolo_done, 2 * KT)

            def normalize(t, slot):
                if not isinstance(t, int) or t < NB - 2:
                    mix_split(NB + t + 2, t + 2, slot)
                h_square(t)
                if not isinstance(t, int) or t >= 1:
                    h_high(t - 1)

            normalize(0, 0)
            normalize(1, 1)
            with act.Fori(1, 3) as i:
                normalize(2 * i, 0)
                normalize(2 * i + 1, 1)
            normalize(NB - 2, 0)

            def mw_split(r, dst, slot):
                act.wait_ge(s_m[slot], 8 * (r - 8) + 16 - 8 * slot)
                nc.scalar.activation(dst, m_raw[:, slot, :], ACT.Copy).then_inc(mwhi_done, 1)

            def w1_split(q, i):
                mw_split(16 * q + i, w1_parts[:, i // 2, 0, HALF * (i % 2):HALF * (i % 2 + 1)], i % 2)

            def w2_split(q, i):
                if i == 0:
                    act.wait_ge(out_done, 2 * NB + NB * q)
                mw_split(16 * q + 8 + i, w2_hi[:, i // 2, HALF * (i % 2):HALF * (i % 2 + 1)], i % 2)

            def hidden(q, i):
                G = 8 * q + i
                act.wait_ge(m1_done, G + 1)
                if i >= 2:
                    act.wait_ge(alo_done, G - 1)
                nc.scalar.activation(act32[:, i % 2, :], ps[:, i % 4, :], ACT.Relu).then_inc(relu_done, 1)
                w2_split(q, i)
                act.wait_ge(asq_done, G + 1)
                nc.scalar.activation(a_hi[:, i % 4, HALF * (i // 4):HALF * (i // 4 + 1)], act32[:, i % 2, :],
                                     ACT.Copy).then_inc(ahi_done, 1)

            def w1_first_split(i):
                act.wait_ge(s_w1_first[i], 16)
                if i == 0:
                    act.wait_ge(out_done, 2 * NB - 1)
                elif i == 2:
                    act.wait_ge(out_done, 2 * NB)
                elif i == 4:
                    act.wait_ge(h_tr_done, NB)
                    act.wait_ge(h2lo_done, NB)
                    act.wait_ge(h_ss_done, NB)
                nc.scalar.activation(w1_parts[:, i // 2, 0, HALF * (i % 2):HALF * (i % 2 + 1)], w1_first[:, i, :],
                                     ACT.Copy).then_inc(mwhi_done, 1)

            w1_first_split(0)
            w1_first_split(1)
            h_square(NB - 1)
            h_high(NB - 2)
            w1_first_split(2)
            w1_first_split(3)
            h_high(NB - 1)
            for i in range(4, 8):
                w1_first_split(i)
            act.wait_ge(mwlo_done, 8)
            with act.Fori(0, CH - 1) as q:
                for i in range(8):
                    hidden(q, i)
                for i in range(8):
                    if i == 0:
                        act.wait_ge(m1_done, 8 * q + 8)
                    w1_split(q + 1, i)
            for i in range(8):
                hidden(CH - 1, i)
            for t in range(NB):
                act.wait_ge(h_evac, 2 * NB + NB * (CH - 1) + t + 1)
                if t:
                    act.wait_ge(y_ss_done, t)
                nc.scalar.activation(y_squares[:, :], h[:, t, :], ACT.Square, accum_out=sumsq[:, t:t + 1]).then_inc(y_ss_done, 1)
                act.wait_ge(y_ss_done, t + 1)
                nc.scalar.activation(std[:, t:t + 1], sumsq[:, t:t + 1], ACT.Sqrt, scale=1.0 / D, bias=eps[:, :]).then_inc(y_std_done, 1)

        @block.vector
        def _(dve):
            def g_of(first, n):
                return prm[:, first:first + KT].unsqueeze(2).broadcast_to([P, KT, n])

            def scale_x(i):
                T = TILES[i]
                rows = cols_of(T)[1]
                dve.wait_ge(std_done, i + 1)
                nc.vector.reciprocal(rstd[0:rows, T:T + 1], std[0:rows, T:T + 1]).then_inc(rstd_done, 1)
                dve.wait_ge(rstd_done, i + 1)
                if i >= 2:
                    dve.wait_ge(tr_done, i - 1)
                nc.vector.tensor_scalar(xs[0:rows, i % 2, :], x_tile(T), rstd[0:rows, T:T + 1], None,
                                        ALU.mult).then_inc(xs_done, 1)

            def gain(i):
                rows = cols_of(TILES[i])[1]
                if i == 0:
                    dve.wait_ge(s_par, 16)
                dve.wait_ge(tr_done, i + 1)
                if i >= 2:
                    dve.wait_ge(hnlo_done, i - 1)
                b = 2 * (i % 2)
                nc.vector.tensor_tensor(hn32[i % 2][:, :, 0:rows],
                                        ps[:, b:b + 2, :].rearrange("p b (k c) -> p (b k) c", c=P)[:, :, 0:rows],
                                        g_of(G1, rows), ALU.mult).then_inc(hn32_done, 1)

            def split_hn(i):
                k0, rows = cols_of(TILES[i])
                dve.wait_ge(hnhi_done, i + 1)
                nc.vector.tensor_tensor(hn_lo[:, :, k0:k0 + rows], hn32[i % 2][:, :, 0:rows],
                                        hn_hi[:, :, k0:k0 + rows].bitcast(F32), ALU.subtract).then_inc(hnlo_done, 1)

            def split_wv(i):
                dve.wait_ge(wvhi_done, i + 1)
                nc.vector.tensor_tensor(wv_lo[:, 2 * i:2 * i + 2, :], wv_raw[:, 2 * i:2 * i + 2, :],
                                        wv_hi[:, 2 * i:2 * i + 2, :].bitcast(F32), ALU.subtract).then_inc(wvlo_done, 1)

            nc.vector.memset(eps[:, :], EPS).then_inc(eps_ready, 1)
            scale_x(0)
            split_wv(0)
            gain(0)
            split_hn(0)
            split_wv(1)
            scale_x(1)
            split_wv(2)
            split_wv(3)
            for i in range(1, NB + 1):
                if i < NB:
                    scale_x(i + 1)
                gain(i)
                split_hn(i)
                if i == 3:
                    dve.wait_ge(s_masks, 16)
                    nc.vector.tensor_copy(identb[:, :], consts_f[:, 0, :])
                    nc.vector.tensor_copy(mask_qk[:, :], consts_f[:, 1, :])
                    nc.vector.tensor_copy(mask_kq[:, :], consts_f[:, 2, :]).then_inc(masks_ready, 1)

            def split_lo(n, slot, size=D):
                dve.wait_ge(whi_done, n + 1)
                hi = w_hi[:, slot, :, :].rearrange("p k c -> p (k c)").bitcast(F32)
                lo = w_lo[:, slot, :, :].rearrange("p k c -> p (k c)")
                nc.vector.tensor_tensor(lo[:, 0:size], w_raw[:, slot, 0:size], hi[:, 0:size], ALU.subtract).then_inc(wlo_done, 1)

            split_lo(0, 0)
            split_lo(1, 1)
            dve.wait_ge(xs_done, NB + 1)
            nc.vector.memset(glu[0][:, 0:PAD], 0.0)
            nc.vector.memset(glu[1][:, 0:PAD], 0.0).then_inc(pad_done, 1)
            dve.wait_ge(v_evac, NB + 1)
            step = [0]

            def chain(ins):
                ins.then_inc(lf_dve, 1)
                step[0] += 1

            chain(nc.vector.tensor_tensor(lf[0][:, :, :], f_raw[:, :, :],
                                          prm[:, B_F:B_F + HEADS].unsqueeze(1).broadcast_to([P, NB + 1, HEADS]), ALU.add))
            dve.wait_ge(lf_act, 2)
            chain(nc.vector.tensor_scalar(lf[3][:, :, :], lf[2][:, :, :], 1.0, None, ALU.add))
            dve.wait_ge(lf_dve, 2)
            chain(nc.vector.tensor_scalar(lf[5][:, :, :], lf[3][:, :, :], 1.0, None, ALU.subtract))
            dve.wait_ge(lf_dve, 3)
            chain(nc.vector.tensor_tensor(lf[6][:, :, :], lf[2][:, :, :], lf[5][:, :, :], ALU.subtract))
            chain(nc.vector.reciprocal(lf[7][:, :, :], lf[3][:, :, :]))
            dve.wait_ge(lf_dve, 5)
            chain(nc.vector.tensor_tensor(lf[8][:, :, :], lf[6][:, :, :], lf[7][:, :, :], ALU.mult))
            dve.wait_ge(lf_dve, 6)
            dve.wait_ge(lf_act, 3)
            chain(nc.vector.tensor_tensor(lf[9][:, :, :], lf[8][:, :, :], lf[4][:, :, :], ALU.add))
            dve.wait_ge(lf_dve, 7)
            chain(nc.vector.scalar_tensor_tensor(lf[6][:, :, :].rearrange("p t h -> p (t h)"),
                                                 lf[0][:, :, :].rearrange("p t h -> p (t h)"), 0.0,
                                                 lf[9][:, :, :].rearrange("p t h -> p (t h)"), ALU.min, ALU.subtract))

            def projected(n, dst, other):
                b = banks(n)
                dve.wait_ge(proj_done, n + 1)
                c0 = ALL_TOKENS[0][1]
                two = "p (b c) -> p b c"
                nc.vector.tensor_tensor(dst[:, 0:c0], ps[:, b, 0:c0], other[:, 0:c0], ALU.mult)
                return nc.vector.tensor_tensor(dst[:, c0:TOK].rearrange(two, b=2), ps[:, b + 1:b + 3, 0:ALL_TOKENS[1][1]],
                                               other[:, c0:TOK].rearrange(two, b=2), ALU.mult)

            def conv_tap(j, k):
                if isinstance(k, int) and k == 0:
                    nc.vector.tensor_scalar(dw[:, j, :], glu[j][:, 0:SEQ], prm[:, W_DW + CONF_K * j:W_DW + CONF_K * j + 1],
                                            prm[:, B_DW + j:B_DW + j + 1], ALU.mult, ALU.add).then_inc(conv_step[j], 1)
                else:
                    dve.wait_ge(conv_step[j], k)
                    nc.vector.scalar_tensor_tensor(dw[:, j, :], glu[j][:, bass.ds(k, SEQ)], prm[:, bass.ds(W_DW + CONF_K * j + k, 1)],
                                                   dw[:, j, :], ALU.mult, ALU.add).then_inc(conv_step[j], 1)

            for n in range(N_EARLY):
                kind, j = ORDER[n]
                if kind == CONF_A:
                    dve.wait_ge(pad_done, 1)
                    dve.wait_ge(sig_done, j + 1)
                    projected(n, glu[j][:, PAD:PAD + TOK], sig_gate).then_inc(glu_done, 1)
                elif kind == SC_U:
                    dve.wait_ge(scc_done, j + 1)
                    if j:
                        dve.wait_ge(sc_step, 4)
                    projected(n, sc_cu, sc_c).then_inc(cu_done, 1)
                    dve.wait_ge(cu_done, j + 1)
                    for k in range(SC_K):
                        w = prm[:, W_SC + SC_K * j + k:W_SC + SC_K * j + k + 1]
                        src = sc_cu[:, META - SC_K + 1 + k:META - SC_K + 1 + k + SEQ]
                        if k == 0:
                            nc.vector.tensor_scalar(mix[:, 6 + j, :], src, w, None, ALU.mult).then_inc(sc_step, 1)
                        else:
                            dve.wait_ge(sc_step, 4 * j + k)
                            nc.vector.scalar_tensor_tensor(mix[:, 6 + j, :], src, w, mix[:, 6 + j, :],
                                                           ALU.mult, ALU.add).then_inc(sc_step, 1)
                elif kind == SC_B:
                    dve.wait_ge(sc_step, 4 * j + SC_K)
                    dve.wait_ge(proj_done, n + 1)
                    b = banks(n)
                    view = mix[:, 6 + j, :].rearrange("p (b c) -> p b c", b=2)
                    nc.vector.tensor_tensor(view, ps[:, b:b + 2, :], view, ALU.mult).then_inc(sc_step, 1)
                split_lo(n + 2, n % 2)
                if n == 1:
                    dve.wait_ge(lft_done, 1)
                    nc.vector.tensor_copy(lf_t[:, 0:SEQ].rearrange("p (b c) -> p b c", b=2), ps[0:HEADS, 6:8, :]).then_inc(lft_evac, 1)
                if n == 2:
                    dve.wait_ge(lft_done, 2)
                    nc.vector.tensor_copy(lf_t[:, SEQ:TOK], ps[0:HEADS, 6, 0:META]).then_inc(lft_evac, 1)
                    dve.wait_ge(lft_evac, 2)
                    chain(nc.vector.tensor_tensor_scan(c_t[:, :], lf_t[:, :], lf_t[:, :], 0.0, ALU.add, ALU.bypass))
                    dve.wait_ge(lf_dve, 9)
                    chain(nc.vector.tensor_scalar(c_neg[:, :], c_t[:, :], -1.0, None, ALU.mult))
                    dve.wait_ge(lf_dve, 10)
                    dve.wait_ge(v_done, NB + 1)
                    chain(nc.vector.tensor_copy(c_hi[:, :], c_neg[:, :]))
                    dve.wait_ge(lf_dve, 11)
                    chain(nc.vector.tensor_tensor(c_lo[:, :], c_neg[:, :], c_hi[:, :].bitcast(F32), ALU.subtract))
                if n == 4:
                    dve.wait_ge(cq_tr, 1)
                    nc.vector.tensor_copy(c_q[:, :, :].rearrange("p h t -> p t h"),
                                          ps[:, 6, 0:NB * HEADS].rearrange("p (t h) -> p t h", h=HEADS)).then_inc(cq_evac, 1)
                if n == 2:
                    dve.wait_ge(glu_done, 1)
                if n == 4:
                    dve.wait_ge(glu_done, 2)
                for j_, k in EARLY_TAPS[n]:
                    conv_tap(j_, k)
            with dve.Fori(0, 2) as p:
                for i in range(2):
                    split_lo(N_EARLY + 2 * p + 2 + i, i)
                    for k in range(LATE // 4):
                        for j in range(2):
                            conv_tap(j, CONF_K - LATE + LATE // 2 * p + LATE // 4 * i + k)

            def ln_statistics(r):
                dve.wait_ge(ln_tr, r + 1)
                view = ps[:, 6:8, :].rearrange("p b (t c) -> p (b t) c", c=D_CONF)
                for i in range(4):
                    ins = nc.vector.bn_stats(ln_stats[:, 4 * r + i, :], view[:, i, :])
                ins.then_inc(ln_dve, 1)
                dve.wait_ge(ln_dve, 3 * r + 1)
                for i in range(4):
                    nc.vector.bn_aggr(ln_mv[:, 4 * r + i, :], ln_stats[:, 4 * r + i, :]).then_inc(ln_norm, 1)
                dve.wait_ge(ln_norm, 8 * r + 4)
                nc.vector.tensor_scalar(ln_rstd[:, 4 * r:4 * r + 4], ln_mv[:, 4 * r:4 * r + 4, 1], EPS, None,
                                        ALU.add).then_inc(ln_dve, 1)
                dve.wait_ge(ln_sqrt, r + 1)
                nc.vector.reciprocal(ln_rstd[:, 4 * r:4 * r + 4], ln_std[:, 4 * r:4 * r + 4]).then_inc(ln_dve, 1)
                dve.wait_ge(ln_dve, 3 * r + 3)
                for i in range(4):
                    t = 4 * r + i
                    nc.vector.tensor_scalar(normed[:, t, :], view[:, i, :], ln_mv[:, t, 0:1], ln_rstd[:, t:t + 1],
                                            ALU.subtract, ALU.mult).then_inc(ln_norm, 1)

            def swish(j):
                dve.wait_ge(zsig_done, j + 1)
                nc.vector.tensor_tensor(silu[:, j, :], z[:, j, :], silu[:, j, :], ALU.mult).then_inc(silu_done, 1)
                dve.wait_ge(shi_done, j + 1)
                nc.vector.tensor_tensor(s_lo[:, j, :], silu[:, j, :], s_hi[:, j, :].bitcast(F32), ALU.subtract).then_inc(slo_done, 1)

            for j in range(2):
                dve.wait_ge(conv_step[j], CONF_K)
            split_lo(N_PROJ - 2, 0)
            ln_statistics(0)
            split_lo(N_PROJ - 1, 1)
            ln_statistics(1)
            split_lo(N_PROJ, 0, 2 * D_CONF)
            swish(0)
            swish(1)

            def prep(g, p, s, step):
                rows = slice(HD * s, HD * (s + 1))
                q = q_raw[rows, bass.ds(p, 1), :].rearrange("p a c -> p (a c)")
                k = k_raw[rows, bass.ds(p, 1), :].rearrange("p a c -> p (a c)")
                if step == 0:
                    if not isinstance(g, int) or g >= 2:
                        dve.wait_ge(sc_done, NU * (g - 1))
                    nc.vector.tensor_copy(qx[s][HD:P, :], q).then_inc(q_dup, 1)
                elif step == 1:
                    ins = nc.vector.tensor_copy(kx[s][0:HD, :], k)
                    if s == 1:
                        ins = nc.vector.tensor_copy(kx[s][HD:P, :], k)
                    ins.then_inc(k_dup, 1)
                elif step == 2:
                    dst, src = (km[1], k) if s else (qm[0], q)
                    nc.vector.tensor_copy(dst[0:HD, :], src).then_inc(dve_hi, 1)
                elif s == 0:
                    dve.wait_ge(act_hi, g + 1)
                    nc.vector.tensor_tensor(kx[s][HD:P, :], k, km[s][0:HD, :].bitcast(F32), ALU.subtract).then_inc(dve_lo, 1)
                else:
                    dve.wait_ge(q_dup, g + 1)
                    nc.vector.tensor_tensor(qx[s][0:HD, :], q, qx[s][HD:P, :].bitcast(F32), ALU.subtract).then_inc(dve_lo, 1)

            def row_max(g, s, m):
                _, _, w, parts = MAXES[m]
                G, b = NM * g + m, 2 + 2 * ((NM * s + m) % 2)
                dve.wait_ge(mx_mm, G + 1)
                nc.vector.tensor_reduce(mx[:, m:m + 1], ps[:, b:b + parts, 0:w], AX.XY if parts > 1 else AX.X,
                                        ALU.max).then_inc(mx_red, 1)

            def shift(g, hd):
                def nxt(ins, i):
                    ins.then_inc(r_step, 1)
                    dve.wait_ge(r_step, 6 * g + i + 1)

                dve.wait_ge(mx_red, NM * (g + 1))
                nxt(nc.vector.tensor_tensor(mx[:, 7:8], mx[:, 7:8], mx[:, 8:9], ALU.max), 0)
                c = c_q[:, bass.ds(hd, 1), :].rearrange("p a t -> p (a t)")
                nxt(nc.vector.tensor_tensor(m_q[:, :], mx[:, 0:NB], c, ALU.add), 1)
                nxt(nc.vector.tensor_tensor(r_q[:, :], c, m_q[:, :], ALU.subtract), 2)
                nxt(nc.vector.tensor_copy(r_hi[:, :], r_q[:, :]), 3)
                if not isinstance(g, int) or g >= 1:
                    dve.wait_ge(rt_done, g)
                nxt(nc.vector.tensor_copy(r_pad[:, :, HD + 2], r_hi[:, :].bitcast(F32)), 4)
                nxt(nc.vector.tensor_tensor(r_pad[:, :, HD + 3], r_q[:, :], r_hi[:, :].bitcast(F32), ALU.subtract), 5)

            def finish(g, p, s, c):
                C = 2 * g + c
                o, sums = (slice(0, HD), slice(HD, P)) if s == 0 else (slice(HD, P), slice(0, HD))
                dve.wait_ge(o_inv, C + 1)
                nc.vector.tensor_tensor(o_t[sums, :], ps[sums, 6 + c, :], o_r0[sums, :], ALU.mult).then_inc(o_step, 1)
                dve.wait_ge(o_step, 2 * C + 1)
                nc.vector.scalar_tensor_tensor(o_r1[o, :], o_t[sums, :], 2.0, o_r0[sums, :], ALU.subtract, ALU.mult).then_inc(o_step, 1)
                dve.wait_ge(o_step, 2 * C + 2)
                nc.vector.scalar_tensor_tensor(mix[o, bass.ds(p, 1), HALF * c:HALF * (c + 1)].rearrange("p a c -> p (a c)"),
                                               ps[o, 6 + c, :], -1.0, o_r1[o, :], ALU.mult, ALU.mult).then_inc(o_evac, 1)

            def wo_split(w):
                dve.wait_ge(wohi_done, w + 1)
                nc.vector.tensor_tensor(wo_lo[:, w % KT, :], wo_buffer(w)[0], wo_hi[:, w % KT, :].bitcast(F32),
                                        ALU.subtract).then_inc(wolo_done, 1)

            def mix_split(v, t, slot):
                dve.wait_ge(mixhi_done, v + 1)
                nc.vector.tensor_tensor(mix_parts[:, slot, 1, :, :], mix[:, :, bass.ds(t * P, P)],
                                        mix_parts[:, slot, 0, :, :].bitcast(F32), ALU.subtract).then_inc(mixlo_done, 1)

            def head(g, p, s, nxt):
                for u in range(NU):
                    if nxt is not None:
                        if u == 0:
                            for i in range(4):
                                prep(*nxt, i)
                        for m in MAX_STEPS.get(u, ()):
                            row_max(nxt[0], nxt[2], m)
                        if u == max(MAX_STEPS):
                            shift(nxt[0], nxt[0])
                    if u == LAG and not (isinstance(g, int) and g == 0):
                        finish(g - 1, p - 1 + s, 1 - s, 1)
                    if u == LAST[0] + LAG + 2:
                        finish(g, p, s, 0)
                    if nxt is None:
                        if u in WO_UNITS:
                            wo_split(WO_UNITS.index(u))
                        elif u in (11, 12):
                            mix_split(u - 11, u - 11, u - 11)

            dve.wait_ge(proj_evac, N_PROJ - N_EARLY)
            for i in range(4):
                prep(0, 0, 0, i)
            for m in range(NM):
                row_max(0, 0, m)
            dve.wait_ge(att_init, R_FILLS)
            shift(0, 0)
            dve.wait_ge(pw_done, 2)
            head(0, 0, 0, (1, 0, 1))
            head(1, 0, 1, (2, 1, 0))
            with dve.Fori(1, 3) as p:
                head(2 * p, p, 0, (2 * p + 1, p, 1))
                head(2 * p + 1, p, 1, (2 * p + 2, p + 1, 0))
            head(6, 3, 0, (7, 3, 1))
            head(7, 3, 1, None)
            finish(7, 3, 1, 1)

            def residual(v, t, c, slot):
                dve.wait_ge(out_done, v + 1)
                dst = h[:, bass.ds(t, 1), HALF * c:HALF * (c + 1)].rearrange("p a c -> p (a c)")
                nc.vector.tensor_tensor(dst, ps[:, slot, :], dst, ALU.add).then_inc(h_evac, 1)

            def h_scale(t, slot):
                dve.wait_ge(h_std_done, t + 1)
                nc.vector.reciprocal(rstd[:, bass.ds(t, 1)], std[:, bass.ds(t, 1)]).then_inc(h_rstd_done, 1)
                dve.wait_ge(h_rstd_done, t + 1)
                nc.vector.tensor_scalar(hs[:, slot, :], h[:, bass.ds(t, 1), :].rearrange("p a c -> p (a c)"),
                                        rstd[:, bass.ds(t, 1)], None, ALU.mult).then_inc(h_scaled, 1)

            def h_gain(t, slot):
                dve.wait_ge(h_tr_done, t + 1)
                if not isinstance(t, int) or t >= 1:
                    dve.wait_ge(h2lo_done, t)
                b = 4 + 2 * slot
                nc.vector.tensor_tensor(h32[:, :, :], ps[:, b:b + 2, :].rearrange("p b (k c) -> p (b k) c", c=P),
                                        g_of(G2, P), ALU.mult).then_inc(h32_done, 1)

            def h_low(t):
                dve.wait_ge(h2hi_done, t + 1)
                nc.vector.tensor_tensor(hn2_lo[:, :, bass.ds(t * P, P)], h32[:, :, :],
                                        hn2_hi[:, :, bass.ds(t * P, P)].bitcast(F32), ALU.subtract).then_inc(h2lo_done, 1)

            def next_pair(i):
                mix_split(2 * i + 2, 2 * i + 2, 0)
                residual(2 * i, 2 * i, 0, 0)
                mix_split(2 * i + 3, 2 * i + 3, 1)
                residual(2 * i + 1, 2 * i + 1, 0, 1)

            def normalize(t, slot):
                residual(NB + t, t, 1, slot)
                if not isinstance(t, int) or t < NB - 2:
                    mix_split(NB + t + 2, t + 2, slot)
                if not isinstance(t, int) or t >= 1:
                    h_gain(t - 1, 1 - slot)
                h_scale(t, slot)
                if not isinstance(t, int) or t >= 1:
                    h_low(t - 1)

            for i in range(NB):
                dve.wait_ge(s_x_again[i], 16)
            next_pair(0)
            with dve.Fori(1, 3) as i:
                next_pair(i)
            mix_split(NB, 0, 0)
            residual(NB - 2, NB - 2, 0, 0)
            for w in range(KT, 2 * KT):
                wo_split(w)
            residual(NB - 1, NB - 1, 0, 1)
            mix_split(NB + 1, 1, 1)
            normalize(0, 0)
            normalize(1, 1)
            with dve.Fori(1, 3) as i:
                normalize(2 * i, 0)
                normalize(2 * i + 1, 1)
            normalize(NB - 2, 0)

            def mw_split(r, lo, hi, slot):
                dve.wait_ge(mwhi_done, r + 1)
                nc.vector.tensor_tensor(lo, m_raw[:, slot, :], hi.bitcast(F32), ALU.subtract).then_inc(mwlo_done, 1)

            def w1_split(q, i):
                c = slice(HALF * (i % 2), HALF * (i % 2 + 1))
                mw_split(16 * q + i, w1_parts[:, i // 2, 1, c], w1_parts[:, i // 2, 0, c], i % 2)

            def w2_split(q, i):
                c = slice(HALF * (i % 2), HALF * (i % 2 + 1))
                mw_split(16 * q + 8 + i, w2_lo[:, i // 2, c], w2_hi[:, i // 2, c], i % 2)

            def hidden(q, i):
                G = 8 * q + i
                dve.wait_ge(relu_done, G + 1)
                nc.vector.tensor_tensor(act32[:, i % 2, :], act32[:, i % 2, :], act32[:, i % 2, :], ALU.mult).then_inc(asq_done, 1)
                w2_split(q, i)
                dve.wait_ge(ahi_done, G + 1)
                c = slice(HALF * (i // 4), HALF * (i // 4 + 1))
                nc.vector.tensor_tensor(a_lo[:, i % 4, c], act32[:, i % 2, :], a_hi[:, i % 4, c].bitcast(F32),
                                        ALU.subtract).then_inc(alo_done, 1)

            def accumulate(q, t):
                b = 4 + 2 * (t % 2)
                dve.wait_ge(out_done, 2 * NB + NB * q + t + 1)
                dst = h[:, t, :].rearrange("p (b c) -> p b c", b=2)
                nc.vector.tensor_tensor(dst, ps[:, b:b + 2, :], dst, ALU.add).then_inc(h_evac, 1)

            def w1_first_split(i):
                dve.wait_ge(mwhi_done, i + 1)
                c = slice(HALF * (i % 2), HALF * (i % 2 + 1))
                nc.vector.tensor_tensor(w1_parts[:, i // 2, 1, c], w1_first[:, i, :], w1_parts[:, i // 2, 0, c].bitcast(F32),
                                        ALU.subtract).then_inc(mwlo_done, 1)

            w1_first_split(0)
            w1_first_split(1)
            normalize(NB - 1, 1)
            w1_first_split(2)
            w1_first_split(3)
            h_gain(NB - 1, 1)
            h_low(NB - 1)
            for i in range(4, 8):
                w1_first_split(i)
            with dve.Fori(0, CH - 1) as q:
                for i in range(8):
                    hidden(q, i)
                for t in range(NB):
                    w1_split(q + 1, t)
                    accumulate(q, t)
            for i in range(8):
                hidden(CH - 1, i)

            def output(t):
                dve.wait_ge(y_std_done, t + 1)
                nc.vector.reciprocal(rstd[:, t:t + 1], std[:, t:t + 1]).then_inc(y_rstd_done, 1)
                dve.wait_ge(y_rstd_done, t + 1)
                if t >= 2:
                    dve.wait_ge(s_out[t % 2], 16 * (t // 2))
                for c0, c1 in out_parts(t):
                    nc.vector.scalar_tensor_tensor(y[:, t % 2, c0:c1], h[:, t, c0:c1], rstd[:, t:t + 1], g_row[:, c0:c1],
                                                   ALU.mult, ALU.mult).then_inc(y_done, 1)

            for t in range(NB):
                accumulate(CH - 1, t)
                if t == 0:
                    dve.wait_ge(s_g, 16)
                output(t)

        @block.tensor
        def _(pe):
            def three(dst, stat, mov, first, last):
                nc.tensor.matmul(dst, stat[0], mov[0], start=first, stop=False)
                nc.tensor.matmul(dst, stat[0], mov[1], start=False, stop=False)
                return nc.tensor.matmul(dst, stat[1], mov[0], start=False, stop=last)

            def transpose_x(i):
                rows = cols_of(TILES[i])[1]
                pe.wait_ge(xs_done, i + 1)
                if i >= 2:
                    pe.wait_ge(hn32_done, i - 1)
                for k in range(KT):
                    ins = nc.tensor.transpose(ps[:, 2 * (i % 2) + k // 4, P * (k % 4):P * (k % 4) + rows],
                                              xs[0:rows, i % 2, P * k:P * (k + 1)], ident[0:rows, 0:rows])
                ins.then_inc(tr_done, 1)

            def project_v(i):
                k0, rows = cols_of(TILES[i])
                pe.wait_ge(hnlo_done, i + 1)
                if i >= 2:
                    pe.wait_ge(v_evac, i - 1)
                b = 4 + 2 * (i % 2)
                n = VF // 2
                for half in range(2):
                    for k in range(KT):
                        if i == 0 and half == 0:
                            pe.wait_ge(wvlo_done, k // 2 + 1)
                            if k == KT // 2:
                                transpose_x(1)
                        c = slice(n * half, n * (half + 1))
                        ins = three(ps[0:rows, b + half, 0:n], (hn_hi[:, k, k0:k0 + rows], hn_lo[:, k, k0:k0 + rows]),
                                    (wv_hi[:, k, c], wv_lo[:, k, c]), k == 0, k == KT - 1)
                ins.then_inc(v_done, 1)

            pe.wait_ge(s_ident, 16)
            transpose_x(0)
            project_v(0)
            for i in range(1, NB + 1):
                if i < NB:
                    transpose_x(i + 1)
                project_v(i)

            def project(n, slot, tokens, between=None):
                pe.wait_ge(wlo_done, n + 1)
                for k in range(KT):
                    if k == KT // 2 - 1 and between:
                        between()
                    stat = (w_hi[:, slot, k, :], w_lo[:, slot, k, :])
                    for a, b_ in ((0, 0), (0, 1), (1, 0)):
                        for i, (c0, width) in enumerate(tokens):
                            mov = (hn_hi, hn_lo)[b_][:, k, c0:c0 + width]
                            ins = nc.tensor.matmul(ps[:, 3 * slot + i, 0:width], stat[a], mov,
                                                   start=(k == 0 and a + b_ == 0), stop=(k == KT - 1 and a == 1))
                ins.then_inc(proj_done, 1)

            for n in range(N_EARLY):
                kind, j = ORDER[n]
                if n == 1:
                    pe.wait_ge(v_evac, NB + 1)
                elif n >= 2:
                    before, jb = ORDER[n - 2]
                    if before == GATE:
                        pe.wait_ge(sig_done, jb + 1)
                    elif before == CONF_A:
                        pe.wait_ge(glu_done, jb + 1)
                    elif before == SC_C:
                        pe.wait_ge(scc_done, jb + 1)
                    elif before == SC_U:
                        pe.wait_ge(cu_done, jb + 1)
                    else:
                        pe.wait_ge(sc_step, 4 * jb + 4)
                project(n, n % 2, REAL_TOKENS if kind == SC_B else ALL_TOKENS)
                if n == 1:
                    pe.wait_ge(lf_dve, 8)
                    for T in range(NB):
                        k0, rows = cols_of(T)
                        b, c0 = (6 + T // 4, k0 % HALF)
                        ins = nc.tensor.transpose(ps[0:HEADS, b, c0:c0 + rows], lf[6][0:rows, T, :], ident[0:rows, 0:rows])
                    ins.then_inc(lft_done, 1)
                if n == 2:
                    pe.wait_ge(lft_evac, 1)
                    nc.tensor.transpose(ps[0:HEADS, 6, 0:META], lf[6][0:META, NB, :],
                                        ident[0:META, 0:META]).then_inc(lft_done, 1)
                if n == 3:
                    pe.wait_ge(lf_dve, 9)
                    pe.wait_ge(lft_evac, 2)
                    for t in range(NB):
                        ins = nc.tensor.transpose(ps[:, 6, HEADS * t:HEADS * (t + 1)],
                                                  c_t[:, META + P * t:META + P * (t + 1)], ident[0:HEADS, 0:HEADS])
                    ins.then_inc(cq_tr, 1)

            def ln_transposes(r):
                for j in range(2):
                    pe.wait_ge(conv_step[j], CONF_K)
                if r == 0:
                    pe.wait_ge(cq_evac, 1)
                else:
                    pe.wait_ge(ln_norm, 8)
                for i in range(4):
                    t = 4 * r + i
                    for j in range(2):
                        c0 = D_CONF * (i % 2) + P * j
                        ins = nc.tensor.transpose(ps[:, 6 + i // 2, c0:c0 + P], dw[:, j, P * t:P * (t + 1)], ident[:, :])
                ins.then_inc(ln_tr, 1)

            def queries(n):
                if isinstance(n, int) and n == N_EARLY:
                    pe.wait_ge(cu_done, 2)
                elif not isinstance(n, int) or n > N_EARLY:
                    pe.wait_ge(proj_evac, n - N_EARLY - 1)
                project(n, 0, REAL_TOKENS)

            def keys(n, between=None):
                if isinstance(n, int) and n == N_EARLY + 1:
                    pe.wait_ge(sc_step, 8)
                else:
                    pe.wait_ge(proj_evac, n - N_EARLY - 1)
                project(n, 1, ALL_TOKENS, between)

            queries(N_EARLY)
            keys(N_EARLY + 1)
            def ln_transposes_back(j):
                if j == 0:
                    pe.wait_ge(ln_norm, 16)
                else:
                    pe.wait_ge(z_done, 1)
                for t in range(NB):
                    ins = nc.tensor.transpose(ps[:, 6 + t // 4, P * (t % 4):P * (t % 4 + 1)],
                                              normed[:, t, P * j:P * (j + 1)], ident[:, :])
                ins.then_inc(ln_back, 1)

            queries(N_PROJ - 6)
            keys(N_PROJ - 5)
            queries(N_PROJ - 4)
            ln_transposes(0)
            keys(N_PROJ - 3)
            ln_transposes(1)
            queries(N_PROJ - 2)
            ln_transposes_back(0)
            keys(N_PROJ - 1, lambda: ln_transposes_back(1))

            def row_max(g, s, m):
                block_, c0, w, parts = MAXES[m]
                G, b = NM * g + m, 2 + 2 * ((NM * s + m) % 2)
                if m == 0:
                    pe.wait_ge(act_hi, g + 1)
                    pe.wait_ge(dve_hi, g + 1)
                    pe.wait_ge(s_c[s], 16 * (g // 2 + 1) if isinstance(g, int) else 8 * g + 16 - 8 * s)
                    if not isinstance(g, int) or g >= 1:
                        pe.wait_ge(r_ready, g)
                if not isinstance(G, int) or G >= 2:
                    pe.wait_ge(mx_red, G - 1)
                last = c0 + w * parts == META + P * (block_ + 1)
                for i in range(parts):
                    masked = last and i == parts - 1
                    a = c0 + w * i
                    ins = nc.tensor.matmul(ps[:, b + i, 0:w], qm[s][0:HD + 2, P * block_:P * (block_ + 1)],
                                           km[s][0:HD + 2, a:a + w], start=True, stop=not masked)
                    if masked:
                        ins = nc.tensor.matmul(ps[:, b + i, w - P:w], identb[:, :], mask_qk[:, :], start=False, stop=True)
                ins.then_inc(mx_mm, 1)

            def r_transposes(g):
                pe.wait_ge(r_step, 6 * g + 6)
                for t in range(NB):
                    ins = nc.tensor.transpose(ps[0:HD + 4, 2 + t // 4, P * (t % 4):P * (t % 4 + 1)], r_pad[:, t, :], ident[:, :])
                ins.then_inc(rt_done, 1)

            def scores(g, s, u):
                U, b = NU * g + u, (NU * s + u) % 2
                k0, rows, q0, n, mask = unit(u)
                if u == 0:
                    pe.wait_ge(dve_lo, g + 1)
                    pe.wait_ge(pool_lo, g + 1)
                    pe.wait_ge(r_ready, g + 1)
                if not isinstance(U, int) or U >= 2:
                    pe.wait_ge(exp_done, U - 1)
                dst = ps[0:rows, b, 0:n]
                nc.tensor.matmul(dst, km[s][0:HD + 4, k0:k0 + rows], qm[s][0:HD + 4, q0:q0 + n], start=True, stop=False)
                ins = nc.tensor.matmul(dst, kx[s][:, k0:k0 + rows], qx[s][:, q0:q0 + n], start=False, stop=mask is None)
                if mask is not None:
                    first, w = mask
                    ins = nc.tensor.matmul(ps[0:rows, b, 0:w], identb[:, 0:rows], mask_kq[:, first:first + w], start=False, stop=True)
                ins.then_inc(sc_done, 1)

            def weigh(g, s, u):
                U, b = NU * g + u, (NU * s + u) % RING
                _, rows, q0, n, _ = unit(u)
                c, T = UNITS[u]
                pe.wait_ge(exp_done, U + 1)
                if u == 0:
                    pe.wait_ge(v_ready, g + 1)
                if T == 0:
                    if isinstance(g, int) and g == 0:
                        pe.wait_ge(pw_evac, 2)
                    else:
                        pe.wait_ge(o_evac, 2 * g + c - 1)
                c0 = q0 - HALF * c
                last = u == LAST[c]
                ins = nc.tensor.matmul(ps[:, 6 + c, c0:c0 + n], v_one[s][0:rows, T, :], p32[0:rows, b, 0:n],
                                       start=T == 0, stop=last)
                ins.then_inc(pv_done, 1)

            def head(g, s, nxt):
                for u in range(NU):
                    scores(g, s, u)
                    if nxt is not None:
                        for m in MAX_STEPS.get(u, ()):
                            row_max(nxt[0], nxt[1], m)
                        if u == R_UNIT:
                            r_transposes(nxt[0])
                    if u >= LAG:
                        weigh(g, s, u - LAG)
                    elif not (isinstance(g, int) and g == 0):
                        weigh(g - 1, 1 - s, NU - LAG + u)

            def pointwise(o, k, i):
                if k + i == 0:
                    pe.wait_ge(slo_done, 2)
                    pe.wait_ge(wlo_done, N_PROJ + 1)
                    pe.wait_ge(z_done, 2)
                    pe.wait_ge(proj_evac, N_PROJ - N_EARLY - 1)
                c0 = D_CONF * k + P * o
                stat = [w[:, 0, :, :].rearrange("p k c -> p (k c)")[:, c0:c0 + P] for w in (w_hi, w_lo)]
                c = slice(HALF * i, HALF * (i + 1))
                ins = three(ps[:, 6 - 6 * o + i, :], stat, (s_hi[:, k, c], s_lo[:, k, c]), k == 0, k == 1)
                if k + i == 2:
                    ins.then_inc(pw_done, 1)

            for k, i in ((0, 0), (0, 1), (1, 0), (1, 1)):
                pointwise(0, k, i)
            pe.wait_ge(att_init, 2)
            pe.wait_ge(masks_ready, 1)
            pe.wait_ge(proj_evac, N_PROJ - N_EARLY)
            for m in range(NM):
                row_max(0, 0, m)
                if 1 <= m <= 4:
                    pointwise(1, (m - 1) // 2, (m - 1) % 2)
            r_transposes(0)
            pe.wait_ge(att_init, 4)
            pe.wait_ge(pw_evac, 2)
            head(0, 0, (1, 1))
            head(1, 1, (2, 0))
            with pe.Fori(1, 3) as p:
                head(2 * p, 0, (2 * p + 1, 1))
                head(2 * p + 1, 1, (2 * p + 2, 0))
            head(6, 0, (7, 1))
            head(7, 1, None)
            for u in range(NU - LAG, NU):
                weigh(7, 1, u)

            def project_out(v, b, slot):
                pe.wait_ge(mixlo_done, v + 1)
                if not isinstance(v, int) or v >= 2:
                    pe.wait_ge(h_evac, v - 1)
                for k in range(KT):
                    pe.wait_ge(wolo_done, KT * b + k + 1)
                    ins = three(ps[:, slot, :], (mix_parts[:, slot, 0, k, :], mix_parts[:, slot, 1, k, :]),
                                (wo_hi[:, k, :], wo_lo[:, k, :]), k == 0, k == KT - 1)
                    if b == 0 and k < KT - 1:
                        ins.then_inc(wo_used, 1)
                ins.then_inc(out_done, 1)

            def transpose_h(t, slot):
                pe.wait_ge(h_scaled, t + 1)
                if not isinstance(t, int) or t >= 2:
                    pe.wait_ge(h32_done, t - 1)
                for k in range(KT):
                    ins = nc.tensor.transpose(ps[:, 4 + 2 * slot + k // 4, P * (k % 4):P * (k % 4 + 1)],
                                              hs[:, slot, P * k:P * (k + 1)], ident[:, :])
                ins.then_inc(h_tr_done, 1)

            project_out(0, 0, 0)
            project_out(1, 0, 1)
            with pe.Fori(1, 4) as i:
                project_out(2 * i, 0, 0)
                project_out(2 * i + 1, 0, 1)
            project_out(NB, 1, 0)
            project_out(NB + 1, 1, 1)
            transpose_h(0, 0)
            project_out(NB + 2, 1, 0)
            transpose_h(1, 1)
            with pe.Fori(1, 3) as i:
                project_out(NB + 2 * i + 1, 1, 1)
                transpose_h(2 * i, 0)
                project_out(NB + 2 * i + 2, 1, 0)
                transpose_h(2 * i + 1, 1)
            project_out(2 * NB - 1, 1, 1)
            transpose_h(NB - 2, 0)

            def mlp(q):
                for i in range(2 * FT):
                    if isinstance(q, int) and q == 0 and i < 2:
                        if i == 0:
                            pe.wait_ge(h_evac, 2 * NB)
                            pe.wait_ge(h2lo_done, FT)
                        else:
                            transpose_h(NB - 1, 1)
                    f, half = i % FT, i // FT
                    if half == 0:
                        pe.wait_ge(mwlo_done, 16 * q + 2 * f + 2)
                    else:
                        pe.wait_ge(relu_done, 8 * q + i - 3)
                        if isinstance(q, int) and q == 0 and i == FT:
                            pe.wait_ge(h2lo_done, NB)
                    c = slice(HALF * half, HALF * (half + 1))
                    for k in range(KT):
                        w = slice(P * k, P * (k + 1))
                        ins = three(ps[:, f, :], (w1_parts[:, f, 0, w], w1_parts[:, f, 1, w]), (hn2_hi[:, k, c], hn2_lo[:, k, c]),
                                    k == 0, k == KT - 1)
                    ins.then_inc(m1_done, 1)
                for t in range(NB):
                    b = 4 + 2 * (t % 2)
                    if t % 4 == 0:
                        pe.wait_ge(alo_done, 8 * q + t + 4)
                    pe.wait_ge(h_evac, 2 * NB + NB * q + t - 1)
                    for f in range(FT):
                        if t == 0:
                            pe.wait_ge(mwlo_done, 16 * q + 8 + 2 * f + 2)
                        a = (a_hi[:, f, P * t:P * (t + 1)], a_lo[:, f, P * t:P * (t + 1)])
                        for i in range(2):
                            c = slice(HALF * i, HALF * (i + 1))
                            ins = three(ps[:, b + i, :], a, (w2_hi[:, f, c], w2_lo[:, f, c]), f == 0, f == FT - 1)
                    ins.then_inc(out_done, 1)

            mlp(0)
            with pe.Fori(1, CH - 1) as q:
                mlp(q)
            mlp(CH - 1)


def kernel(x, meta_tokens, mix_norm_g, w_in, b_forget, w_conf_dw, b_conf_dw, conf_ln_g, conf_ln_b, w_conf_pw,
           b_conf_pw, w_sc_conv, w_out, mlp_norm_g, w_mlp1, w_mlp2, final_norm_g):
    import concourse.bacc as bacc
    from concourse.bass_utils import run_bass_kernel_spmd

    def tiles(a):
        a = np.asarray(a)
        return a.reshape(-1, P, *a.shape[1:]).swapaxes(0, 1)

    win = tiles(w_in[0])
    par = np.concatenate([
        tiles(mix_norm_g[0]), tiles(mlp_norm_g[0]), tiles(b_conf_dw[0]),
        tiles(np.asarray(w_conf_dw[0]).T).reshape(P, -1), tiles(conf_ln_g[0]), tiles(conf_ln_b[0]), tiles(b_conf_pw[0]),
        tiles(np.asarray(w_sc_conv[0]).T).reshape(P, -1), np.broadcast_to(np.asarray(b_forget[0]), (P, HEADS))], axis=1)
    row, col = np.arange(P)[:, None], np.arange(P)[None, :]
    hidden = -1e30
    consts = np.stack([np.eye(P), np.where(col > row, hidden, 0.0), np.where(row > col, hidden, 0.0)], 1).astype(np.float32)
    arrays = {
        "x": np.asarray(x)[0], "meta": np.asarray(meta_tokens), "par": par, "consts": consts,
        "w_vf": win[:, :, 2 * D_ATTN:2 * D_ATTN + VF],
        "w_proj": np.stack([win[:, :, FIRST_COL[kind] + P * j:FIRST_COL[kind] + P * (j + 1)].reshape(P, -1)
                            for kind, j in ORDER]),
        "w_pw": tiles(w_conf_pw[0]).reshape(P, -1), "w_out": np.asarray(w_out[0]),
        "w1": np.asarray(w_mlp1[0]).reshape(KT, P, FF // P, P).transpose(2, 1, 0, 3).reshape(FF // P, P, D),
        "w2": np.asarray(w_mlp2[0]).reshape(FF // P, P, D),
        "g_fin": np.broadcast_to(np.asarray(final_norm_g), (P, D)),
    }
    nc = bacc.Bacc("TRN2", target_bir_lowering=False, num_devices=1)
    arrays = {f"in_{n}": np.ascontiguousarray(a) for n, a in arrays.items()}
    ins = [nc.dram_tensor(n, a.shape, mybir.dt.from_np(a.dtype), kind="ExternalInput").ap() for n, a in arrays.items()]
    out = nc.dram_tensor("out", (SEQ, D), F32, kind="ExternalOutput").ap()
    build(nc, *ins, out)
    r = run_bass_kernel_spmd(nc, [arrays], core_ids=[0])
    return r.results[0]["out"].reshape(1, SEQ, D)
```
